# Optimizing a Trainium2 kernel written in Bass

```python
import jax
import jax.numpy as jnp
from jax import lax
import numpy as np

D_MODEL = 1024
BATCH = 1
SEQ = 256
DEPTH = 2

GRID_W = 64
CTX_LEN = 256
EPS = 1e-6
HG_HEADS = 4
HG_DK = 128
HG_DV = 128
HG_WIDTH = HG_HEADS * HG_DV
HG_CHUNK = 64
MLA_HEADS = 8
MLA_NOPE = 64
MLA_ROPE = 32
MLA_V = 64
MLA_Q_RANK = 384
MLA_KV_RANK = 256
MLA_WIDTH = MLA_HEADS * MLA_V
MLA_SCALE = (MLA_NOPE + MLA_ROPE) ** -0.5
Q_BLOCK = 128
ROPE_THETA = 10000.0
N_EXPERTS = 16
N_GROUPS = 4
EXPERTS_PER_GROUP = N_EXPERTS // N_GROUPS
TOP_K = 2
D_EXPERT = 512
MOE_BLOCK = 128
IN_SPLITS = (HG_HEADS * HG_DK, HG_WIDTH, HG_HEADS * HG_DK, HG_HEADS * HG_DK, HG_WIDTH,
             MLA_Q_RANK, MLA_KV_RANK + MLA_ROPE, D_MODEL, D_MODEL)
IN_DIM = sum(IN_SPLITS)

kernel_name = 'hybrid_hgrn2_mla_grouped_moe_dit'

def rmsnorm(x, g):
    xf = x.astype(jnp.float32)
    y = xf * lax.rsqrt(jnp.mean(xf * xf, axis=-1, keepdims=True) + EPS)
    return (y * g.astype(jnp.float32)).astype(x.dtype)

def modulate(h, shift, scale):
    return h * (1 + scale) + shift

def split_in(p):
    offs = [int(o) for o in np.cumsum(IN_SPLITS)[:-1]]
    return jnp.split(p, offs, axis=-1)

def to_heads(t, n_heads):
    b_, l_, w = t.shape
    return t.reshape(b_, l_, n_heads, w // n_heads).transpose(0, 2, 1, 3)

def from_heads(t):
    b_, h_, l_, d_ = t.shape
    return t.transpose(0, 2, 1, 3).reshape(b_, l_, h_ * d_)

def axial_angles(n_tok):
    rows = n_tok // GRID_W
    row = jnp.broadcast_to(jnp.arange(rows, dtype=jnp.float32)[:, None], (rows, GRID_W)).reshape(-1)
    col = jnp.broadcast_to(jnp.arange(GRID_W, dtype=jnp.float32)[None, :], (rows, GRID_W)).reshape(-1)
    axis_dim = MLA_ROPE // 2
    inv_freq = ROPE_THETA ** (-jnp.arange(0, axis_dim, 2, dtype=jnp.float32) / axis_dim)
    return row[:, None] * inv_freq, col[:, None] * inv_freq

def rotate(x, ang):
    m = ang.shape[-1]
    cos, sin = jnp.cos(ang), jnp.sin(ang)
    x1, x2 = x[..., :m], x[..., m:]
    return jnp.concatenate([x1 * cos - x2 * sin, x1 * sin + x2 * cos], axis=-1)

def rope_2d(x, ang):
    ang_r, ang_c = ang
    a = MLA_ROPE // 2
    xf = x.astype(jnp.float32)
    return jnp.concatenate([rotate(xf[..., :a], ang_r), rotate(xf[..., a:], ang_c)], axis=-1).astype(x.dtype)

def lower_bound(gamma, layer):
    p = jnp.cumsum(jax.nn.softmax(gamma.astype(jnp.float32), axis=0), axis=0)
    return (p[layer] - p[0]).reshape(HG_HEADS, 1, HG_DK)

def forget_gate(f_pre, lb):
    f = lb + (1.0 - lb) * jax.nn.sigmoid(f_pre)
    return jnp.log(f), 1.0 - f

def gla_chunk_scan(q, k, v, logf, s0):
    b_, h_, L, _ = q.shape
    dv = v.shape[-1]
    nc = L // HG_CHUNK

    def to_chunks(t):
        return jnp.moveaxis(t.reshape(b_, h_, nc, HG_CHUNK, t.shape[-1]), 2, 0)

    mask = jnp.tril(jnp.ones((HG_CHUNK, HG_CHUNK), dtype=bool))

    def step(state, inp):
        qc, kc, vc, lc = inp
        bcum = jnp.cumsum(lc, axis=2)
        o_inter = jnp.einsum('bhtk,bhkv->bhtv', qc * jnp.exp(bcum), state)
        diff = bcum[:, :, :, None, :] - bcum[:, :, None, :, :]
        decay = jnp.exp(jnp.where(mask[:, :, None], diff, -jnp.inf))
        att = jnp.einsum('bhtk,bhtsk,bhsk->bhts', qc, decay, kc)
        o = o_inter + jnp.einsum('bhts,bhsv->bhtv', att, vc)
        blast = bcum[:, :, -1:, :]
        new_state = (jnp.exp(bcum[:, :, -1, :])[..., None] * state
                     + jnp.einsum('bhsk,bhsv->bhkv', kc * jnp.exp(blast - bcum), vc))
        return new_state, o

    s_final, o = lax.scan(step, s0, (to_chunks(q), to_chunks(k), to_chunks(v), to_chunks(logf)))
    return jnp.moveaxis(o, 0, 2).reshape(b_, h_, L, dv), s_final

def hgrn2_direction(q_c, v_c, f_c, q_x, v_x, f_x, lb, reverse):
    if reverse:
        q_c, v_c, f_c, q_x, v_x, f_x = [jnp.flip(t, axis=2) for t in (q_c, v_c, f_c, q_x, v_x, f_x)]
    logf_c, k_c = forget_gate(f_c, lb)
    logf_x, k_x = forget_gate(f_x, lb)
    s0 = jnp.zeros((q_c.shape[0], HG_HEADS, HG_DK, HG_DV), jnp.float32)
    o_c, s_c = gla_chunk_scan(q_c, k_c, v_c, logf_c, s0)
    o_x, _ = gla_chunk_scan(q_x, k_x, v_x, logf_x, s_c)
    if reverse:
        o_c, o_x = jnp.flip(o_c, axis=2), jnp.flip(o_x, axis=2)
    return o_c, o_x

def hgrn2_readout(o, g, gain):
    b_, h_, L, dv = o.shape
    o = o.transpose(0, 2, 1, 3)
    o = o * lax.rsqrt(jnp.mean(o * o, axis=-1, keepdims=True) + EPS) * gain.astype(jnp.float32).reshape(h_, dv)
    return (o.reshape(b_, L, h_ * dv) * jax.nn.silu(g.astype(jnp.float32))).astype(g.dtype)

def mla_qkv(dq, dkv, q_norm_g, kv_norm_g, w_uq, w_ukv, ang):
    b_, L, _ = dq.shape
    q = (rmsnorm(dq, q_norm_g) @ w_uq).reshape(b_, L, MLA_HEADS, MLA_NOPE + MLA_ROPE).transpose(0, 2, 1, 3)
    kv = (rmsnorm(dkv[..., :MLA_KV_RANK], kv_norm_g) @ w_ukv).reshape(b_, L, MLA_HEADS, MLA_NOPE + MLA_V).transpose(0, 2, 1, 3)
    q_nope, q_pe = q[..., :MLA_NOPE], q[..., MLA_NOPE:]
    k_nope, v = kv[..., :MLA_NOPE], kv[..., MLA_NOPE:]
    k_pe = dkv[..., MLA_KV_RANK:][:, None]
    if ang is not None:
        q_pe = rope_2d(q_pe, ang)
        k_pe = rope_2d(k_pe, ang)
    q = jnp.concatenate([q_nope, q_pe], axis=-1)
    k = jnp.concatenate([k_nope, jnp.broadcast_to(k_pe, (b_, MLA_HEADS, L, MLA_ROPE))], axis=-1)
    return q, k, v

def softmax_attend(q, k, v):
    s = jnp.einsum('bhqe,bhke->bhqk', q, k, preferred_element_type=jnp.float32) * MLA_SCALE
    p = jax.nn.softmax(s, axis=-1)
    return jnp.einsum('bhqk,bhkv->bhqv', p.astype(v.dtype), v)

def blocked_attend(q, k, v):
    b_, h_, L, e = q.shape
    nb = L // Q_BLOCK
    qb = jnp.moveaxis(q.reshape(b_, h_, nb, Q_BLOCK, e), 2, 0)
    o = lax.map(lambda qq: softmax_attend(qq, k, v), qb)
    return jnp.moveaxis(o, 0, 2).reshape(b_, h_, L, v.shape[-1])

def merge_branches(a, m, gate_a, gate_b, w_pa, w_pb, w_o):
    mixed = jax.nn.sigmoid(gate_a) * (a @ w_pa) + jax.nn.sigmoid(gate_b) * (m @ w_pb)
    return mixed @ w_o

def token_mixer(hc, hx, ang, lb_f, lb_b, w_in, hg_norm_g, q_norm_g, kv_norm_g, w_uq, w_ukv, w_pa, w_pb, w_o, need_ctx):
    qc, ic, ffc, fbc, gc, dqc, dkvc, gac, gbc = split_in(hc @ w_in)
    qx, ix, ffx, fbx, gx, dqx, dkvx, gax, gbx = split_in(hx @ w_in)
    hg = lambda t: to_heads(t, HG_HEADS).astype(jnp.float32)
    qc4, ic4, qx4, ix4 = hg(qc), hg(ic), hg(qx), hg(ix)
    ocf, oxf = hgrn2_direction(qc4, ic4, hg(ffc), qx4, ix4, hg(ffx), lb_f, False)
    ocb, oxb = hgrn2_direction(qc4, ic4, hg(fbc), qx4, ix4, hg(fbx), lb_b, True)
    a_x = hgrn2_readout(oxf + oxb, gx, hg_norm_g)
    q_c, k_c, v_c = mla_qkv(dqc, dkvc, q_norm_g, kv_norm_g, w_uq, w_ukv, None)
    q_x, k_x, v_x = mla_qkv(dqx, dkvx, q_norm_g, kv_norm_g, w_uq, w_ukv, ang)
    m_x = from_heads(blocked_attend(q_x, jnp.concatenate([k_c, k_x], axis=2), jnp.concatenate([v_c, v_x], axis=2)))
    y_x = merge_branches(a_x, m_x, gax, gbx, w_pa, w_pb, w_o)
    if not need_ctx:
        return None, y_x
    a_c = hgrn2_readout(ocf + ocb, gc, hg_norm_g)
    m_c = from_heads(softmax_attend(q_c, k_c, v_c))
    y_c = merge_branches(a_c, m_c, gac, gbc, w_pa, w_pb, w_o)
    return y_c, y_x

def moe_ffn(h, w_router, router_bias, w_gate, w_up, w_down):
    n, d = h.shape
    scores = jax.nn.sigmoid(jnp.dot(h, w_router, preferred_element_type=jnp.float32))
    sel = (scores + router_bias.astype(jnp.float32)).reshape(n, N_GROUPS, EXPERTS_PER_GROUP)
    group_score = lax.top_k(sel, TOP_K)[0].sum(-1)
    g_idx = jnp.argmax(group_score, axis=-1).astype(jnp.int32)
    in_group = jnp.take_along_axis(sel, g_idx[:, None, None], axis=1)[:, 0]
    _, local = lax.top_k(in_group, TOP_K)
    experts = g_idx[:, None] * EXPERTS_PER_GROUP + local
    wts = jnp.take_along_axis(scores, experts, axis=1)
    wts = wts / jnp.sum(wts, axis=-1, keepdims=True)
    n_assign = n * TOP_K
    e_flat = experts.reshape(-1)
    tok = jnp.repeat(jnp.arange(n, dtype=jnp.int32), TOP_K)
    order = jnp.argsort(e_flat)
    e_s, tok_s, w_s = e_flat[order], tok[order], wts.reshape(-1)[order]
    counts = jnp.zeros((N_EXPERTS,), jnp.int32).at[e_flat].add(1)
    starts = jnp.cumsum(counts) - counts
    padded = (counts + MOE_BLOCK - 1) // MOE_BLOCK * MOE_BLOCK
    pad_ends = jnp.cumsum(padded)
    pad_starts = pad_ends - padded
    dest = pad_starts[e_s] + jnp.arange(n_assign, dtype=jnp.int32) - starts[e_s]
    n_blocks = -(-n_assign // MOE_BLOCK) + N_EXPERTS
    buf = jnp.zeros((n_blocks * MOE_BLOCK, d), h.dtype).at[dest].set(h[tok_s])
    block_expert = jnp.minimum(
        jnp.searchsorted(pad_ends, jnp.arange(n_blocks, dtype=jnp.int32) * MOE_BLOCK, side='right'),
        N_EXPERTS - 1)

    def expert_block(args):
        xb, e = args
        return (jax.nn.silu(xb @ w_gate[e]) * (xb @ w_up[e])) @ w_down[e]

    yb = lax.map(expert_block, (buf.reshape(n_blocks, MOE_BLOCK, d), block_expert))
    y = yb.reshape(-1, d)[dest] * w_s[:, None].astype(h.dtype)
    return jnp.zeros_like(h).at[tok_s].add(y)

def setup_inputs(seed: int = 0) -> dict:
    key = jax.random.key(seed)
    ks = jax.random.split(key, 25)
    nrm = lambda k, shape, scale: jax.random.normal(k, shape, jnp.float32) * scale
    gain = lambda k, shape: 1.0 + 0.1 * jax.random.normal(k, shape, jnp.float32)
    return {
        'x': nrm(ks[0], (BATCH, SEQ, D_MODEL), 1.0),
        'c': nrm(ks[1], (BATCH, D_MODEL), 1.0),
        'ctx': nrm(ks[2], (BATCH, CTX_LEN, D_MODEL), 1.0),
        'c_ctx': nrm(ks[3], (D_MODEL,), 1.0),
        'w_mod': nrm(ks[4], (DEPTH, D_MODEL, 6 * D_MODEL), 0.5 * D_MODEL ** -0.5),
        'b_mod': nrm(ks[5], (DEPTH, 6 * D_MODEL), 0.02),
        'norm1_g': gain(ks[6], (DEPTH, D_MODEL)),
        'norm2_g': gain(ks[7], (DEPTH, D_MODEL)),
        'w_in': nrm(ks[8], (DEPTH, D_MODEL, IN_DIM), D_MODEL ** -0.5),
        'gamma_fwd': nrm(ks[9], (DEPTH, HG_HEADS * HG_DK), 1.0),
        'gamma_bwd': nrm(ks[10], (DEPTH, HG_HEADS * HG_DK), 1.0),
        'hg_norm_g': gain(ks[11], (DEPTH, HG_WIDTH)),
        'q_norm_g': gain(ks[12], (DEPTH, MLA_Q_RANK)),
        'kv_norm_g': gain(ks[13], (DEPTH, MLA_KV_RANK)),
        'w_uq': nrm(ks[14], (DEPTH, MLA_Q_RANK, MLA_HEADS * (MLA_NOPE + MLA_ROPE)), MLA_Q_RANK ** -0.5),
        'w_ukv': nrm(ks[15], (DEPTH, MLA_KV_RANK, MLA_HEADS * (MLA_NOPE + MLA_V)), MLA_KV_RANK ** -0.5),
        'w_pa': nrm(ks[16], (DEPTH, HG_WIDTH, D_MODEL), HG_WIDTH ** -0.5),
        'w_pb': nrm(ks[17], (DEPTH, MLA_WIDTH, D_MODEL), MLA_WIDTH ** -0.5),
        'w_o': nrm(ks[18], (DEPTH, D_MODEL, D_MODEL), D_MODEL ** -0.5),
        'w_router': nrm(ks[19], (D_MODEL, N_EXPERTS), D_MODEL ** -0.5),
        'router_bias': nrm(ks[20], (N_EXPERTS,), 0.01),
        'w_gate_e': nrm(ks[21], (DEPTH, N_EXPERTS, D_MODEL, D_EXPERT), D_MODEL ** -0.5),
        'w_up_e': nrm(ks[22], (DEPTH, N_EXPERTS, D_MODEL, D_EXPERT), D_MODEL ** -0.5),
        'w_down_e': nrm(ks[23], (DEPTH, N_EXPERTS, D_EXPERT, D_MODEL), D_EXPERT ** -0.5),
        'final_g': gain(ks[24], (D_MODEL,)),
    }

def reference(x, c, ctx, c_ctx, w_mod, b_mod, norm1_g, norm2_g, w_in, gamma_fwd, gamma_bwd, hg_norm_g,
              q_norm_g, kv_norm_g, w_uq, w_ukv, w_pa, w_pb, w_o, w_router, router_bias,
              w_gate_e, w_up_e, w_down_e, final_g):
    b_, n_lat, d = x.shape
    n_ctx = ctx.shape[1]
    ang = axial_angles(n_lat)
    zx, zc = x, ctx
    for l in range(DEPTH):
        last = l == DEPTH - 1
        mx = jnp.split(jax.nn.silu(c) @ w_mod[l] + b_mod[l], 6, axis=-1)
        mc = jnp.split(jax.nn.silu(c_ctx) @ w_mod[l] + b_mod[l], 6, axis=-1)
        hx = modulate(rmsnorm(zx, norm1_g[l]), mx[0][:, None], mx[1][:, None])
        hc = modulate(rmsnorm(zc, norm1_g[l]), mc[0], mc[1])
        yc, yx = token_mixer(hc, hx, ang, lower_bound(gamma_fwd, l), lower_bound(gamma_bwd, l), w_in[l],
                             hg_norm_g[l], q_norm_g[l], kv_norm_g[l], w_uq[l], w_ukv[l], w_pa[l], w_pb[l], w_o[l],
                             not last)
        zx = zx + mx[2][:, None] * yx
        hx = modulate(rmsnorm(zx, norm2_g[l]), mx[3][:, None], mx[4][:, None])
        if last:
            fx = moe_ffn(hx.reshape(-1, d), w_router, router_bias, w_gate_e[l], w_up_e[l], w_down_e[l]).reshape(b_, n_lat, d)
        else:
            zc = zc + mc[2] * yc
            hc = modulate(rmsnorm(zc, norm2_g[l]), mc[3], mc[4])
            f = moe_ffn(jnp.concatenate([hc, hx], axis=1).reshape(-1, d), w_router, router_bias,
                        w_gate_e[l], w_up_e[l], w_down_e[l]).reshape(b_, n_ctx + n_lat, d)
            zc = zc + mc[5] * f[:, :n_ctx]
            fx = f[:, n_ctx:]
        zx = zx + mx[5][:, None] * fx
    return rmsnorm(zx, final_g)


_drawn_inputs = setup_inputs


def setup_inputs(seed=0):
    import zlib

    import numpy as np

    out = dict(_drawn_inputs(seed))
    spreads = {}
    factors = {'q_norm_g': 8.0, 'kv_norm_g': 8.0, 'gamma_fwd': 3.076, 'gamma_bwd': 2.742}
    for name, (base, spread) in spreads.items():
        noise = np.random.default_rng([zlib.crc32(name.encode()), seed]).standard_normal(out[name].shape)
        drawn = base * np.exp(spread * noise) if base else spread * noise
        out[name] = jnp.asarray(drawn.astype(out[name].dtype))
    for name, factor in factors.items():
        out[name] = (out[name] * factor).astype(out[name].dtype)
    return out
```

```python
from contextlib import ExitStack

import numpy as np

import concourse.bass as bass
from concourse import mybir

ALU = mybir.AluOpType
ACT = mybir.ActivationFunctionType
F32 = mybir.dt.float32
I32 = mybir.dt.int32
U8 = mybir.dt.uint8
AX_X = mybir.AxisListType.X

P = 128
D = 1024
KD = D // P
NCTX, NX = 256, 256
T = NCTX + NX
TILES = T // P
DEPTH = 2
EPS = 1e-6
HEADS = 4
MH, NOPE, ROPE, MV = 8, 64, 32, 64
QK = NOPE + ROPE
QR, KVR = 384, 256
SCALE = QK ** -0.5
NE, NG, EG = 16, 4, 4
DE = 512
CAP = P
MOD = 6 * D
CH = 512
OFF = dict(q=0, i=512, ff=1024, fb=1536, g=2048, dq=2560, dkv=2944, ga=3232, gb=4256)
LEVELS = (64, 32, 16, 8, 4, 2, 1)
STEPS = [(m, h) for m in LEVELS for h in range(HEADS)]
ORDER = ((0, 1, 2, 3), (1, 0, 3, 2))
FAR = 10000.0

IN_LAYER_0 = dict(
    sq1=8, sq1_used=7, rs1=2, h1_n=8, h1=16, f_exp=8, v_ready=4, q_ready=4, g_exp=4, g_ready=4, dq_raw=3, ckv_raw=2,
    kpe_mul=2, kpe_ready=1, kpe_sw=1, uq_sw=3, kpe_in=8, k_gate=8, att_zero=2, logf=8, b_ready=8, att_in=64, exponent=56,
    decay=56, qk_ready=56, e_b=4, kd_exponent=8, kd_decay=8, kd_ready=8, qe_ready=2, kdT_ready=6, state=24, o_acc=8,
    o_sq=4, o_rs=8, a_ready=4, dq_sq=3, dq_sq_used=2, ckv_sq=2, ckv_sq_used=1, mla_rs=4, dq_n=3, ckv_n=2, q_rot=16,
    q_rope=8, k_ready=8, v2_ready=4, neg_max=32, p_exp=32, p_norm=32, pT_ready=32, m_ready=32, mix_exp=16, mix_a=8,
    mix_b=8, mixed=8, z_mixed=8, sq2=8, sq2_used=7, rs2=2, h2_n=8, h2=16, score_exp=1, htok=8, taken=1, nb_ready=1,
    z_ready=1)

VEC = {}
for _name, _rows in (("c", 8), ("c_ctx", 8), ("norm1_g", 16), ("norm2_g", 16), ("final_g", 8), ("hg_norm_g", 8),
                     ("q_norm_g", 6), ("kv_norm_g", 4), ("gamma_fwd", 8), ("gamma_bwd", 8)):
    VEC[_name] = (sum(r for _, r in VEC.values()), _rows)
NVEC = sum(r for _, r in VEC.values())
NBMOD = DEPTH * MOD // P


def first_token(l):
    return NCTX if l == DEPTH - 1 else 0


def attention_steps(l):
    return [(qt, h) for qt in range(first_token(l) // P, TILES) for h in range(MH)]


def psum_plan():
    turns = [(("vec", 0), "g", "vec_read", 1), (("vec", 1), "g", "vec_read", 2)]
    turns += [(("z", k), "g", "z_loaded", k + 1) for k in range(KD)]
    turns += [(("mod", l, j), "g", "mod_rows", l * 12 + j + 1) for l in range(DEPTH) for j in range(12)]
    turns += [(("modT",), "g", "mod_ready", 1)]
    for l in range(DEPTH):
        tiles = range(first_token(l) // P, TILES)
        turns += [(("ssq1", l), l, "rs1", 1)]
        turns += [(("f", l, d, h), l, "f_exp", d * HEADS + h + 1) for d in range(2) for h in range(HEADS)]
        turns += [(("v", l, t), l, "v_ready", t + 1) for t in range(TILES)]
        turns += [(("q", l, h), l, "q_ready", h + 1) for h in range(HEADS)]
        turns += [(("g", l, h), l, "g_ready", h + 1) for h in range(HEADS)]
        turns += [(("dq", l, k), l, "dq_raw", k + 1) for k in range(QR // P)]
        turns += [(("ckv", l, k), l, "ckv_raw", k + 1) for k in range(KVR // P)]
        turns += [(("kpe", l, s), l, "kpe_mul", s + 1) for s in range(2)]
        for d in range(2):
            turns += [(("diag", l, d, h), l, "att_in", d * 32 + h + 1) for h in range(HEADS)]
            turns += [(("lev", l, d, n), l, "att_in", d * 32 + HEADS + n + 1) for n in range(len(STEPS))]
            outs = 0
            for i, c in enumerate(ORDER[d]):
                if i < 3:
                    turns += [(("kdT", l, d, i), l, "kdT_ready", d * 3 + i + 1),
                              (("st", l, d, i), l, "state", (d * 3 + i + 1) * HEADS)]
                if c in tiles:
                    outs += 1
                    turns += [(("out", l, d, i), l, "o_acc", d * len(tiles) + outs)]
        turns += [(("ossq", l, h), l, "o_rs", 2 * h + 1) for h in range(HEADS)]
        turns += [(("qssq", l), l, "mla_rs", 1), (("kssq", l), l, "mla_rs", 3)]
        for h in range(MH):
            turns += [(("Q", l, h), l, "q_rot", 2 * h + 1), (("Qsw", l, h), l, "q_rot", 2 * h + 2)]
        turns += [(("K", l, h), l, "k_ready", h + 1) for h in range(MH)]
        turns += [(("V", l, t), l, "v2_ready", t + 1) for t in range(TILES)]
        nj = len(attention_steps(l))
        for j in range(nj + 2):
            if j < nj:
                turns += [(("sc", l, j), l, "p_exp", j + 1)]
            if 1 <= j <= nj:
                turns += [(("pT", l, j - 1), l, "pT_ready", j)]
            if j >= 2:
                turns += [(("pv", l, j - 2), l, "m_ready", j - 1)]
        for m in range(KD):
            turns += [(("pa", l, m), l, "mix_a", m + 1), (("ga", l, m), l, "mix_exp", 2 * m + 1),
                      (("pb", l, m), l, "mix_b", m + 1), (("gb", l, m), l, "mix_exp", 2 * m + 2)]
        turns += [(("y", l, m), l, "z_mixed", m + 1) for m in range(KD)]
        turns += [(("ssq2", l), l, "rs2", 1)]
        turns += [(("logit", l), l, "score_exp", 1)]
        turns += [(("hT", l, t, g), l, "htok", (t - tiles[0]) * 2 + g + 1) for t in tiles for g in range(2)]
        turns += [(("rank", l), l, "nb_ready", 1)]
    turns += [(("ssqf",), "g", "rsf", 1)]
    turns += [(("fin", t, g), "g", "fin_rows", t * 2 + g + 1) for t in range(NX // P) for g in range(2)]
    bank, nth, before, last = {}, {}, {}, {}
    for n, (turn, *freed) in enumerate(turns):
        b = n % 8
        bank[turn], nth[turn] = b, n // 8 + 1
        before[turn] = turns[n - 8][1:] if n >= 8 else None
    for n, (turn, *freed) in enumerate(turns):
        if turn[0] == "rank":
            last[turn[1]] = [turns[x][1:] for x in range(n - 7, n + 1)]
    return bank, nth, before, last


def weight_plan(a):
    units = []

    def rows(w):
        return w.rearrange("(k p) n -> p k n", p=P)

    for l in range(DEPTH):
        for j in range(12):
            units.append((("mod", l, j), j % 4, rows(a["w_mod"][l, :, j * CH:(j + 1) * CH]), ("mod", l, j)))
    for l in range(DEPTH):
        def w_in(name, width, shift=0):
            o = OFF[name] + shift
            return rows(a["w_in"][l, :, o:o + width])
        units += [
            (("ff", l), 0, w_in("ff", CH), ("f", l, 0, 3)), (("fb", l), 1, w_in("fb", CH), ("f", l, 1, 3)),
            (("i", l), 2, w_in("i", CH), ("v", l, 3)), (("q", l), 3, w_in("q", CH), ("q", l, 3)),
            (("g", l), 0, w_in("g", CH), ("g", l, 3)), (("dq", l), 1, w_in("dq", QR), ("dq", l, 2)),
            (("dkv", l), 2, w_in("dkv", KVR + ROPE), ("kpe", l, 1)),
            (("uq", l), 3, rows(a["w_uq"][l]), ("Qsw", l, 7)), (("ukv", l), 0, rows(a["w_ukv"][l]), ("V", l, 3)),
            (("pa", l), 1, rows(a["w_pa"][l]), ("pa", l, 7)), (("pb", l), 2, rows(a["w_pb"][l]), ("pb", l, 7)),
            (("ga0", l), 3, w_in("ga", CH), ("ga", l, 3)), (("gb0", l), 0, w_in("gb", CH), ("gb", l, 3)),
            (("ga1", l), 3, w_in("ga", CH, CH), ("ga", l, 7)), (("gb1", l), 0, w_in("gb", CH, CH), ("gb", l, 7)),
            (("o0", l), 1, rows(a["w_o"][l, :, 0:CH]), ("y", l, 3)), (("o1", l), 2, rows(a["w_o"][l, :, CH:D]), ("y", l, 7)),
        ]
    slot, landed, count = {}, {}, [0] * 4
    for unit, s, _, _ in units:
        count[s] += 1
        slot[unit], landed[unit] = s, 16 * count[s]
    return units, slot, landed


def bass_hybrid_transformer(nc, a, out):
    bank, nth, before, last_turns = psum_plan()
    units, slot_of, landed_at = weight_plan(a)

    with ExitStack() as ctx:
        def sb(name, shape, dt=F32):
            return ctx.enter_context(nc.sbuf_tensor(name, shape, dt))

        sems = {}

        def S(name, l="g"):
            if name in IN_LAYER_0:
                l = "layers"
            if (name, l) not in sems:
                sems[name, l] = ctx.enter_context(nc.semaphore(f"{name}_{l}"))
            return sems[name, l]

        def at(name, l, value):
            return S(name, l), value + (IN_LAYER_0[name] if name in IN_LAYER_0 and l else 0)

        banks = ctx.enter_context(nc.psum_tensor("banks", [P, 8, 512], F32))
        bank_full = [ctx.enter_context(nc.semaphore(f"bank_full{b}")) for b in range(8)]
        slot_landed = [ctx.enter_context(nc.semaphore(f"slot_landed{s}")) for s in range(4)]

        ident = sb("ident_sb", [P, P])
        ones = sb("ones_sb", [P, P])
        before_m = sb("before_sb", [P, P])
        slot_no = sb("slot_no_sb", [P, P])
        masks = sb("masks_sb", [P, 2, 8, P], U8)
        rope = sb("rope_sb", [P, 2, T])
        vrows = sb("vrows", [P, 2, P])
        vecs = sb("vecs", [P, NVEC])
        bmod = sb("bmod", [P, NBMOD])
        eps = sb("eps", [P, 1])
        rbias = sb("rbias", [1, NE])
        rb = sb("rb", [P, NE])
        wr = sb("wr", [P, KD, NE])
        modT = sb("modT", [P, DEPTH, 48, 2])
        gainA = sb("gainA", [P, DEPTH, 2, KD, 2])
        lb = sb("lb", [P, 2, DEPTH, HEADS])
        oml = sb("oml", [P, 2, DEPTH, HEADS])
        small = sb("small", [P, 8, 16])
        silu_c = sb("silu_c", [P, 16])

        Z = sb("Z", [P, KD, T])
        H = sb("H", [P, KD, T])
        W = sb("W", [P, 4, KD * CH])
        V = sb("V", [P, TILES, 512])
        G = sb("G", [P, HEADS, T])
        O = sb("O", [P, HEADS, T])
        dq = sb("dq", [P, 3, T])
        ckv = sb("ckv", [P, 2, T])
        kpe = sb("kpe", [P, T])
        RS = sb("RS", [P, T])
        SQ = sb("SQ", [P, 2, T])
        kdT = SQ[:, 0, :].rearrange("p (h t) -> p h t", h=HEADS)
        state = SQ[:, 1, :].rearrange("p (h t) -> p h t", h=HEADS)
        mx = sb("mx", [P, 4, 32])
        ebl = sb("ebl", [P, HEADS, TILES])
        uq_pad = sb("uq_pad", [P, NOPE + 3 * MH * ROPE])
        kpe_pad = sb("kpe_pad", [P, NOPE + KD * ROPE])
        uq_sw = uq_pad[:, NOPE:].rearrange("p (k h c) -> p k h c", k=3, h=MH)
        kpe_sw = kpe_pad[:, NOPE:].rearrange("p (k c) -> p k c", k=KD)
        arena = sb("arena", [P, 6 * 2048 + 1024])

        def part(first, n, shape, **sizes):
            return arena[:, first * 2048:first * 2048 + n].rearrange(shape, **sizes)

        q = part(0, 2048, "p (h t) -> p h t", h=HEADS)
        F = [part(1 + d, 2048, "p (h t) -> p h t", h=HEADS) for d in range(2)]
        K = part(3, 2048, "p (h t) -> p h t", h=HEADS)
        Ex = part(4, 2048, "p (h t) -> p h t", h=HEADS)
        att = part(5, 2048, "p (h t) -> p h t", h=HEADS)
        QKd = part(6, 1024, "p (h t) -> p h t", h=2)
        QT = part(0, 4096, "p (h t) -> p h t", h=MH)
        KT = part(2, 4096, "p (h t) -> p h t", h=MH)
        V2 = part(4, 2048, "p (t c) -> p t c", t=TILES)
        PR = part(5, 1024, "p (r t) -> p r t", r=2)
        PT = arena[:, 5 * 2048 + 1024:6 * 2048].rearrange("p (r t) -> p r t", r=2)
        tmpQ = SQ
        MT = V
        mix = part(0, 4096, "p (k t) -> p k t", k=KD)
        mixT = part(4, 2048, "p (r t) -> p r t", r=4)
        htok = part(2, 4096, "p (t n) -> p t n", t=TILES)
        sel = part(0, 512, "p (t s) -> p t s", t=TILES)
        selw = arena[:, 512:1024].rearrange("p (t s) -> p t s", t=TILES)
        selT = arena[:, 1024:1536]
        xsT = arena[:, 1536:2560].rearrange("p (k s) -> p k s", k=KD)
        hidden = arena[:, 2560:3072]
        gate_t = arena[:, 3072:3584]
        yd = part(4, 1024, "p (n) -> p n")
        rt = arena[:, 5 * 2048:5 * 2048 + 1024].rearrange("p (a t e) -> p a t e", a=16, t=TILES)
        pos = arena[:, 5 * 2048 + 1024:5 * 2048 + 1024 + 68].rearrange("p (t e) -> p t e", t=TILES)
        gw = arena[:, 5 * 2048 + 1100:5 * 2048 + 1168].rearrange("p (t e) -> p t e", t=TILES)
        modrows = arena[:, 0:DEPTH * MOD]
        masks_in = O[:, :, :].rearrange("p h t -> p (h t)").bitcast(I32)
        ztok = H[:, :, :].rearrange("p k t -> p (k t)").rearrange("p (t n) -> p t n", t=TILES)
        nbi = sb("nbi", [P, 1], I32)
        cnt = sb("cnt", [P, 8])

        def slot(unit, cols):
            return W[:, slot_of[unit], 0:KD * CH // cols * cols].rearrange("p (k n) -> p k n", n=cols)

        def read(eng, turn):
            eng.wait_ge(bank_full[bank[turn]], nth[turn])
            return banks[:, bank[turn], :]

        def vec(name):
            first, n = VEC[name]
            return vecs[:, first:first + n]

        def Nx(l):
            return slice(first_token(l), T)

        block = ctx.enter_context(nc.Block())

        @block.sync
        def _(sp):
            for t in range(2):
                sp.dma_start(ztok[:, t, :], a["ctx"][0, t * P:(t + 1) * P, :]).then_inc(S("x_in"), 16)
                sp.dma_start(ztok[:, 2 + t, :], a["x"][0, t * P:(t + 1) * P, :]).then_inc(S("x_in"), 16)
            for dst, src in ((ident, "k_ident"), (ones, "k_ones"), (before_m, "k_before"), (slot_no, "k_slot"),
                             (masks_in, "k_masks"), (rope, "k_rope")):
                sp.dma_start(dst[:, :, :] if len(dst.shape) == 3 else dst[:, :], a[src]).then_inc(S("consts"), 16)
            for name, (first, n) in VEC.items():
                src = a[name]
                if len(src.shape) == 2:
                    src = src.rearrange("a n -> (a n)")
                sp.dma_start(vrows[first:first + n, 0, :], src.rearrange("(r p) -> r p", p=P)).then_inc(S("consts"), 16)
            sp.dma_start(vrows[0:NBMOD, 1, :], a["b_mod"].rearrange("l (r p) -> (l r) p", p=P)).then_inc(S("consts"), 16)
            sp.dma_start(rbias[:], a["router_bias"].rearrange("(o n) -> o n", o=1)).then_inc(S("consts"), 16)
            sp.dma_start(wr[:], a["w_router"].rearrange("(k p) n -> p k n", p=P)).then_inc(S("consts"), 16)

            previous = [None] * 4

            def load(n):
                unit, s, src, last = units[n]
                if previous[s]:
                    sp.wait_ge(bank_full[bank[previous[s]]], nth[previous[s]])
                previous[s] = last
                k, cols = src.shape[1], src.shape[2]
                sp.dma_start(W[:, s, 0:k * cols].rearrange("p (k n) -> p k n", n=cols), src).then_inc(slot_landed[s], 16)

            n = 0
            for _ in range(24):
                load(n)
                n += 1
            for l in range(DEPTH):
                for _ in range(17):
                    load(n)
                    n += 1
                for s in range(3):
                    sp.wait_ge(bank_full[bank[previous[s]]], nth[previous[s]])
                sp.wait_ge(*at("nb_ready", l, 1))
                nb = sp.value_load(nbi[0:1, 0:1], min_val=1, max_val=4)
                with sp.Fori(0, nb) as r:
                    with sp.Fori(0, NE) as e:
                        for s, (w, name) in enumerate((("w_gate_e", "gate"), ("w_up_e", "up"), ("w_down_e", "down"))):
                            sp.wait_ge(*at(f"{name}_used", l, r * NE + e + 1))
                            cols = CH if s < 2 else D
                            src = a[w][l, bass.ds(e, 1)].rearrange("o (k p) n -> p (o k) n", p=P)
                            sp.dma_start(W[:, s, :].rearrange("p (k n) -> p k n", n=cols), src) \
                              .then_inc(S(f"{name}_in", l), 16)
                for name in ("gate", "up", "down"):
                    sp.wait_ge(*at(f"{name}_used", l, nb * NE + 1))
                previous = [None] * 3 + [previous[3]]
            sp.wait_ge(*at("fin_rows", "g", 4))
            for t in range(NX // P):
                sp.dma_start(out[0, t * P:(t + 1) * P, :], ztok[:, t, :]).then_inc(S("out"), 16)
            sp.wait_ge(*at("out", "g", 16 * (NX // P)))

        N_CONSTS = 16 * (6 + len(VEC) + 3)

        @block.tensor
        def _(pe):
            mm = nc.tensor.matmul

            def claim(turn):
                if before[turn]:
                    l, name, value = before[turn]
                    pe.wait_ge(*at(name, l, value))
                return banks[:, bank[turn], :]

            def full(ins, turn):
                ins.then_inc(bank_full[bank[turn]], 1)

            def landed(unit):
                pe.wait_ge(slot_landed[slot_of[unit]], landed_at[unit])

            pe.wait_ge(*at("consts", "g", N_CONSTS))
            for i, n in ((0, NVEC), (1, NBMOD)):
                o = claim(("vec", i))
                x = nc.tensor.transpose(o[:, 0:n], vrows[0:n, i, :], ident[0:n, 0:n])
                if i == 0:
                    x = mm(o[:, 256:256 + NE], ones[0:1, :], rbias[0:1, :], start=True, stop=True)
                full(x, ("vec", i))
            pe.wait_ge(*at("x_in", "g", 64))
            for k in range(KD):
                o = claim(("z", k))
                for t in range(TILES):
                    x = nc.tensor.transpose(o[:, t * P:(t + 1) * P], ztok[:, t, k * P:(k + 1) * P], ident[:, :])
                full(x, ("z", k))
            pe.wait_ge(*at("silu_c", "g", 1))
            sc = silu_c[:, :].rearrange("p (v k) -> p k v", v=2)
            for l in range(DEPTH):
                for j in range(12):
                    u = ("mod", l, j)
                    o = claim(u)
                    landed(u)
                    w = slot(u, CH)
                    for k in range(KD):
                        x = mm(o[0:2, :], sc[:, k, :], w[:, k, :], start=(k == 0), stop=(k == KD - 1))
                    full(x, u)
            o = claim(("modT",))
            pe.wait_ge(*at("mod_rows", "g", 24))
            for n in range(DEPTH * 48):
                x = nc.tensor.transpose(o[:, 2 * n:2 * n + 2], modrows[0:2, n * P:(n + 1) * P], ident[0:2, 0:2])
            full(x, ("modT",))

            def sum_squares(turn, l, sem, cols, tiles=KD):
                o = claim(turn)
                for k in range(tiles):
                    pe.wait_ge(*at(sem, l, k + 1))
                    x = mm(o[:, cols], ones[:, :], SQ[:, k % 2, cols], start=(k == 0), stop=(k == tiles - 1))
                    if k < tiles - 1:
                        x.then_inc(S(sem + "_used", l), 1)
                full(x, turn)

            def project(turn, unit, width, c0, m, cols, kt=KD, rhs=None):
                o = claim(turn)
                landed(unit)
                w = slot(unit, width)
                rhs = H if rhs is None else rhs
                for k in range(kt):
                    x = mm(o[0:m, cols], w[:, k, c0:c0 + m], rhs[:, k, cols], start=(k == 0), stop=(k == kt - 1))
                full(x, turn)

            for l in range(DEPTH):
                every, some = slice(0, T), Nx(l)
                tiles = range(first_token(l) // P, TILES)
                if l:
                    pe.wait_ge(*at("z_ready", l - 1, 1))
                sum_squares(("ssq1", l), l, "sq1", every)
                pe.wait_ge(*at("h1", l, 2 * KD))
                for d, u in ((0, "ff"), (1, "fb")):
                    for h in range(HEADS):
                        project(("f", l, d, h), (u, l), CH, h * P, P, every)
                landed(("i", l))
                for t in range(TILES):
                    o = claim(("v", l, t))
                    for k in range(KD):
                        x = mm(o[:, :], H[:, k, t * P:(t + 1) * P], slot(("i", l), CH)[:, k, :],
                               start=(k == 0), stop=(k == KD - 1))
                    full(x, ("v", l, t))
                for h in range(HEADS):
                    project(("q", l, h), ("q", l), CH, h * P, P, some)
                for h in range(HEADS):
                    project(("g", l, h), ("g", l), CH, h * P, P, some)
                for k in range(3):
                    project(("dq", l, k), ("dq", l), QR, k * P, P, some)
                for k in range(2):
                    project(("ckv", l, k), ("dkv", l), KVR + ROPE, k * P, P, every)
                project(("kpe", l, 0), ("dkv", l), KVR + ROPE, KVR - NOPE, QK, every)
                o = claim(("kpe", l, 1))
                pe.wait_ge(*at("kpe_sw", l, 1))
                for k in range(KD):
                    x = mm(o[0:QK, :], kpe_pad[:, k * ROPE:k * ROPE + QK], H[:, k, :],
                           start=(k == 0), stop=(k == KD - 1))
                full(x, ("kpe", l, 1))

                for d in range(2):
                    pe.wait_ge(*at("q_ready", l, HEADS))
                    for h in range(HEADS):
                        o = claim(("diag", l, d, h))
                        pe.wait_ge(*at("k_gate", l, d * HEADS + h + 1))
                        for c in tiles:
                            s = slice(c * P, (c + 1) * P)
                            x = mm(o[:, s], K[:, h, s], q[:, h, s], start=True, stop=True)
                        full(x, ("diag", l, d, h))
                    for n in range(len(STEPS)):
                        o = claim(("lev", l, d, n))
                        pe.wait_ge(*at("qk_ready", l, d * len(STEPS) + n + 1))
                        for c in tiles:
                            s = slice(c * P, (c + 1) * P)
                            x = mm(o[:, s], QKd[:, n % 2, s], QKd[:, n % 2, s], start=True, stop=True)
                        full(x, ("lev", l, d, n))
                    for i, c in enumerate(ORDER[d]):
                        s = slice(c * P, (c + 1) * P)
                        if i < 3:
                            o = claim(("kdT", l, d, i))
                            pe.wait_ge(*at("kd_ready", l, (d + 1) * HEADS))
                            for h in range(HEADS):
                                x = nc.tensor.transpose(o[:, h * P:(h + 1) * P], K[:, h, s], ident[:, :])
                            full(x, ("kdT", l, d, i))
                            o = claim(("st", l, d, i))
                            pe.wait_ge(*at("kdT_ready", l, d * 3 + i + 1))
                            pe.wait_ge(*at("v_ready", l, TILES))
                            for h in range(HEADS):
                                x = mm(o[:, h * P:(h + 1) * P], kdT[:, h, :], V[:, c, h * P:(h + 1) * P], start=True, stop=True)
                            full(x, ("st", l, d, i))
                        if c in tiles:
                            o = claim(("out", l, d, i))
                            pe.wait_ge(*at("att_in", l, d * 32 + 32))
                            pe.wait_ge(*at("qe_ready", l, d + 1))
                            if i:
                                pe.wait_ge(*at("state", l, (d * 3 + i) * HEADS))
                            for h in range(HEADS):
                                hp = slice(h * P, (h + 1) * P)
                                x = mm(o[:, hp], V[:, c, hp], att[:, h, s], start=True, stop=(i == 0))
                                if i:
                                    x = mm(o[:, hp], state[:, h, :], Ex[:, h, s], start=False, stop=True)
                            full(x, ("out", l, d, i))
                for h in range(HEADS):
                    o = claim(("ossq", l, h))
                    pe.wait_ge(*at("o_sq", l, h + 1))
                    full(mm(o[:, some], ones[:, :], SQ[:, h % 2, some], start=True, stop=True), ("ossq", l, h))

                sum_squares(("qssq", l), l, "dq_sq", some, 3)
                sum_squares(("kssq", l), l, "ckv_sq", every, 2)
                pe.wait_ge(*at("dq_n", l, 3))
                pe.wait_ge(*at("uq_sw", l, 3))
                for h in range(MH):
                    project(("Q", l, h), ("uq", l), MH * QK, h * QK, QK, some, 3, dq)
                    o = claim(("Qsw", l, h))
                    for k in range(3):
                        x = mm(o[0:QK, some], uq_pad[:, (k * MH + h) * ROPE:(k * MH + h) * ROPE + QK], dq[:, k, some],
                               start=(k == 0), stop=(k == 2))
                    full(x, ("Qsw", l, h))
                pe.wait_ge(*at("ckv_n", l, 2))
                for h in range(MH):
                    project(("K", l, h), ("ukv", l), MH * P, h * P, NOPE, every, 2, ckv)
                for t in range(TILES):
                    o = claim(("V", l, t))
                    w = slot(("ukv", l), MH * P)
                    for k in range(2):
                        x = mm(o[:, :].rearrange("p (h c) -> p h c", h=MH), ckv[:, k, t * P:(t + 1) * P],
                               w[:, k, :].rearrange("p (h c) -> p h c", h=MH)[:, :, NOPE:P],
                               start=(k == 0), stop=(k == 1))
                    full(x, ("V", l, t))
                steps = attention_steps(l)
                pe.wait_ge(*at("q_rope", l, MH))
                pe.wait_ge(*at("k_ready", l, MH))
                pe.wait_ge(*at("kpe_in", l, MH))
                for j in range(len(steps) + 2):
                    if j < len(steps):
                        qt, h = steps[j]
                        keys = NCTX if qt < 2 else T
                        o = claim(("sc", l, j))
                        full(mm(o[:, 0:keys], QT[0:QK, h, qt * P:(qt + 1) * P], KT[0:QK, h, 0:keys],
                                start=True, stop=True), ("sc", l, j))
                    if 1 <= j <= len(steps):
                        qt, h = steps[j - 1]
                        o = claim(("pT", l, j - 1))
                        pe.wait_ge(*at("p_norm", l, j))
                        for k in range(2 if qt < 2 else 4):
                            x = nc.tensor.transpose(o[:, k * P:(k + 1) * P], PR[:, (j - 1) % 2, k * P:(k + 1) * P], ident[:, :])
                        full(x, ("pT", l, j - 1))
                    if j >= 2:
                        qt, h = steps[j - 2]
                        o = claim(("pv", l, j - 2))
                        pe.wait_ge(*at("pT_ready", l, j - 1))
                        pe.wait_ge(*at("v2_ready", l, TILES))
                        n = 2 if qt < 2 else 4
                        for k in range(n):
                            x = mm(o[:, 0:P], V2[:, k, h // 2 * P:(h // 2 + 1) * P], PT[:, (j - 2) % 2, k * P:(k + 1) * P],
                                   start=(k == 0), stop=(k == n - 1))
                        full(x, ("pv", l, j - 2))

                pe.wait_ge(*at("a_ready", l, HEADS))
                pe.wait_ge(*at("m_ready", l, len(steps)))
                for m in range(KD):
                    c0 = m % 4 * P
                    project(("pa", l, m), ("pa", l), D, m * P, P, some, 4, O)
                    project(("ga", l, m), (f"ga{m // 4}", l), CH, c0, P, some)
                    project(("pb", l, m), ("pb", l), D, m * P, P, some, 4, MT)
                    project(("gb", l, m), (f"gb{m // 4}", l), CH, c0, P, some)
                pe.wait_ge(*at("mixed", l, KD))
                for m in range(KD):
                    project(("y", l, m), (f"o{m // 4}", l), CH, m % 4 * P, P, some, KD, mix)
                sum_squares(("ssq2", l), l, "sq2", some)
                pe.wait_ge(*at("h2", l, 2 * KD if l == 0 else KD))
                o = claim(("logit", l))
                for n, t in enumerate(tiles):
                    for k in range(KD):
                        x = mm(o[:, n * NE:(n + 1) * NE], H[:, k, t * P:(t + 1) * P], wr[:, k, :],
                               start=(k == 0), stop=(k == KD - 1))
                full(x, ("logit", l))
                for t in tiles:
                    for g in range(2):
                        o = claim(("hT", l, t, g))
                        for k in range(4):
                            x = nc.tensor.transpose(o[:, k * P:(k + 1) * P], H[:, 4 * g + k, t * P:(t + 1) * P], ident[:, :])
                        full(x, ("hT", l, t, g))
                o = claim(("rank", l))
                pe.wait_ge(*at("taken", l, 1))
                n = len(tiles)
                for i in range(n):
                    for j in range(i + 1):
                        mm(o[:, i * NE:(i + 1) * NE], (before_m if j == i else ones)[:, :], rt[:, 0, j, :],
                           start=(j == 0), stop=(j == i))
                for j in range(n):
                    x = mm(o[:, n * NE:(n + 1) * NE], ones[:, :], rt[:, 0, j, :], start=(j == 0), stop=(j == n - 1))
                full(x, ("rank", l))

                bX, bST, bG, bU, bC = (0, 1), 2, 3, 4, (5, 6)
                for ll, name, value in last_turns[l]:
                    pe.wait_ge(*at(name, ll, value))
                pe.wait_ge(*at("htok", l, 2 * n))
                nb = pe.value_load(nbi[0:1, 0:1], min_val=1, max_val=4)

                def gather(it):
                    pe.wait_ge(*at("sel", l, it + 1))
                    for k in range(KD):
                        for j in range(n):
                            x = mm(banks[:, bX[k // 4], k % 4 * P:(k % 4 + 1) * P], htok[:, j, k * P:(k + 1) * P],
                                   sel[:, j, :], start=(j == 0), stop=(j == n - 1))
                    x.then_inc(S("gathered", l), 1)

                for name in ("gate", "up", "down"):
                    pe.nop().then_inc(S(f"{name}_used", l), 1)
                gather(0)
                with pe.Fori(0, nb) as r:
                    with pe.Fori(0, NE) as e:
                        it = r * NE + e
                        wg, wu = (W[:, s, :].rearrange("p (k n) -> p k n", n=CH) for s in (0, 1))
                        wd = W[:, 2, :].rearrange("p (k n) -> p k n", n=D)
                        pe.wait_ge(*at("xs_ready", l, it * 2 + 2))
                        for w, b, name in ((wg, bG, "gate"), (wu, bU, "up")):
                            pe.wait_ge(*at(f"{name}_in", l, (it + 1) * 16))
                            for f in range(4):
                                for k in range(KD):
                                    x = mm(banks[:, b, f * P:(f + 1) * P], w[:, k, f * P:(f + 1) * P], xsT[:, k, :],
                                           start=(k == 0), stop=(k == KD - 1))
                            x.then_inc(S(f"{name}_used", l), 1)
                        pe.wait_ge(*at("selw", l, it + 1))
                        for j in range(n):
                            x = nc.tensor.transpose(banks[:, bST, j * P:(j + 1) * P], selw[:, j, :], ident[:, :])
                        x.then_inc(S("selT_full", l), 1)
                        pe.wait_ge(*at("hidden", l, it + 1))
                        pe.wait_ge(*at("down_in", l, (it + 1) * 16))
                        for half in range(2):
                            for f in range(4):
                                x = mm(banks[:, bX[half], :], hidden[:, f * P:(f + 1) * P], wd[:, f, half * CH:(half + 1) * CH],
                                       start=(f == 0), stop=(f == 3))
                            if half == 0:
                                x.then_inc(S("y0_full", l), 1)
                        x.then_inc(S("down_used", l), 1)
                        pe.wait_ge(*at("yd_ready", l, it * 2 + 2))
                        pe.wait_ge(*at("selT", l, it + 1))
                        for k in range(KD):
                            if k >= 2:
                                pe.wait_ge(*at("z_added", l, it * KD + k - 1))
                            x = mm(banks[:, bC[k % 2], 0:n * P], yd[:, k * P:(k + 1) * P], selT[:, 0:n * P], start=True, stop=True)
                            x.then_inc(S("combined", l), 1)
                        gather(it + 1)
                        pe.wait_ge(*at("z_added", l, it * KD + KD))
                pe.wait_ge(*at("xs_ready", l, nb * NE * 2 + 2))

            pe.wait_ge(*at("z_ready", DEPTH - 1, 1))
            sum_squares(("ssqf",), "g", "sqf", slice(NCTX, T))
            pe.wait_ge(*at("zf", "g", KD))
            for t in range(NX // P):
                for g in range(2):
                    o = claim(("fin", t, g))
                    for k in range(4):
                        s = slice(NCTX + t * P, NCTX + (t + 1) * P)
                        x = nc.tensor.transpose(o[:, k * P:(k + 1) * P], Z[:, 4 * g + k, s], ident[:, :])
                    full(x, ("fin", t, g))

        @block.scalar
        def _(act):
            fn = nc.scalar.activation

            def squares(src, l, sem, cols, tiles=KD):
                for k in range(tiles):
                    if k >= 2:
                        act.wait_ge(*at(sem + "_used", l, k - 1))
                    fn(SQ[:, k % 2, cols], src[:, k, cols], ACT.Square).then_inc(S(sem, l), 1)

            def rsqrt(dst, turn, l, sem, n, cols, first=0):
                o = read(act, turn)
                fn(dst, o[:, cols], ACT.Ln, bias=eps[:, 0:1], scale=1.0 / n).then_inc(S(sem, l), 1)
                act.wait_ge(*at(sem, l, first + 1))
                fn(dst, dst, ACT.Exp, scale=-0.5).then_inc(S(sem, l), 1)

            act.wait_ge(*at("vec_read", "g", 2))
            fn(silu_c[:, :], vecs[:, 0:16], ACT.Exp, scale=-1.0).then_inc(S("c_exp"), 1)
            act.wait_ge(*at("gam_in", "g", 1))
            fn(small[:, 3, :], small[:, 3, :], ACT.Exp).then_inc(S("gam_exp"), 1)
            for l in range(DEPTH):
                for j in range(12):
                    o = read(act, ("mod", l, j))
                    fn(modrows[0:2, (l * 12 + j) * CH:(l * 12 + j + 1) * CH], o[0:2, :], ACT.Copy).then_inc(S("mod_rows"), 1)

            def modulate(l, sem, n_norm, vecs_):
                for k in range(KD):
                    act.wait_ge(*at(sem + "_n", l, k + 1))
                    for v in vecs_:
                        s = slice(v * NCTX, (v + 1) * NCTX)
                        fn(H[:, k, s], H[:, k, s], ACT.Identity, bias=modT[:, l, n_norm * 24 + k, v:v + 1],
                           scale=gainA[:, l, n_norm, k, v:v + 1]).then_inc(S(sem, l), 1)

            for l in range(DEPTH):
                every, some = slice(0, T), Nx(l)
                tiles = range(first_token(l) // P, TILES)
                if l == 0:
                    act.wait_ge(*at("z_loaded", "g", KD))
                    act.wait_ge(*at("eps", "g", 1))
                else:
                    act.wait_ge(*at("z_ready", l - 1, 1))
                squares(Z, l, "sq1", every)
                rsqrt(RS[:, :], ("ssq1", l), l, "rs1", D, every)
                if l == 0:
                    act.wait_ge(*at("gains", "g", 1))
                modulate(l, "h1", 0, (0, 1))
                for d in range(2):
                    for h in range(HEADS):
                        o = read(act, ("f", l, d, h))
                        fn(F[d][:, h, :], o, ACT.Exp, scale=-1.0).then_inc(S("f_exp", l), 1)
                for h in range(HEADS):
                    o = read(act, ("q", l, h))
                    fn(q[:, h, some], o[:, some], ACT.Copy).then_inc(S("q_ready", l), 1)
                for h in range(HEADS):
                    o = read(act, ("g", l, h))
                    fn(G[:, h, some], o[:, some], ACT.Exp, scale=-1.0).then_inc(S("g_exp", l), 1)
                for k in range(3):
                    o = read(act, ("dq", l, k))
                    fn(dq[:, k, some], o[:, some], ACT.Copy).then_inc(S("dq_raw", l), 1)
                for k in range(2):
                    o = read(act, ("ckv", l, k))
                    fn(ckv[:, k, :], o, ACT.Copy).then_inc(S("ckv_raw", l), 1)
                for d in range(2):
                    for h in range(HEADS):
                        act.wait_ge(*at("k_gate", l, d * HEADS + h + 1))
                        fn(F[d][:, h, :], F[d][:, h, :], ACT.Ln).then_inc(S("logf", l), 1)
                    for n, (m, h) in enumerate(STEPS):
                        act.wait_ge(*at("exponent", l, d * len(STEPS) + n + 1))
                        v = Ex[:, n % 4, some].rearrange("p (b s m) -> p b s m", s=2, m=m)
                        qs = 1 - d
                        fn(v[:, :, 1 - qs, :], v[:, :, 1 - qs, :], ACT.Exp, scale=-1.0)
                        fn(v[:, :, qs, :], v[:, :, qs, :], ACT.Exp).then_inc(S("decay", l), 1)
                    act.wait_ge(*at("qk_ready", l, (d + 1) * len(STEPS)))
                    fn(Ex[:, :, some], F[d][:, :, some], ACT.Exp).then_inc(S("e_b", l), 1)
                    edge = P - 1 if d == 0 else 0
                    fn(ebl[:, :, :], F[d].rearrange("p h (c t) -> p h c t", t=P)[:, :, :, edge], ACT.Exp).then_inc(S("e_b", l), 1)
                    for h in range(HEADS):
                        act.wait_ge(*at("kd_exponent", l, d * HEADS + h + 1))
                        fn(QKd[:, h % 2, :], QKd[:, h % 2, :], ACT.Exp, scale=-1.0).then_inc(S("kd_decay", l), 1)
                    for i in range(3):
                        o = read(act, ("kdT", l, d, i))
                        if i:
                            read(act, ("st", l, d, i - 1))
                        elif d:
                            read(act, ("st", l, 0, 2))
                        fn(kdT[:, :, :].rearrange("p h t -> p (h t)"), o, ACT.Copy).then_inc(S("kdT_ready", l), 1)
                act.wait_ge(*at("o_acc", l, 2 * len(tiles)))
                for h in range(HEADS):
                    if h >= 2:
                        read(act, ("ossq", l, h - 2))
                    fn(SQ[:, h % 2, some], O[:, h, some], ACT.Square).then_inc(S("o_sq", l), 1)
                for h in range(HEADS):
                    rsqrt(Ex[:, h, some], ("ossq", l, h), l, "o_rs", P, some, 2 * h)
                squares(dq, l, "dq_sq", some, 3)
                rsqrt(RS[:, some], ("qssq", l), l, "mla_rs", QR, some)
                act.wait_ge(*at("dq_n", l, 3))
                squares(ckv, l, "ckv_sq", every, 2)
                rsqrt(RS[:, :], ("kssq", l), l, "mla_rs", KVR, every, 2)
                act.wait_ge(*at("a_ready", l, HEADS))
                for h in range(MH):
                    o = read(act, ("K", l, h))
                    fn(KT[0:NOPE, h, :], o[0:NOPE, :], ACT.Copy).then_inc(S("k_ready", l), 1)
                steps = attention_steps(l)
                for j in range(len(steps) + 1):
                    if j < len(steps):
                        keys = NCTX if steps[j][0] < 2 else T
                        act.wait_ge(*at("neg_max", l, j + 1))
                        o = read(act, ("sc", l, j))
                        fn(PR[:, j % 2, 0:keys], o[:, 0:keys], ACT.Exp, bias=mx[:, 1, j:j + 1], scale=SCALE,
                           accum_out=mx[:, 2, j:j + 1]).then_inc(S("p_exp", l), 1)
                    if j:
                        keys = NCTX if steps[j - 1][0] < 2 else T
                        o = read(act, ("pT", l, j - 1))
                        fn(PT[:, (j - 1) % 2, 0:keys], o[:, 0:keys], ACT.Copy).then_inc(S("pT_ready", l), 1)
                for m in range(KD):
                    for i, g in enumerate(("ga", "gb")):
                        o = read(act, (g, l, m))
                        if m >= 2:
                            act.wait_ge(*at("mixed", l, m - 1))
                        fn(mixT[:, m % 2 * 2 + i, some], o[:, some], ACT.Exp, scale=-1.0).then_inc(S("mix_exp", l), 1)
                act.wait_ge(*at("z_mixed", l, KD))
                squares(Z, l, "sq2", some)
                rsqrt(RS[:, some], ("ssq2", l), l, "rs2", D, some)
                modulate(l, "h2", 1, (0, 1) if l == 0 else (1,))
                n = len(tiles)
                o = read(act, ("logit", l))
                fn(rt[:, 1, 0:n, :], o[:, 0:n * NE].rearrange("p (t e) -> p t e", e=NE), ACT.Exp, scale=-1.0) \
                    .then_inc(S("score_exp", l), 1)
                for j, t in enumerate(tiles):
                    for g in range(2):
                        o = read(act, ("hT", l, t, g))
                        fn(htok[:, j, g * CH:(g + 1) * CH], o, ACT.Copy).then_inc(S("htok", l), 1)
                act.wait_ge(*at("nb_ready", l, 1))
                nb = act.value_load(nbi[0:1, 0:1], min_val=1, max_val=4)

                def take_gathered(it):
                    act.wait_ge(*at("gathered", l, it + 1))
                    for half in range(2):
                        fn(xsT[:, half * 4:half * 4 + 4, :].rearrange("p k s -> p (k s)"), banks[:, half, :], ACT.Copy) \
                            .then_inc(S("xs_ready", l), 1)

                take_gathered(0)
                with act.Fori(0, nb) as r:
                    with act.Fori(0, NE) as e:
                        it = r * NE + e
                        act.wait_ge(*at("gate_used", l, it + 2))
                        fn(gate_t, banks[:, 3, :], ACT.Exp, scale=-1.0).then_inc(S("gate_exp", l), 1)
                        act.wait_ge(*at("selT_full", l, it + 1))
                        fn(selT[:, 0:n * P], banks[:, 2, 0:n * P], ACT.Copy).then_inc(S("selT", l), 1)
                        act.wait_ge(*at("y0_full", l, it + 1))
                        fn(yd[:, 0:CH], banks[:, 0, :], ACT.Copy).then_inc(S("yd_ready", l), 1)
                        act.wait_ge(*at("down_used", l, it + 2))
                        fn(yd[:, CH:D], banks[:, 1, :], ACT.Copy).then_inc(S("yd_ready", l), 1)
                        take_gathered(it + 1)
            act.wait_ge(*at("z_ready", DEPTH - 1, 1))
            squares(Z, "g", "sqf", slice(NCTX, T))
            rsqrt(RS[:, NCTX:T], ("ssqf",), "g", "rsf", D, slice(NCTX, T))
            for t in range(NX // P):
                for g in range(2):
                    o = read(act, ("fin", t, g))
                    fn(ztok[:, t, g * CH:(g + 1) * CH], o, ACT.Copy).then_inc(S("fin_rows"), 1)

        @block.gpsimd
        def _(pool):
            nc.gpsimd.memset(uq_pad[:, 0:NOPE], 0.0)
            nc.gpsimd.memset(kpe_pad[:, 0:NOPE], 0.0)
            for l in range(DEPTH):
                def swapped(dst, src):
                    d4 = dst.rearrange("p h (a s i) -> p h a s i", a=2, s=2)
                    s4 = src.rearrange("p h (a s i) -> p h a s i", a=2, s=2)
                    for ax in range(2):
                        nc.gpsimd.tensor_scalar(d4[:, :, ax, 0, :], s4[:, :, ax, 1, :], -1.0, None, ALU.mult)
                        x = nc.gpsimd.tensor_copy(d4[:, :, ax, 1, :], s4[:, :, ax, 0, :])
                    return x

                u = ("dkv", l)
                pool.wait_ge(slot_landed[slot_of[u]], landed_at[u])
                swapped(kpe_sw[:, :, :], slot(u, KVR + ROPE)[:, 0:KD, KVR:KVR + ROPE]).then_inc(S("kpe_sw", l), 1)
                u = ("uq", l)
                pool.wait_ge(slot_landed[slot_of[u]], landed_at[u])
                if l:
                    read(pool, ("Qsw", l - 1, MH - 1))
                for k in range(3):
                    w = slot(u, MH * QK)[:, k, :].rearrange("p (h c) -> p h c", h=MH)
                    swapped(uq_sw[:, k, :, :], w[:, :, NOPE:QK]).then_inc(S("uq_sw", l), 1)
                pool.wait_ge(*at("uq_sw", l, 3))
                pool.wait_ge(*at("kpe_ready", l, 1))
                pool.wait_ge(*at("a_ready", l, HEADS))
                for h in range(MH):
                    nc.gpsimd.tensor_copy(KT[NOPE:QK, h, :], kpe[NOPE:QK, :]).then_inc(S("kpe_in", l), 1)

        @block.vector
        def _(dve):
            vv = nc.vector
            chain = [0]

            def link(ins):
                chain[0] += 1
                ins.then_inc(S("chain"), 1)
                dve.wait_ge(*at("chain", "g", chain[0]))

            vv.memset(eps[:], EPS).then_inc(S("eps"), 1)
            dve.wait_ge(*at("consts", "g", N_CONSTS))
            vv.tensor_copy(masks[:, :, :, :].rearrange("p d v t -> p (d v t)"), masks_in)
            o = read(dve, ("vec", 0))
            vv.tensor_copy(rb[:], o[:, 256:256 + NE])
            vv.tensor_copy(vecs[:], o[:, 0:NVEC]).then_inc(S("vec_read"), 1)
            o = read(dve, ("vec", 1))
            vv.tensor_copy(bmod[:], o[:, 0:NBMOD]).then_inc(S("vec_read"), 1)
            for k in range(KD):
                o = read(dve, ("z", k))
                vv.tensor_copy(Z[:, k, :], o).then_inc(S("z_loaded"), 1)
            dve.wait_ge(*at("c_exp", "g", 1))
            link(vv.tensor_scalar(silu_c[:], silu_c[:], 1.0, None, ALU.add))
            link(vv.reciprocal(silu_c[:], silu_c[:]))
            link(vv.tensor_tensor(small[:, 0, :], silu_c[:], vecs[:, 0:16], ALU.mult))
            link(vv.tensor_copy(silu_c[:, 0:8], small[:, 0, 8:16]))
            vv.tensor_copy(silu_c[:, 8:16], small[:, 0, 0:8]).then_inc(S("silu_c"), 1)
            for d, name in enumerate(("gamma_fwd", "gamma_bwd")):
                g = vec(name).rearrange("p (l h) -> p l h", l=DEPTH)
                e_, s_ = small[:, 3, 8 * d:8 * d + 8].rearrange("p (l h) -> p l h", l=2), small[:, 1 + d, 0:4]
                link(vv.tensor_tensor(s_, g[:, 0, :], g[:, 1, :], ALU.max))
                x = vv.tensor_tensor(e_, g, s_.unsqueeze(1).to_broadcast([P, 2, HEADS]), ALU.subtract)
            x.then_inc(S("gam_in"), 1)
            dve.wait_ge(*at("gam_exp", "g", 1))
            g4 = small[:, 3, :].rearrange("p (d l h) -> p d l h", d=2, l=2)
            s4 = small[:, 4, 0:8].rearrange("p (d h) -> p d h", d=2)
            link(vv.tensor_tensor(s4, g4[:, :, 0, :], g4[:, :, 1, :], ALU.add))
            link(vv.reciprocal(s4, s4))
            link(vv.tensor_tensor(g4, g4, s4.unsqueeze(2).to_broadcast([P, 2, 2, HEADS]), ALU.mult))
            link(vv.tensor_tensor(s4, g4[:, :, 0, :], g4[:, :, 1, :], ALU.add))
            vv.tensor_tensor(lb[:, :, 0, :], g4[:, :, 0, :], g4[:, :, 0, :], ALU.subtract)
            link(vv.tensor_tensor(lb[:, :, 1, :], s4, g4[:, :, 0, :], ALU.subtract))
            link(vv.tensor_scalar(oml[:], lb[:], -1.0, 1.0, ALU.mult, ALU.add))
            o = read(dve, ("modT",))
            link(vv.tensor_tensor(modT[:].rearrange("p l n v -> p (l n) v"), o[:, 0:2 * NBMOD].rearrange("p (n v) -> p n v", v=2),
                                  bmod[:, :].unsqueeze(2).to_broadcast([P, NBMOD, 2]), ALU.add))
            vv.tensor_copy(small[:, 5, 0:1], small[:, 4, 0:1]).then_inc(S("mod_ready"), 1)
            for l in range(DEPTH):
                for i, name in enumerate(("norm1_g", "norm2_g")):
                    first = VEC[name][0] + l * KD
                    x = vv.scalar_tensor_tensor(
                        out=gainA[:, l, i, :, :], in0=modT[:, l, i * 24 + 8:i * 24 + 16, :], scalar=1.0,
                        in1=vecs[:, first:first + KD].unsqueeze(2).to_broadcast([P, KD, 2]), op0=ALU.add, op1=ALU.mult)
            x.then_inc(S("gains"), 1)

            for l in range(DEPTH):
                every, some = slice(0, T), Nx(l)
                tiles = range(first_token(l) // P, TILES)
                n = len(tiles)
                halves = (0, 1) if l == 0 else (1,)
                dve.wait_ge(*at("rs1", l, 2))
                for k in range(KD):
                    vv.tensor_tensor(H[:, k, :], Z[:, k, :], RS[:, :], ALU.mult).then_inc(S("h1_n", l), 1)
                for d in range(2):
                    for h in range(HEADS):
                        f = F[d][:, h, :]
                        dve.wait_ge(*at("f_exp", l, d * HEADS + h + 1))
                        link(vv.tensor_scalar(f, f, 1.0, None, ALU.add))
                        link(vv.reciprocal(f, f))
                        link(vv.tensor_scalar(f, f, oml[:, d, l, h:h + 1], lb[:, d, l, h:h + 1], ALU.mult, ALU.add))
                        if d == 0:
                            vv.tensor_scalar(K[:, h, :], f, -1.0, 1.0, ALU.mult, ALU.add).then_inc(S("k_gate", l), 1)
                for t in range(TILES):
                    o = read(dve, ("v", l, t))
                    vv.tensor_copy(V[:, t, :], o).then_inc(S("v_ready", l), 1)
                for h in range(HEADS):
                    dve.wait_ge(*at("g_exp", l, h + 1))
                    g = G[:, h, some]
                    link(vv.tensor_scalar(g, g, 1.0, None, ALU.add))
                    link(vv.reciprocal(g, g))
                    o = read(dve, ("g", l, h))
                    vv.tensor_tensor(g, o[:, some], g, ALU.mult).then_inc(S("g_ready", l), 1)
                rp = slice(NOPE, QK)
                o = read(dve, ("kpe", l, 0))
                vv.tensor_tensor(kpe[rp, :], o[rp, :], rope[rp, 0, :], ALU.mult).then_inc(S("kpe_mul", l), 1)
                o = read(dve, ("kpe", l, 1))
                vv.tensor_tensor(RS[rp, :], o[rp, :], rope[rp, 1, :], ALU.mult).then_inc(S("kpe_mul", l), 1)
                dve.wait_ge(*at("kpe_mul", l, 2))
                vv.tensor_tensor(kpe[rp, :], kpe[rp, :], RS[rp, :], ALU.add).then_inc(S("kpe_ready", l), 1)

                for d in range(2):
                    if d:
                        for h in range(HEADS):
                            vv.tensor_scalar(K[:, h, :], F[1][:, h, :], -1.0, 1.0, ALU.mult, ALU.add).then_inc(S("k_gate", l), 1)
                    vv.memset(att[:, :, :], 0.0).then_inc(S("att_zero", l), 1)
                    for h in range(HEADS):
                        dve.wait_ge(*at("logf", l, d * HEADS + h + 1))
                        for c in range(TILES):
                            b = F[d][:, h, c * P:(c + 1) * P]
                            b = b if d == 0 else b[:, ::-1]
                            x = vv.tensor_tensor_scan(b, ones[:, :], b, 0.0, ALU.mult, ALU.add)
                        x.then_inc(S("b_ready", l), 1)
                    dve.wait_ge(*at("b_ready", l, (d + 1) * HEADS))
                    dve.wait_ge(*at("q_ready", l, HEADS))
                    dve.wait_ge(*at("att_zero", l, d + 1))

                    def insert(turn, level, h):
                        o = read(dve, turn)
                        vv.copy_predicated(
                            att[:, h, some].rearrange("p (c t) -> p c t", t=P),
                            masks[:, d, level, :].unsqueeze(1).to_broadcast([P, n, P]),
                            o[:, some].rearrange("p (c t) -> p c t", t=P)).then_inc(S("att_in", l), 1)

                    for h in range(HEADS):
                        insert(("diag", l, d, h), 7, h)
                    base = d * len(STEPS)
                    for i in range(len(STEPS) + 3):
                        if i >= 3:
                            m, h = STEPS[i - 3]
                            insert(("lev", l, d, i - 3), LEVELS.index(m), h)
                        if i < len(STEPS):
                            m, h = STEPS[i]
                            v = F[d][:, h, some].rearrange("p (b s m) -> p b s m", s=2, m=m)
                            mid = v[:, :, 0, m - 1:m] if d == 0 else v[:, :, 1, 0:1]
                            nbk = n * P // (2 * m)
                            vv.tensor_tensor(Ex[:, i % 4, some].rearrange("p (b m) -> p b m", m=2 * m),
                                             F[d][:, h, some].rearrange("p (b m) -> p b m", m=2 * m),
                                             mid.to_broadcast([P, nbk, 2 * m]), ALU.subtract).then_inc(S("exponent", l), 1)
                        if 1 <= i <= len(STEPS):
                            m, h = STEPS[i - 1]
                            dve.wait_ge(*at("decay", l, base + i))
                            split = lambda x: x.rearrange("p (b s m) -> p b s m", s=2, m=m)
                            qs = 1 - d
                            for src, s, last in ((q, qs, False), (K, 1 - qs, True)):
                                x = vv.tensor_tensor(split(QKd[:, (i - 1) % 2, some])[:, :, s, :],
                                                     split(src[:, h, some])[:, :, s, :],
                                                     split(Ex[:, (i - 1) % 4, some])[:, :, s, :], ALU.mult)
                            x.then_inc(S("qk_ready", l), 1)
                    edge = P - 1 if d == 0 else 0

                    def decay_keys(h):
                        dve.wait_ge(*at("kd_decay", l, d * HEADS + h + 1))
                        vv.tensor_tensor(K[:, h, :], QKd[:, h % 2, :], K[:, h, :], ALU.mult).then_inc(S("kd_ready", l), 1)

                    for h in range(HEADS):
                        b = F[d][:, h, :].rearrange("p (c t) -> p c t", t=P)
                        if h >= 2:
                            dve.wait_ge(*at("kd_ready", l, d * HEADS + h - 1))
                        vv.tensor_tensor(QKd[:, h % 2, :].rearrange("p (c t) -> p c t", t=P), b,
                                         b[:, :, edge:edge + 1].to_broadcast([P, TILES, P]), ALU.subtract) \
                          .then_inc(S("kd_exponent", l), 1)
                        if h >= 1:
                            decay_keys(h - 1)
                    decay_keys(HEADS - 1)
                    dve.wait_ge(*at("e_b", l, 2 * d + 2))
                    vv.tensor_tensor(Ex[:, :, some], Ex[:, :, some], q[:, :, some], ALU.mult).then_inc(S("qe_ready", l), 1)
                    for i, c in enumerate(ORDER[d]):
                        if c in tiles:
                            s = slice(c * P, (c + 1) * P)
                            o = read(dve, ("out", l, d, i)).rearrange("p (h t) -> p h t", h=HEADS)
                            if d == 0:
                                vv.tensor_copy(O[:, :, s], o).then_inc(S("o_acc", l), 1)
                            else:
                                vv.tensor_tensor(O[:, :, s], o, O[:, :, s], ALU.add).then_inc(S("o_acc", l), 1)
                        if i < 3:
                            o = read(dve, ("st", l, d, i))
                            if i:
                                dve.wait_ge(*at("state", l, (d * 3 + i) * HEADS))
                            for h in range(HEADS):
                                ps = o[:, h * P:(h + 1) * P]
                                if i == 0:
                                    x = vv.tensor_copy(state[:, h, :], ps)
                                else:
                                    x = vv.scalar_tensor_tensor(out=state[:, h, :], in0=state[:, h, :], scalar=ebl[:, h, c:c + 1],
                                                                in1=ps, op0=ALU.mult, op1=ALU.add)
                                x.then_inc(S("state", l), 1)
                for h in range(HEADS):
                    dve.wait_ge(*at("o_rs", l, 2 * h + 2))
                    link(vv.tensor_tensor(O[:, h, some], O[:, h, some], Ex[:, h, some], ALU.mult))
                    vv.scalar_tensor_tensor(out=O[:, h, some], in0=O[:, h, some], scalar=vec("hg_norm_g")[:, l * HEADS + h:l * HEADS + h + 1],
                                            in1=G[:, h, some], op0=ALU.mult, op1=ALU.mult).then_inc(S("a_ready", l), 1)
                dve.wait_ge(*at("mla_rs", l, 2))
                for k in range(3):
                    vv.scalar_tensor_tensor(out=dq[:, k, some], in0=dq[:, k, some], scalar=vec("q_norm_g")[:, l * 3 + k:l * 3 + k + 1],
                                            in1=RS[:, some], op0=ALU.mult, op1=ALU.mult).then_inc(S("dq_n", l), 1)
                dve.wait_ge(*at("mla_rs", l, 4))
                for k in range(2):
                    vv.scalar_tensor_tensor(out=ckv[:, k, :], in0=ckv[:, k, :], scalar=vec("kv_norm_g")[:, l * 2 + k:l * 2 + k + 1],
                                            in1=RS[:, :], op0=ALU.mult, op1=ALU.mult).then_inc(S("ckv_n", l), 1)
                for h in range(MH):
                    o = read(dve, ("Q", l, h))
                    vv.tensor_tensor(QT[0:QK, h, some], o[0:QK, some], rope[0:QK, 0, some], ALU.mult).then_inc(S("q_rot", l), 1)
                    o = read(dve, ("Qsw", l, h))
                    vv.tensor_tensor(tmpQ[0:QK, h % 2, some], o[0:QK, some], rope[0:QK, 1, some], ALU.mult).then_inc(S("q_rot", l), 1)
                    dve.wait_ge(*at("q_rot", l, 2 * h + 2))
                    vv.tensor_tensor(QT[0:QK, h, some], QT[0:QK, h, some], tmpQ[0:QK, h % 2, some], ALU.add).then_inc(S("q_rope", l), 1)
                for t in range(TILES):
                    o = read(dve, ("V", l, t))
                    vv.tensor_copy(V2[:, t, :], o).then_inc(S("v2_ready", l), 1)
                steps = attention_steps(l)
                for j in range(len(steps) + 2):
                    if j < len(steps):
                        keys = NCTX if steps[j][0] < 2 else T
                        o = read(dve, ("sc", l, j))
                        link(vv.reduce_max(mx[:, 0, j:j + 1], o[:, 0:keys], AX_X))
                        vv.tensor_scalar(mx[:, 1, j:j + 1], mx[:, 0, j:j + 1], -SCALE, None, ALU.mult).then_inc(S("neg_max", l), 1)
                    if 1 <= j <= len(steps):
                        i = j - 1
                        keys = NCTX if steps[i][0] < 2 else T
                        dve.wait_ge(*at("p_exp", l, i + 1))
                        link(vv.reciprocal(mx[:, 3, i:i + 1], mx[:, 2, i:i + 1]))
                        vv.tensor_scalar(PR[:, i % 2, 0:keys], PR[:, i % 2, 0:keys], mx[:, 3, i:i + 1], None, ALU.mult) \
                          .then_inc(S("p_norm", l), 1)
                    if j >= 2:
                        qt, h = steps[j - 2]
                        rows = slice(h % 2 * MV, (h % 2 + 1) * MV)
                        o = read(dve, ("pv", l, j - 2))
                        vv.tensor_copy(MT[rows, h // 2, qt * P:(qt + 1) * P], o[rows, 0:P]).then_inc(S("m_ready", l), 1)
                for m in range(KD):
                    for i, (g, w, sem) in enumerate((("ga", "pa", "mix_a"), ("gb", "pb", "mix_b"))):
                        t_ = mixT[:, m % 2 * 2 + i, some]
                        dve.wait_ge(*at("mix_exp", l, 2 * m + i + 1))
                        link(vv.tensor_scalar(t_, t_, 1.0, None, ALU.add))
                        link(vv.reciprocal(t_, t_))
                        o = read(dve, (w, l, m))
                        vv.tensor_tensor(t_, o[:, some], t_, ALU.mult).then_inc(S(sem, l), 1)
                    dve.wait_ge(*at("mix_a", l, m + 1))
                    dve.wait_ge(*at("mix_b", l, m + 1))
                    vv.tensor_tensor(mix[:, m, some], mixT[:, m % 2 * 2, some], mixT[:, m % 2 * 2 + 1, some], ALU.add) \
                      .then_inc(S("mixed", l), 1)
                for m in range(KD):
                    o = read(dve, ("y", l, m))
                    for v in halves:
                        s = slice(v * NCTX, (v + 1) * NCTX)
                        x = vv.scalar_tensor_tensor(out=Z[:, m, s], in0=o[:, s], scalar=modT[:, l, 16 + m, v:v + 1], in1=Z[:, m, s],
                                                    op0=ALU.mult, op1=ALU.add)
                    x.then_inc(S("z_mixed", l), 1)
                dve.wait_ge(*at("z_mixed", l, KD))
                dve.wait_ge(*at("rs2", l, 2))
                for k in range(KD):
                    vv.tensor_tensor(H[:, k, some], Z[:, k, some], RS[:, some], ALU.mult).then_inc(S("h2_n", l), 1)

                dve.wait_ge(*at("score_exp", l, 1))
                R = lambda i: rt[:, i, 0:n, :]
                G4 = lambda i: R(i).rearrange("p t (g e) -> p t g e", g=NG)
                link(vv.tensor_scalar(R(1), R(1), 1.0, None, ALU.add))
                link(vv.reciprocal(R(1), R(1)))
                link(vv.tensor_tensor(R(2), R(1), rb[:, :].unsqueeze(1).to_broadcast([P, n, NE]), ALU.add))
                pairs = [(i, j) for i in range(4) for j in range(i + 1, 4)]
                gs = rt[:, 3, 0:n, 0:NG]
                ps = rt[:, 4, 0:n, 0:NG]
                for x, (i, j) in enumerate(pairs):
                    link(vv.tensor_tensor(ps if x else gs, G4(2)[:, :, :, i], G4(2)[:, :, :, j], ALU.add))
                    if x:
                        link(vv.tensor_tensor(gs, gs, ps, ALU.max))
                link(vv.memset(R(5), 0.0))
                link(vv.memset(rt[:, 6, 0:n, :], 0.0))
                ge, lt = rt[:, 7, 0:n, 0:NG], rt[:, 8, 0:n, 0:NG]
                ahead = G4(5)
                for i, j in pairs:
                    link(vv.tensor_tensor(ge, G4(2)[:, :, :, i], G4(2)[:, :, :, j], ALU.is_ge))
                    link(vv.tensor_scalar(lt, ge, -1.0, 1.0, ALU.mult, ALU.add))
                    vv.tensor_tensor(ahead[:, :, :, j], ahead[:, :, :, j], ge, ALU.add)
                    link(vv.tensor_tensor(ahead[:, :, :, i], ahead[:, :, :, i], lt, ALU.add))
                    g1, g2 = ge[:, :, 0:1], lt[:, :, 0:1]
                    link(vv.tensor_tensor(g1, gs[:, :, i:i + 1], gs[:, :, j:j + 1], ALU.is_ge))
                    link(vv.tensor_scalar(g2, g1, -1.0, 1.0, ALU.mult, ALU.add))
                    gr = rt[:, 6, 0:n, 0:NG]
                    vv.tensor_tensor(gr[:, :, j:j + 1], gr[:, :, j:j + 1], g1, ALU.add)
                    link(vv.tensor_tensor(gr[:, :, i:i + 1], gr[:, :, i:i + 1], g2, ALU.add))
                link(vv.tensor_scalar(rt[:, 6, 0:n, 0:NG], rt[:, 6, 0:n, 0:NG], 0.5, None, ALU.is_lt))
                link(vv.tensor_scalar(R(5), R(5), 1.5, None, ALU.is_lt))
                vv.tensor_tensor(G4(0), G4(5), rt[:, 6, 0:n, 0:NG].unsqueeze(3).to_broadcast([P, n, NG, EG]), ALU.mult) \
                  .then_inc(S("taken", l), 1)
                dve.wait_ge(*at("taken", l, 1))
                link(vv.tensor_tensor(R(9), R(1), R(0), ALU.mult))
                wsum = rt[:, 10, 0:n, 0]
                link(vv.tensor_reduce(wsum, R(9), AX_X, ALU.add))
                link(vv.reciprocal(wsum, wsum))
                link(vv.tensor_tensor(gw[:, 0:n, 0:NE], R(9), wsum.unsqueeze(2).to_broadcast([P, n, NE]), ALU.mult))
                link(vv.tensor_copy(gw[:, 0:n, NE:NE + 1], gw[:, 0:n, 0:1]))
                o = read(dve, ("rank", l))
                link(vv.scalar_tensor_tensor(out=pos[:, 0:n, 0:NE], in0=o[:, 0:n * NE].rearrange("p (t e) -> p t e", e=NE), scalar=FAR,
                                             in1=R(0), op0=ALU.add, op1=ALU.mult))
                link(vv.tensor_scalar(pos[:, 0:n, 0:NE], pos[:, 0:n, 0:NE], -FAR, None, ALU.add))
                link(vv.tensor_scalar(pos[:, 0:n, NE:NE + 1], pos[:, 0:n, 0:1], -float(CAP), None, ALU.add))
                link(vv.reduce_max(cnt[:, 0:1], o[:, n * NE:(n + 1) * NE], AX_X))
                for i in range(1, 4):
                    link(vv.tensor_scalar(cnt[:, i:i + 1], cnt[:, 0:1], float(CAP * i), None, ALU.is_gt))
                link(vv.tensor_tensor(cnt[:, 1:2], cnt[:, 1:2], cnt[:, 2:3], ALU.add))
                link(vv.scalar_tensor_tensor(out=cnt[:, 4:5], in0=cnt[:, 1:2], scalar=1.0, in1=cnt[:, 3:4], op0=ALU.add, op1=ALU.add))
                vv.tensor_copy(nbi[:, :], cnt[:, 4:5]).then_inc(S("nb_ready", l), 1)
                dve.wait_ge(*at("nb_ready", l, 1))
                nb = dve.value_load(nbi[0:1, 0:1], min_val=1, max_val=4)

                def select(col):
                    for j in range(n):
                        x = vv.tensor_scalar(sel[:, j, :], slot_no[:, :], pos[:, j, col], None, ALU.is_equal)
                    x.then_inc(S("sel", l), 1)

                def select_weighted(col):
                    for j in range(n):
                        x = vv.tensor_scalar(selw[:, j, :], slot_no[:, :], pos[:, j, col], gw[:, j, col],
                                             ALU.is_equal, ALU.mult)
                    x.then_inc(S("selw", l), 1)

                select(slice(0, 1))
                select_weighted(slice(0, 1))
                with dve.Fori(0, nb) as r:
                    with dve.Fori(0, NE) as e:
                        it = r * NE + e
                        dve.wait_ge(*at("gate_exp", l, it + 1))
                        vv.tensor_scalar(gate_t, gate_t, 1.0, None, ALU.add).then_inc(S("silu", l), 1)
                        dve.wait_ge(*at("silu", l, it * 3 + 1))
                        vv.reciprocal(gate_t, gate_t).then_inc(S("silu", l), 1)
                        dve.wait_ge(*at("silu", l, it * 3 + 2))
                        vv.tensor_tensor(gate_t, banks[:, 3, :], gate_t, ALU.mult).then_inc(S("silu", l), 1)
                        dve.wait_ge(*at("silu", l, it * 3 + 3))
                        dve.wait_ge(*at("up_used", l, it + 2))
                        vv.tensor_tensor(hidden, banks[:, 4, :], gate_t, ALU.mult).then_inc(S("hidden", l), 1)
                        select(bass.ds(e + 1, 1))
                        dve.wait_ge(*at("selT_full", l, it + 1))
                        select_weighted(bass.ds(e + 1, 1))
                        for k in range(KD):
                            dve.wait_ge(*at("combined", l, it * KD + k + 1))
                            for v in halves:
                                s = slice(v * NCTX, (v + 1) * NCTX)
                                c0 = v * NCTX - first_token(l)
                                x = vv.scalar_tensor_tensor(out=Z[:, k, s], in0=banks[:, 5 + k % 2, c0:c0 + NCTX],
                                                            scalar=modT[:, l, 40 + k, v:v + 1], in1=Z[:, k, s],
                                                            op0=ALU.mult, op1=ALU.add)
                            x.then_inc(S("z_added", l), 1)
                    vv.tensor_scalar(pos[:, 0:n, :], pos[:, 0:n, :], -float(CAP), None, ALU.add).then_inc(S("round", l), 1)
                    dve.wait_ge(*at("round", l, r + 1))
                vv.tensor_copy(small[:, 6, 0:1], small[:, 4, 0:1]).then_inc(S("z_ready", l), 1)

            dve.wait_ge(*at("rsf", "g", 2))
            for k in range(KD):
                vv.scalar_tensor_tensor(out=Z[:, k, NCTX:T], in0=Z[:, k, NCTX:T], scalar=vec("final_g")[:, k:k + 1],
                                        in1=RS[:, NCTX:T], op0=ALU.mult, op1=ALU.mult).then_inc(S("zf"), 1)


def shape_constants():
    p = np.arange(P)
    s, t = p[:, None], p[None, :]
    masks = np.zeros((P, 2, 8, P), np.int32)
    for i, m in enumerate(LEVELS):
        same = s // (2 * m) == t // (2 * m)
        masks[:, 0, i] = same & (s % (2 * m) < m) & (t % (2 * m) >= m)
        masks[:, 1, i] = same & (s % (2 * m) >= m) & (t % (2 * m) < m)
    masks[:, :, 7] = (s == t)[:, None, :]
    rope = np.zeros((P, 2, T), np.float32)
    rope[:, 0] = 1.0
    axis = ROPE // 2
    inv = np.float32(10000.0) ** (-np.arange(0, axis, 2, dtype=np.float32) / np.float32(axis))
    tok = np.arange(NX)
    for ax, at in enumerate((tok // 64, tok % 64)):
        ang = (at.astype(np.float32)[None, :] * inv[:, None]).astype(np.float32)
        for half in range(2):
            r = NOPE + ax * axis + half * 8
            rope[r:r + 8, 0, NCTX:] = np.cos(ang)
            rope[r:r + 8, 1, NCTX:] = np.sin(ang)
    return {
        "k_ident": np.eye(P, dtype=np.float32), "k_ones": np.ones((P, P), np.float32),
        "k_before": (s < t).astype(np.float32), "k_slot": np.broadcast_to(p.astype(np.float32), (P, P)).copy(),
        "k_masks": masks.reshape(P, -1), "k_rope": rope,
    }


_INS = ['x', 'c', 'ctx', 'c_ctx', 'w_mod', 'b_mod', 'norm1_g', 'norm2_g', 'w_in', 'gamma_fwd', 'gamma_bwd', 'hg_norm_g',
        'q_norm_g', 'kv_norm_g', 'w_uq', 'w_ukv', 'w_pa', 'w_pb', 'w_o', 'w_router', 'router_bias',
        'w_gate_e', 'w_up_e', 'w_down_e', 'final_g']


def kernel(**inputs):
    import concourse.bacc as _bacc
    from concourse.bass_utils import run_bass_kernel_spmd as _run

    nc = _bacc.Bacc("TRN2", target_bir_lowering=False, num_devices=1)
    arrays, args = {}, {}
    given = {name: np.ascontiguousarray(inputs[name]) for name in _INS}
    for name, value in {**given, **shape_constants()}.items():
        arrays[f"in_{name}"] = value
        args[name] = nc.dram_tensor(f"in_{name}", value.shape, mybir.dt.from_np(value.dtype), kind="ExternalInput").ap()
    out = nc.dram_tensor("out_0", (1, NX, D), F32, kind="ExternalOutput").ap()
    bass_hybrid_transformer(nc, args, out)
    r = _run(nc, [arrays], core_ids=[0])
    return r.results[0]["out_0"]
```

```python
from contextlib import ExitStack

import numpy as np

import concourse.bass as bass
from concourse import mybir

ALU = mybir.AluOpType
ACT = mybir.ActivationFunctionType
F32 = mybir.dt.float32
F32R = mybir.dt.float32r
I32 = mybir.dt.int32
U8 = mybir.dt.uint8
AX_X = mybir.AxisListType.X

P = 128
D = 1024
KD = D // P
NCTX, NX = 256, 256
T = NCTX + NX
TILES = T // P
DEPTH = 2
EPS = 1e-6
HEADS = 4
MH, NOPE, ROPE, MV = 8, 64, 32, 64
QK = NOPE + ROPE
QR, KVR = 384, 256
SCALE = QK ** -0.5
NE, NG, EG = 16, 4, 4
DE = 512
COMBINE = (6, 7, 0, 1)
CHUNKS = 4
CAP = P
MOD = 6 * D
CH = 512
OFF = dict(q=0, i=512, ff=1024, fb=1536, g=2048, dq=2560, dkv=2944, ga=3232, gb=4256)
LEVELS = (64, 32, 16, 8, 4, 2, 1)
STEPS = [(m, h) for m in LEVELS for h in range(HEADS)]
ORDER = ((0, 1, 2, 3), (1, 0, 3, 2))
MODS = [(l, j) for l in range(DEPTH) for j in range(12)]
MODS_EARLY = MODS[:4]
MODS_IN = (MODS[4:16], MODS[16:])
ROWS_BANKS, TURNED_BANK = (6, 7), 5
FAR = 10000.0

SHARED = {
    "sq1": ("squared", 0), "o_sq": ("squared", 8), "dq_sq": ("squared", 12), "ckv_sq": ("squared", 15), "sq2": ("squared", 17),
    "sq1_used": ("square_used", 0), "dq_sq_used": ("square_used", 7), "ckv_sq_used": ("square_used", 9),
    "sq2_used": ("square_used", 10),
    "rs1": ("rsqrt", 0), "o_rs": ("rsqrt", 2), "mla_rs": ("rsqrt", 10), "rs2": ("rsqrt", 14),
    "h1": ("modulated", 0), "h2": ("modulated", 16), "h1_n": ("normed", 0), "h2_n": ("normed", 8),
    "dq_raw": ("low_rank", 0), "ckv_raw": ("low_rank", 3), "dq_n": ("low_rank_normed", 0), "ckv_n": ("low_rank_normed", 3),
}
IN_LAYER_0 = dict(
    squared=25, square_used=17, rsqrt=16, modulated=32, normed=16, low_rank=5, low_rank_normed=5,
    f_sig=8, v_ready=4, q_ready=4, g_sig=4, g_ready=4,
    kpe_mul=2, kpe_ready=1, kpe_sw=1, uq_sw=3, kpe_in=8, k_gate=8, att_zero=2, logf=8, b_ready=8, att_in=64, exponent=56,
    decay=56, qk_ready=56, e_b=4, kd_exponent=8, kd_decay=8, kd_ready=8, qe_ready=2, kdT_ready=6, state=24, o_acc=8,
    a_ready=4, q_rot=16, q_rope=8, k_ready=8, v2_ready=4, neg_max=32, p_exp=32, p_norm=32, pT_ready=32, m_ready=32,
    mix_sig=16, mix_a=8, mix_b=8, mixed=8, z_mixed=8, score=1, scored=1, htok=8, htok_lo=8, taken=1, nb_ready=1, z_ready=1)

VEC = {}
for _name, _rows in (("c", 8), ("c_ctx", 8), ("norm1_g", 16), ("norm2_g", 16), ("final_g", 8), ("hg_norm_g", 8),
                     ("q_norm_g", 6), ("kv_norm_g", 4), ("gamma_fwd", 8), ("gamma_bwd", 8)):
    VEC[_name] = (sum(r for _, r in VEC.values()), _rows)
NVEC = sum(r for _, r in VEC.values())
NBMOD = DEPTH * MOD // P


def first_token(l):
    return NCTX if l == DEPTH - 1 else 0


def attention_steps(l):
    return [(qt, h) for qt in range(first_token(l) // P, TILES) for h in range(MH)]


def psum_plan():
    fixed, reserved = {}, []
    turns = [(("vec", 0), "g", "vec_read", 1), (("vec", 1), "g", "vec_read", 2)]
    turns += [(("z", k), "g", "z_loaded", k + 1) for k in range(KD)]

    def mods(some):
        for unit in some:
            m = MODS.index(unit)
            fixed[("mod", *unit)], fixed[("modT", *unit)] = ROWS_BANKS[m % 2], TURNED_BANK
            turns.extend([(("mod", *unit), "g", "mod_rows", m + 1), (("modT", *unit), "g", "mod_added", m + 1)])

    mods(MODS_EARLY)
    for l in range(DEPTH):
        tiles = range(first_token(l) // P, TILES)
        turns += [(("ssq1", l), l, "rs1", 1)]
        turns += [(("f", l, d, h), l, "f_sig", d * HEADS + h + 1) for d in range(2) for h in range(HEADS)]
        turns += [(("v", l, t), l, "v_ready", t + 1) for t in range(TILES)]
        turns += [(("q", l, h), l, "q_ready", h + 1) for h in range(HEADS)]
        turns += [(("g", l, h), l, "g_ready", h + 1) for h in range(HEADS)]
        turns += [(("dq", l, k), l, "dq_raw", k + 1) for k in range(QR // P)]
        turns += [(("ckv", l, k), l, "ckv_raw", k + 1) for k in range(KVR // P)]
        turns += [(("kpe", l, s), l, "kpe_mul", s + 1) for s in range(2)]
        mods(MODS_IN[l])
        start = len(turns)
        for d in range(2):
            turns += [(("diag", l, d, h), l, "att_in", d * 32 + h + 1) for h in range(HEADS)]
            turns += [(("lev", l, d, n), l, "att_in", d * 32 + HEADS + n + 1) for n in range(len(STEPS))]
            outs = 0
            for i, c in enumerate(ORDER[d]):
                if i < 3:
                    turns += [(("kdT", l, d, i), l, "kdT_ready", d * 3 + i + 1),
                              (("st", l, d, i), l, "state", (d * 3 + i + 1) * HEADS)]
                if c in tiles:
                    outs += 1
                    turns += [(("out", l, d, i), l, "o_acc", d * len(tiles) + outs)]
        reserved.append(range(start, len(turns)))
        turns += [(("ossq", l, h), l, "o_rs", 2 * h + 1) for h in range(HEADS)]
        turns += [(("qssq", l), l, "mla_rs", 1), (("kssq", l), l, "mla_rs", 3)]
        for h in range(MH):
            turns += [(("Q", l, h), l, "q_rot", 2 * h + 1), (("Qsw", l, h), l, "q_rot", 2 * h + 2)]
        turns += [(("K", l, h), l, "k_ready", h + 1) for h in range(MH)]
        turns += [(("V", l, t), l, "v2_ready", t + 1) for t in range(TILES)]
        nj = len(attention_steps(l))
        for j in range(nj + 2):
            if j < nj:
                turns += [(("sc", l, j), l, "p_exp", j + 1)]
            if 1 <= j <= nj:
                turns += [(("pT", l, j - 1), l, "pT_ready", j)]
            if j >= 2:
                turns += [(("pv", l, j - 2), l, "m_ready", j - 1)]
        for m in range(KD):
            turns += [(("pa", l, m), l, "mix_a", m + 1), (("ga", l, m), l, "mix_sig", 2 * m + 1),
                      (("pb", l, m), l, "mix_b", m + 1), (("gb", l, m), l, "mix_sig", 2 * m + 2)]
        turns += [(("y", l, m), l, "z_mixed", m + 1) for m in range(KD)]
        turns += [(("ssq2", l), l, "rs2", 1)]
        turns += [(("logit", l), l, "score", 1)]
        turned = [(("hT", l, t, g), l, "htok_lo", (t - tiles[0]) * 2 + g + 1) for t in tiles for g in range(2)]
        turns += [turned[0], (("logitT", l), l, "scored", 1), *turned[1:]]
        turns += [(("rank", l), l, "nb_ready", 1)]
    turns += [(("ssqf",), "g", "rsf", 1)]
    turns += [(("fin", t, g), "g", "fin_rows", t * 2 + g + 1) for t in range(NX // P) for g in range(2)]
    bank, nth, before, last = {}, {}, {}, {}
    history = [[] for _ in range(8)]
    b = 0
    for n, (turn, *freed) in enumerate(turns):
        if turn in fixed:
            taken = fixed[turn]
        else:
            if any(n in part for part in reserved) and b >= TURNED_BANK:
                b = 0
            taken, b = b, (b + 1) % 8
        bank[turn], nth[turn] = taken, len(history[taken]) + 1
        before[turn] = history[taken][-1] if history[taken] else None
        history[taken].append(tuple(freed))
        if turn[0] == "rank":
            last[turn[1]] = [h[-1] for h in history]
    return bank, nth, before, last


PLACES = []
for _d in range(2):
    PLACES += [(("diag", _d, h), 1) for h in range(HEADS)] + [(("lev", _d, n), 1) for n in range(len(STEPS))]
    PLACES += [(("keys", _d), 8)] + [(("chunk", _d, i), 2) for i in range(3)]
TURN_PART = 4


def mod_parts(l, place):
    total, done = len(MODS_IN[l]) * KD, 0
    for name, n in PLACES:
        if name == place:
            return min(done, total), min(done + n, total)
        done += n
    return min(done, total), total


def mod_copied(l, place):
    return mod_parts(l, place)[1] // KD


def mod_turned(l, place):
    if place == "end":
        return len(MODS_IN[l])
    return max(0, (mod_parts(l, place)[1] - 1 - TURN_PART) // KD)


def weight_plan(a):
    units = []

    def rows(w):
        return w.rearrange("(k p) n -> p k n", p=P)

    def mods(some, s):
        return [(("mod", l, j), (s + i) % 4, rows(a["w_mod"][l, :, j * CH:(j + 1) * CH]), ("mod", l, j))
                for i, (l, j) in enumerate(some)]

    units += mods(MODS_EARLY, 0)
    for l in range(DEPTH):
        def w_in(name, width, shift=0):
            o = OFF[name] + shift
            return rows(a["w_in"][l, :, o:o + width])
        units += [
            (("ff", l), 0, w_in("ff", CH), ("f", l, 0, 3)), (("fb", l), 1, w_in("fb", CH), ("f", l, 1, 3)),
            (("i", l), 2, w_in("i", CH), ("v", l, 3)), (("q", l), 3, w_in("q", CH), ("q", l, 3)),
            (("g", l), 0, w_in("g", CH), ("g", l, 3)), (("dq", l), 1, w_in("dq", QR), ("dq", l, 2)),
            (("dkv", l), 2, w_in("dkv", KVR + ROPE), ("kpe", l, 1)), *mods(MODS_IN[l], 3),
            (("uq", l), 3, rows(a["w_uq"][l]), ("Qsw", l, 7)), (("ukv", l), 0, rows(a["w_ukv"][l]), ("V", l, 3)),
            (("pa", l), 1, rows(a["w_pa"][l]), ("pa", l, 7)), (("pb", l), 2, rows(a["w_pb"][l]), ("pb", l, 7)),
            (("ga0", l), 3, w_in("ga", CH), ("ga", l, 3)), (("gb0", l), 0, w_in("gb", CH), ("gb", l, 3)),
            (("ga1", l), 3, w_in("ga", CH, CH), ("ga", l, 7)), (("gb1", l), 0, w_in("gb", CH, CH), ("gb", l, 7)),
            (("o0", l), 1, rows(a["w_o"][l, :, 0:CH]), ("y", l, 3)), (("o1", l), 2, rows(a["w_o"][l, :, CH:D]), ("y", l, 7)),
        ]
    slot, landed, count = {}, {}, [0] * 4
    for unit, s, _, _ in units:
        count[s] += 1
        slot[unit], landed[unit] = s, 16 * count[s]
    return units, slot, landed


def bass_hybrid_transformer(nc, a, out):
    bank, nth, before, last_turns = psum_plan()
    units, slot_of, landed_at = weight_plan(a)

    with ExitStack() as ctx:
        def sb(name, shape, dt=F32):
            return ctx.enter_context(nc.sbuf_tensor(name, shape, dt))

        def twice(name, shape):
            with nc.sbuf_tensor(name, shape, F32) as plain:
                pass
            return plain, sb(f"{name}_r", shape, F32R)

        sems = {}

        def S(name, l="g"):
            name = SHARED.get(name, (name, 0))[0]
            if name in IN_LAYER_0 and l != "g":
                l = "layers"
            if (name, l) not in sems:
                sems[name, l] = ctx.enter_context(nc.semaphore(f"{name}_{l}"))
            return sems[name, l]

        def at(name, l, value):
            shared, first = SHARED.get(name, (name, 0))
            return S(name, l), value + first + (IN_LAYER_0[shared] if shared in IN_LAYER_0 and l in range(1, DEPTH) else 0)

        banks = ctx.enter_context(nc.psum_tensor("banks", [P, 8, 512], F32))
        bank_full = [ctx.enter_context(nc.semaphore(f"bank_full{b}")) for b in range(8)]
        slot_landed = [ctx.enter_context(nc.semaphore(f"slot_landed{s}")) for s in range(4)]

        ident = sb("ident_sb", [P, P])
        ones = sb("ones_sb", [P, P])
        before_m = sb("before_sb", [P, P])
        slot_no = sb("slot_no_sb", [P, P])
        masks = sb("masks_sb", [P, 2, 8, P], U8)
        rope = sb("rope_sb", [P, 2, T])
        vrows = sb("vrows", [P, 2, P])
        vecs = sb("vecs", [P, NVEC])
        bmod = sb("bmod", [P, NBMOD])
        eps = sb("eps", [P, 1])
        rbias = sb("rbias", [1, NE])
        rb = sb("rb", [P, NE])
        wr = sb("wr", [P, KD, NE])
        pair = sb("pair", [P, 3, EG, EG])
        modT = sb("modT", [P, DEPTH, 48, 2])
        gainA = sb("gainA", [P, DEPTH, 2, KD, 2])
        lb = sb("lb", [P, 2, DEPTH, HEADS])
        oml = sb("oml", [P, 2, DEPTH, HEADS])
        small = sb("small", [P, 8, 16])
        silu_c = sb("silu_c", [P, 16])

        Z = sb("Z", [P, KD, T])
        H, H_r = twice("H", [P, KD, T])
        W, W_r = twice("W", [P, 4, KD * CH])
        VG, VG_r = twice("VG", [P, 8 * T])
        V = VG[:, 0:4 * T].rearrange("p (t c) -> p t c", t=TILES)
        G = VG[:, 4 * T:].rearrange("p (h t) -> p h t", h=HEADS)
        OL, OL_r = twice("OL", [P, 10 * T])
        O = OL[:, 0:4 * T].rearrange("p (h t) -> p h t", h=HEADS)
        dq = OL[:, 4 * T:7 * T].rearrange("p (k t) -> p k t", k=3)
        ckv = OL[:, 7 * T:9 * T].rearrange("p (k t) -> p k t", k=2)
        kpe = OL[:, 9 * T:]
        RS = sb("RS", [P, T])
        SQ = sb("SQ", [P, 2, T])
        kdT = SQ[:, 0, :].rearrange("p (h t) -> p h t", h=HEADS)
        state = SQ[:, 1, :].rearrange("p (h t) -> p h t", h=HEADS)
        mx = sb("mx", [P, 4, 32])
        ebl = sb("ebl", [P, HEADS, TILES])
        uq_pad = sb("uq_pad", [P, NOPE + 3 * MH * ROPE])
        kpe_pad = sb("kpe_pad", [P, NOPE + KD * ROPE])
        uq_sw = uq_pad[:, NOPE:].rearrange("p (k h c) -> p k h c", k=3, h=MH)
        kpe_sw = kpe_pad[:, NOPE:].rearrange("p (k c) -> p k c", k=KD)
        arena, arena_r = twice("arena", [P, 6 * 2048 + 1024])

        def part(first, n, shape, **sizes):
            return arena[:, first * 2048:first * 2048 + n].rearrange(shape, **sizes)

        q = part(0, 2048, "p (h t) -> p h t", h=HEADS)
        F = [part(1 + d, 2048, "p (h t) -> p h t", h=HEADS) for d in range(2)]
        K = part(3, 2048, "p (h t) -> p h t", h=HEADS)
        Ex = part(4, 2048, "p (h t) -> p h t", h=HEADS)
        att = part(5, 2048, "p (h t) -> p h t", h=HEADS)
        QKd = part(6, 1024, "p (h t) -> p h t", h=2)
        QT = part(0, 4096, "p (h t) -> p h t", h=MH)
        KT = part(2, 4096, "p (h t) -> p h t", h=MH)
        V2 = part(4, 2048, "p (t c) -> p t c", t=TILES)
        PR = part(5, 1024, "p (r t) -> p r t", r=2)
        PT = arena[:, 5 * 2048 + 1024:6 * 2048].rearrange("p (r t) -> p r t", r=2)
        tmpQ = SQ
        MT = V
        mix = part(0, 4096, "p (k t) -> p k t", k=KD)
        mixT = part(4, 2048, "p (r t) -> p r t", r=4)
        def piece(first, n):
            return arena[:, first:first + n]

        def piece_r(first, n):
            return arena_r[:, first:first + n]

        htok_hi = piece_r(4096, TILES * D).rearrange("p (t n) -> p t n", t=TILES)
        htok_lo = OL_r[:, 0:TILES * D].rearrange("p (t n) -> p t n", t=TILES)
        sel = piece_r(0, 512).rearrange("p (t s) -> p t s", t=TILES)
        selw = piece(512, 512).rearrange("p (t s) -> p t s", t=TILES)
        selT = piece_r(1024, 512)
        selw_copy = piece(1536, 512)
        gate_t = piece(2048, 512)
        hidden = piece(2560, 512)
        hidT_hi, hidT_lo = piece_r(3072, 512), piece_r(3584, 512)
        xs_tok = piece(8192, D)
        xsT_hi, xsT_lo = (piece_r(i, D).rearrange("p (k s) -> p k s", k=KD) for i in (9216, 10240))
        yd_hi, yd_lo = piece_r(11264, D), piece_r(12288, D)
        scoreT = piece(12288, 512)
        compared = piece(8192, 3 * 512).rearrange("p (a n) -> p a n", a=3)
        rt = piece(11264, 1024).rearrange("p (a t e) -> p a t e", a=16, t=TILES)
        ROUNDS = TILES
        pos, gw = (RS[:, i * 256:(i + 1) * 256].rearrange("p (t e) -> p t e", t=TILES) for i in range(2))
        wslot = sb("wslot", [P, 1])
        w_hi = {"gate": H_r[:, :, :].rearrange("p k t -> p (k t)"), "up": W_r[:, 3, :], "down": VG_r[:, :]}
        mod_row = RS
        masks_in = O[:, :, :].rearrange("p h t -> p (h t)").bitcast(I32)
        ztok = H[:, :, :].rearrange("p k t -> p (k t)").rearrange("p (t n) -> p t n", t=TILES)
        nbi = sb("nbi", [P, 1], I32)
        cnt = sb("cnt", [P, 8])

        def slot(unit, cols):
            return W[:, slot_of[unit], 0:KD * CH // cols * cols].rearrange("p (k n) -> p k n", n=cols)

        def read(eng, turn):
            eng.wait_ge(bank_full[bank[turn]], nth[turn])
            return banks[:, bank[turn], :]

        def vec(name):
            first, n = VEC[name]
            return vecs[:, first:first + n]

        def Nx(l):
            return slice(first_token(l), T)

        block = ctx.enter_context(nc.Block())

        @block.sync
        def _(sp):
            for t in range(2):
                sp.dma_start(ztok[:, t, :], a["ctx"][0, t * P:(t + 1) * P, :]).then_inc(S("x_in"), 16)
                sp.dma_start(ztok[:, 2 + t, :], a["x"][0, t * P:(t + 1) * P, :]).then_inc(S("x_in"), 16)
            for dst, src in ((ident, "k_ident"), (ones, "k_ones"), (before_m, "k_before"), (slot_no, "k_slot"),
                             (masks_in, "k_masks"), (rope, "k_rope"),
                             (pair, "k_pair")):
                sp.dma_start(dst[tuple(slice(None) for _ in dst.shape)], a[src]).then_inc(S("consts"), 16)
            for name, (first, n) in VEC.items():
                src = a[name]
                if len(src.shape) == 2:
                    src = src.rearrange("a n -> (a n)")
                sp.dma_start(vrows[first:first + n, 0, :], src.rearrange("(r p) -> r p", p=P)).then_inc(S("consts"), 16)
            sp.dma_start(vrows[0:NBMOD, 1, :], a["b_mod"].rearrange("l (r p) -> (l r) p", p=P)).then_inc(S("consts"), 16)
            sp.dma_start(rbias[:], a["router_bias"].rearrange("(o n) -> o n", o=1)).then_inc(S("consts"), 16)
            sp.dma_start(wr[:], a["w_router"].rearrange("(k p) n -> p k n", p=P)).then_inc(S("consts"), 16)

            previous = [None] * 4

            def load(n):
                unit, s, src, last = units[n]
                if previous[s]:
                    sp.wait_ge(bank_full[bank[previous[s]]], nth[previous[s]])
                previous[s] = last
                k, cols = src.shape[1], src.shape[2]
                sp.dma_start(W[:, s, 0:k * cols].rearrange("p (k n) -> p k n", n=cols), src).then_inc(slot_landed[s], 16)

            n = 0
            for _ in MODS_EARLY:
                load(n)
                n += 1
            for l in range(DEPTH):
                for _ in range(17 + len(MODS_IN[l])):
                    load(n)
                    n += 1
                for s in range(4):
                    sp.wait_ge(bank_full[bank[previous[s]]], nth[previous[s]])

                def load_expert(e, done):
                    for s, (w, name) in enumerate((("w_gate_e", "gate"), ("w_up_e", "up"), ("w_down_e", "down"))):
                        if done is not None:
                            sp.wait_ge(*at(f"{name}_used", l, done))
                        cols = CH if s < 2 else D
                        src = a[w][l, bass.ds(e, 1)].rearrange("o (k p) n -> p (o k) n", p=P)
                        sp.dma_start(W[:, s, :].rearrange("p (k n) -> p k n", n=cols), src) \
                          .then_inc(S(f"{name}_in", l), 16)

                load_expert(0, None)
                sp.wait_ge(*at("nb_ready", l, 1))
                nb = sp.value_load(nbi[0:1, 0:1], min_val=0, max_val=3) + 1
                with sp.Fori(0, nb * NE - 1) as it:
                    load_expert((it + 1) % NE, it + 1)
                for name in ("gate", "up", "down"):
                    sp.wait_ge(*at(f"{name}_used", l, nb * NE))
                previous = [None] * 4
            sp.wait_ge(*at("fin_rows", "g", 4))
            for t in range(NX // P):
                sp.dma_start(out[0, t * P:(t + 1) * P, :], ztok[:, t, :]).then_inc(S("out"), 16)
            sp.wait_ge(*at("out", "g", 16 * (NX // P)))

        N_CONSTS = 16 * (7 + len(VEC) + 3)

        @block.tensor
        def _(pe):
            mm = nc.tensor.matmul

            def claim(turn):
                if before[turn]:
                    l, name, value = before[turn]
                    pe.wait_ge(*at(name, l, value))
                return banks[:, bank[turn], :]

            def full(ins, turn):
                ins.then_inc(bank_full[bank[turn]], 1)

            def landed(unit):
                pe.wait_ge(slot_landed[slot_of[unit]], landed_at[unit])

            pe.wait_ge(*at("consts", "g", N_CONSTS))
            for i, n in ((0, NVEC), (1, NBMOD)):
                o = claim(("vec", i))
                x = nc.tensor.transpose(o[:, 0:n], vrows[0:n, i, :], ident[0:n, 0:n])
                if i == 0:
                    x = mm(o[:, 256:256 + NE], ones[0:1, :], rbias[0:1, :], start=True, stop=True)
                full(x, ("vec", i))
            pe.wait_ge(*at("x_in", "g", 64))
            for k in range(KD):
                o = claim(("z", k))
                for t in range(TILES):
                    x = nc.tensor.transpose(o[:, t * P:(t + 1) * P], ztok[:, t, k * P:(k + 1) * P], ident[:, :])
                full(x, ("z", k))
            pe.wait_ge(*at("silu_c", "g", 1))
            sc = silu_c[:, :].rearrange("p (v k) -> p k v", v=2)

            def mod_product(unit, k):
                u = ("mod", *unit)
                if k == 0:
                    claim(u)
                    landed(u)
                x = mm(banks[0:2, bank[u], :], sc[:, k, :], slot(u, CH)[:, k, :], start=(k == 0), stop=(k == KD - 1))
                if k == KD - 1:
                    full(x, u)

            def mod_turn(unit):
                o = claim(("modT", *unit))
                pe.wait_ge(*at("mod_rows", "g", MODS.index(unit) + 1))
                for i in range(4):
                    x = nc.tensor.transpose(o[:, 2 * i:2 * i + 2], mod_row[0:2, i * P:(i + 1) * P], ident[0:2, 0:2])
                full(x, ("modT", *unit))

            def mod_at(l, place):
                some = MODS_IN[l]
                for part in range(*mod_parts(l, place)):
                    mod_product(some[part // KD], part % KD)
                    if part % KD == TURN_PART and part > KD:
                        mod_turn(some[part // KD - 1])
                if place == "end":
                    mod_turn(some[-1])

            for i, unit in enumerate(MODS_EARLY):
                for k in range(KD):
                    mod_product(unit, k)
                if i:
                    mod_turn(MODS_EARLY[i - 1])
            mod_turn(MODS_EARLY[-1])

            def sum_squares(turn, l, sem, cols, tiles=KD):
                o = claim(turn)
                for k in range(tiles):
                    pe.wait_ge(*at(sem, l, k + 1))
                    x = mm(o[:, cols], ones[:, :], SQ[:, k % 2, cols], start=(k == 0), stop=(k == tiles - 1))
                    if k < tiles - 1:
                        x.then_inc(S(sem + "_used", l), 1)
                full(x, turn)

            def project(turn, unit, width, c0, m, cols, kt=KD, rhs=None):
                o = claim(turn)
                landed(unit)
                w = slot(unit, width)
                rhs = H if rhs is None else rhs
                for k in range(kt):
                    x = mm(o[0:m, cols], w[:, k, c0:c0 + m], rhs[:, k, cols], start=(k == 0), stop=(k == kt - 1))
                full(x, turn)

            for l in range(DEPTH):
                every, some = slice(0, T), Nx(l)
                tiles = range(first_token(l) // P, TILES)
                if l:
                    pe.wait_ge(*at("z_ready", l - 1, 1))
                sum_squares(("ssq1", l), l, "sq1", every)
                pe.wait_ge(*at("h1", l, 2 * KD))
                for d, u in ((0, "ff"), (1, "fb")):
                    for h in range(HEADS):
                        project(("f", l, d, h), (u, l), CH, h * P, P, every)
                landed(("i", l))
                for t in range(TILES):
                    o = claim(("v", l, t))
                    for k in range(KD):
                        x = mm(o[:, :], H[:, k, t * P:(t + 1) * P], slot(("i", l), CH)[:, k, :],
                               start=(k == 0), stop=(k == KD - 1))
                    full(x, ("v", l, t))
                for h in range(HEADS):
                    project(("q", l, h), ("q", l), CH, h * P, P, some)
                for h in range(HEADS):
                    project(("g", l, h), ("g", l), CH, h * P, P, some)
                for k in range(3):
                    project(("dq", l, k), ("dq", l), QR, k * P, P, some)
                for k in range(2):
                    project(("ckv", l, k), ("dkv", l), KVR + ROPE, k * P, P, every)
                project(("kpe", l, 0), ("dkv", l), KVR + ROPE, KVR - NOPE, QK, every)
                o = claim(("kpe", l, 1))
                pe.wait_ge(*at("kpe_sw", l, 1))
                for k in range(KD):
                    x = mm(o[0:QK, :], kpe_pad[:, k * ROPE:k * ROPE + QK], H[:, k, :],
                           start=(k == 0), stop=(k == KD - 1))
                full(x, ("kpe", l, 1))

                for d in range(2):
                    pe.wait_ge(*at("q_ready", l, HEADS))
                    for h in range(HEADS):
                        mod_at(l, ("diag", d, h))
                        o = claim(("diag", l, d, h))
                        pe.wait_ge(*at("k_gate", l, d * HEADS + h + 1))
                        for c in tiles:
                            s = slice(c * P, (c + 1) * P)
                            x = mm(o[:, s], K[:, h, s], q[:, h, s], start=True, stop=True)
                        full(x, ("diag", l, d, h))
                    for n in range(len(STEPS)):
                        mod_at(l, ("lev", d, n))
                        o = claim(("lev", l, d, n))
                        pe.wait_ge(*at("qk_ready", l, d * len(STEPS) + n + 1))
                        for c in tiles:
                            s = slice(c * P, (c + 1) * P)
                            x = mm(o[:, s], QKd[:, n % 2, s], QKd[:, n % 2, s], start=True, stop=True)
                        full(x, ("lev", l, d, n))
                    mod_at(l, ("keys", d))
                    for i, c in enumerate(ORDER[d]):
                        s = slice(c * P, (c + 1) * P)
                        if i < 3:
                            o = claim(("kdT", l, d, i))
                            pe.wait_ge(*at("kd_ready", l, (d + 1) * HEADS))
                            for h in range(HEADS):
                                x = nc.tensor.transpose(o[:, h * P:(h + 1) * P], K[:, h, s], ident[:, :])
                            full(x, ("kdT", l, d, i))
                            o = claim(("st", l, d, i))
                            pe.wait_ge(*at("kdT_ready", l, d * 3 + i + 1))
                            pe.wait_ge(*at("v_ready", l, TILES))
                            for h in range(HEADS):
                                x = mm(o[:, h * P:(h + 1) * P], kdT[:, h, :], V[:, c, h * P:(h + 1) * P], start=True, stop=True)
                            full(x, ("st", l, d, i))
                            mod_at(l, ("chunk", d, i))
                        if c in tiles:
                            o = claim(("out", l, d, i))
                            pe.wait_ge(*at("att_in", l, d * 32 + 32))
                            pe.wait_ge(*at("qe_ready", l, d + 1))
                            if i:
                                pe.wait_ge(*at("state", l, (d * 3 + i) * HEADS))
                            for h in range(HEADS):
                                hp = slice(h * P, (h + 1) * P)
                                x = mm(o[:, hp], V[:, c, hp], att[:, h, s], start=True, stop=(i == 0))
                                if i:
                                    x = mm(o[:, hp], state[:, h, :], Ex[:, h, s], start=False, stop=True)
                            full(x, ("out", l, d, i))
                mod_at(l, "end")
                for h in range(HEADS):
                    o = claim(("ossq", l, h))
                    pe.wait_ge(*at("o_sq", l, h + 1))
                    full(mm(o[:, some], ones[:, :], SQ[:, h % 2, some], start=True, stop=True), ("ossq", l, h))

                sum_squares(("qssq", l), l, "dq_sq", some, 3)
                sum_squares(("kssq", l), l, "ckv_sq", every, 2)
                pe.wait_ge(*at("dq_n", l, 3))
                pe.wait_ge(*at("uq_sw", l, 3))
                for h in range(MH):
                    project(("Q", l, h), ("uq", l), MH * QK, h * QK, QK, some, 3, dq)
                    o = claim(("Qsw", l, h))
                    for k in range(3):
                        x = mm(o[0:QK, some], uq_pad[:, (k * MH + h) * ROPE:(k * MH + h) * ROPE + QK], dq[:, k, some],
                               start=(k == 0), stop=(k == 2))
                    full(x, ("Qsw", l, h))
                pe.wait_ge(*at("ckv_n", l, 2))
                for h in range(MH):
                    project(("K", l, h), ("ukv", l), MH * P, h * P, NOPE, every, 2, ckv)
                for t in range(TILES):
                    o = claim(("V", l, t))
                    w = slot(("ukv", l), MH * P)
                    for k in range(2):
                        x = mm(o[:, :].rearrange("p (h c) -> p h c", h=MH), ckv[:, k, t * P:(t + 1) * P],
                               w[:, k, :].rearrange("p (h c) -> p h c", h=MH)[:, :, NOPE:P],
                               start=(k == 0), stop=(k == 1))
                    full(x, ("V", l, t))
                steps = attention_steps(l)
                pe.wait_ge(*at("q_rope", l, MH))
                pe.wait_ge(*at("k_ready", l, MH))
                pe.wait_ge(*at("kpe_in", l, MH))
                for j in range(len(steps) + 2):
                    if j < len(steps):
                        qt, h = steps[j]
                        keys = NCTX if qt < 2 else T
                        o = claim(("sc", l, j))
                        full(mm(o[:, 0:keys], QT[0:QK, h, qt * P:(qt + 1) * P], KT[0:QK, h, 0:keys],
                                start=True, stop=True), ("sc", l, j))
                    if 1 <= j <= len(steps):
                        qt, h = steps[j - 1]
                        o = claim(("pT", l, j - 1))
                        pe.wait_ge(*at("p_norm", l, j))
                        for k in range(2 if qt < 2 else 4):
                            x = nc.tensor.transpose(o[:, k * P:(k + 1) * P], PR[:, (j - 1) % 2, k * P:(k + 1) * P], ident[:, :])
                        full(x, ("pT", l, j - 1))
                    if j >= 2:
                        qt, h = steps[j - 2]
                        o = claim(("pv", l, j - 2))
                        pe.wait_ge(*at("pT_ready", l, j - 1))
                        pe.wait_ge(*at("v2_ready", l, TILES))
                        n = 2 if qt < 2 else 4
                        for k in range(n):
                            x = mm(o[:, 0:P], V2[:, k, h // 2 * P:(h // 2 + 1) * P], PT[:, (j - 2) % 2, k * P:(k + 1) * P],
                                   start=(k == 0), stop=(k == n - 1))
                        full(x, ("pv", l, j - 2))

                pe.wait_ge(*at("a_ready", l, HEADS))
                pe.wait_ge(*at("m_ready", l, len(steps)))
                for m in range(KD):
                    c0 = m % 4 * P
                    project(("pa", l, m), ("pa", l), D, m * P, P, some, 4, O)
                    project(("ga", l, m), (f"ga{m // 4}", l), CH, c0, P, some)
                    project(("pb", l, m), ("pb", l), D, m * P, P, some, 4, MT)
                    project(("gb", l, m), (f"gb{m // 4}", l), CH, c0, P, some)
                pe.wait_ge(*at("mixed", l, KD))
                for m in range(KD):
                    project(("y", l, m), (f"o{m // 4}", l), CH, m % 4 * P, P, some, KD, mix)
                sum_squares(("ssq2", l), l, "sq2", some)
                halves = (0, 1) if l == 0 else (1,)
                o = claim(("logit", l))
                for k in range(KD):
                    pe.wait_ge(*at("h2", l, (k + 1) * len(halves)))
                    x = mm(o[0:NE, some], wr[:, k, :], H[:, k, some], start=(k == 0), stop=(k == KD - 1))
                full(x, ("logit", l))

                def turn_rows(t, g):
                    o = claim(("hT", l, t, g))
                    for k in range(4):
                        x = nc.tensor.transpose(o[:, k * P:(k + 1) * P], H[:, 4 * g + k, t * P:(t + 1) * P], ident[:, :])
                    full(x, ("hT", l, t, g))

                turn_rows(tiles[0], 0)
                o = claim(("logitT", l))
                pe.wait_ge(*at("score", l, 1))
                for i, t in enumerate(tiles):
                    x = nc.tensor.transpose(o[:, i * NE:(i + 1) * NE], scoreT[0:NE, t * P:(t + 1) * P], ident[0:NE, 0:NE])
                full(x, ("logitT", l))
                for t in tiles:
                    for g in range(2):
                        if (t, g) != (tiles[0], 0):
                            turn_rows(t, g)
                o = claim(("rank", l))
                pe.wait_ge(*at("taken", l, 1))
                n = len(tiles)
                for i in range(n):
                    for j in range(i + 1):
                        mm(o[:, i * NE:(i + 1) * NE], (before_m if j == i else ones)[:, :], rt[:, 0, j, :],
                           start=(j == 0), stop=(j == i))
                for j in range(n):
                    x = mm(o[:, n * NE:(n + 1) * NE], ones[:, :], rt[:, 0, j, :], start=(j == 0), stop=(j == n - 1))
                full(x, ("rank", l))

                for ll, name, value in last_turns[l]:
                    pe.wait_ge(*at(name, ll, value))
                pe.wait_ge(*at("htok", l, 2 * n))
                pe.wait_ge(*at("htok_lo", l, 2 * n))
                nb = pe.value_load(nbi[0:1, 0:1], min_val=0, max_val=3) + 1

                def gather(it):
                    pe.wait_ge(*at("sel", l, it + 1))
                    for half in range(2):
                        c = slice(half * 512, (half + 1) * 512)
                        for j in range(n):
                            mm(banks[:, half, :], sel[:, j, :], htok_hi[:, j, c], start=(j == 0), stop=False)
                            x = mm(banks[:, half, :], sel[:, j, :], htok_lo[:, j, c], start=False, stop=(j == n - 1))
                    x.then_inc(S("gathered", l), 1)

                def turn_gathered(it):
                    pe.wait_ge(*at("xs_tok", l, 2 * it + 2))
                    for k in range(KD):
                        x = nc.tensor.transpose(banks[:, 2 + k // 4, k % 4 * P:(k % 4 + 1) * P],
                                                xs_tok[:, k * P:(k + 1) * P], ident[:, :])
                    x.then_inc(S("xsT_full", l), 1)

                def product(o, a_hi, a_lo, w_unit, s, kt, col):
                    cols = KD * CH // kt
                    hi = w_hi[w_unit].rearrange("p (k n) -> p k n", n=cols)
                    lo = W_r[:, s, :].rearrange("p (k n) -> p k n", n=cols)
                    for k in range(kt):
                        mm(o, a_hi(k), lo[:, k, col], start=(k == 0), stop=False)
                        mm(o, a_hi(k), hi[:, k, col], start=False, stop=False)
                        x = mm(o, a_lo(k), hi[:, k, col], start=False, stop=(k == kt - 1))
                    return x

                def take_in(it):
                    pe.wait_ge(*at("xh", l, 2 * it + 2))
                    pe.wait_ge(*at("xl", l, 2 * it + 2))
                    for i, name in enumerate(("gate", "up")):
                        pe.wait_ge(*at("w_lo", l, it * 9 + 3 * i + 3))
                        pe.wait_ge(*at("w_lo_pool", l, it * 3 + i + 1))
                        product(banks[:, 4 + i, :], lambda k: xsT_hi[:, k, :], lambda k: xsT_lo[:, k, :], name, i, KD,
                                slice(0, CH)).then_inc(S(f"{name}_used", l), 1)

                def give_out(it, more):
                    pe.wait_ge(*at("selw", l, it + 1))
                    for j in range(n):
                        x = nc.tensor.transpose(banks[:, 2, j * P:(j + 1) * P], selw[:, j, :], ident[:, :])
                    x.then_inc(S("selT_full", l), 1)
                    pe.wait_ge(*at("hidden", l, it + 1))
                    for f in range(4):
                        x = nc.tensor.transpose(banks[:, 3, f * P:(f + 1) * P], hidden[:, f * P:(f + 1) * P], ident[:, :])
                    x.then_inc(S("hidT_full", l), 1)
                    if more:
                        gather(it + 1)
                    pe.wait_ge(*at("hidT", l, it + 1))
                    pe.wait_ge(*at("hidT_lo", l, it + 1))
                    pe.wait_ge(*at("w_lo", l, it * 9 + 9))
                    pe.wait_ge(*at("w_lo_pool", l, it * 3 + 3))
                    for half in range(2):
                        product(banks[:, 4 + half, :], lambda f: hidT_hi[:, f * P:(f + 1) * P], lambda f: hidT_lo[:, f * P:(f + 1) * P],
                                "down", 2, 4, slice(half * CH, (half + 1) * CH)) \
                            .then_inc(S(("y0_full", "down_used")[half], l), 1)
                    if more:
                        turn_gathered(it + 1)
                    pe.wait_ge(*at("selT", l, it + 1))
                    pe.wait_ge(*at("yl", l, it * 2 + 2))
                    for k in range(KD):
                        if k >= 4:
                            pe.wait_ge(*at("z_added", l, it * KD + k - 3))
                        o = banks[:, COMBINE[k % 4], 0:n * P]
                        mm(o, yd_hi[:, k * P:(k + 1) * P], selT[:, 0:n * P], start=True, stop=False)
                        x = mm(o, yd_lo[:, k * P:(k + 1) * P], selT[:, 0:n * P], start=False, stop=True)
                        x.then_inc(S("combined", l), 1)

                gather(0)
                turn_gathered(0)
                take_in(0)
                with pe.Fori(0, nb * NE - 1) as it:
                    give_out(it, True)
                    take_in(it + 1)
                give_out(nb * NE - 1, False)

            pe.wait_ge(*at("z_ready", DEPTH - 1, 1))
            sum_squares(("ssqf",), "g", "sqf", slice(NCTX, T))
            pe.wait_ge(*at("zf", "g", KD))
            for t in range(NX // P):
                for g in range(2):
                    o = claim(("fin", t, g))
                    for k in range(4):
                        s = slice(NCTX + t * P, NCTX + (t + 1) * P)
                        x = nc.tensor.transpose(o[:, k * P:(k + 1) * P], Z[:, 4 * g + k, s], ident[:, :])
                    full(x, ("fin", t, g))

        @block.scalar
        def _(act):
            fn = nc.scalar.activation

            def squares(src, l, sem, cols, tiles=KD):
                for k in range(tiles):
                    if k >= 2:
                        act.wait_ge(*at(sem + "_used", l, k - 1))
                    fn(SQ[:, k % 2, cols], src[:, k, cols], ACT.Square).then_inc(S(sem, l), 1)

            def rsqrt(dst, turn, l, sem, n, cols, first=0):
                o = read(act, turn)
                fn(dst, o[:, cols], ACT.Ln, bias=eps[:, 0:1], scale=1.0 / n).then_inc(S(sem, l), 1)
                act.wait_ge(*at(sem, l, first + 1))
                fn(dst, dst, ACT.Exp, scale=-0.5).then_inc(S(sem, l), 1)

            nc.scalar.preload_act_table_set("natural_log_exp_and_others")
            act.wait_ge(*at("vec_read", "g", 2))
            fn(silu_c[:, :], vecs[:, 0:16], ACT.Exp, scale=-1.0).then_inc(S("c_exp"), 1)
            act.wait_ge(*at("gam_in", "g", 1))
            fn(small[:, 3, :], small[:, 3, :], ACT.Exp).then_inc(S("gam_exp"), 1)

            def take_mod(unit):
                m = MODS.index(unit)
                o = read(act, ("mod", *unit))
                if m:
                    read(act, ("modT", *MODS[m - 1]))
                fn(mod_row[0:2, :], o[0:2, :], ACT.Copy).then_inc(S("mod_rows"), 1)

            for unit in MODS_EARLY:
                take_mod(unit)
            copied = [0] * DEPTH

            def mods_until(l, place):
                for unit in MODS_IN[l][copied[l]:mod_copied(l, place)]:
                    take_mod(unit)
                copied[l] = mod_copied(l, place)


            def modulate(l, sem, n_norm, vecs_):
                for k in range(KD):
                    act.wait_ge(*at(sem + "_n", l, k + 1))
                    for v in vecs_:
                        s = slice(v * NCTX, (v + 1) * NCTX)
                        fn(H[:, k, s], H[:, k, s], ACT.Identity, bias=modT[:, l, n_norm * 24 + k, v:v + 1],
                           scale=gainA[:, l, n_norm, k, v:v + 1]).then_inc(S(sem, l), 1)

            for l in range(DEPTH):
                every, some = slice(0, T), Nx(l)
                tiles = range(first_token(l) // P, TILES)
                nc.scalar.preload_act_table_set("natural_log_exp_and_others")
                if l == 0:
                    act.wait_ge(*at("z_loaded", "g", KD))
                    act.wait_ge(*at("eps", "g", 1))
                else:
                    act.wait_ge(*at("z_ready", l - 1, 1))
                squares(Z, l, "sq1", every)
                read(act, ("modT", *(MODS_EARLY if l == 0 else MODS_IN[l - 1])[-1]))
                rsqrt(RS[:, :], ("ssq1", l), l, "rs1", D, every)
                act.wait_ge(*at("gains", "g", 2 * l + 1))
                modulate(l, "h1", 0, (0, 1))
                nc.scalar.preload_act_table_set("sigmoid_and_others")
                for d in range(2):
                    for h in range(HEADS):
                        o = read(act, ("f", l, d, h))
                        fn(F[d][:, h, :], o, ACT.Sigmoid).then_inc(S("f_sig", l), 1)
                for h in range(HEADS):
                    o = read(act, ("q", l, h))
                    fn(q[:, h, some], o[:, some], ACT.Copy).then_inc(S("q_ready", l), 1)
                for h in range(HEADS):
                    o = read(act, ("g", l, h))
                    fn(G[:, h, some], o[:, some], ACT.Sigmoid).then_inc(S("g_sig", l), 1)
                nc.scalar.preload_act_table_set("natural_log_exp_and_others")
                for k in range(3):
                    o = read(act, ("dq", l, k))
                    fn(dq[:, k, some], o[:, some], ACT.Copy).then_inc(S("dq_raw", l), 1)
                for k in range(2):
                    o = read(act, ("ckv", l, k))
                    fn(ckv[:, k, :], o, ACT.Copy).then_inc(S("ckv_raw", l), 1)
                for d in range(2):
                    for h in range(HEADS):
                        act.wait_ge(*at("k_gate", l, d * HEADS + h + 1))
                        fn(F[d][:, h, :], F[d][:, h, :], ACT.Ln).then_inc(S("logf", l), 1)
                    for n, (m, h) in enumerate(STEPS):
                        act.wait_ge(*at("exponent", l, d * len(STEPS) + n + 1))
                        v = Ex[:, n % 4, some].rearrange("p (b s m) -> p b s m", s=2, m=m)
                        qs = 1 - d
                        fn(v[:, :, 1 - qs, :], v[:, :, 1 - qs, :], ACT.Exp, scale=-1.0)
                        fn(v[:, :, qs, :], v[:, :, qs, :], ACT.Exp).then_inc(S("decay", l), 1)
                        if n >= 3:
                            mods_until(l, ("lev", d, n - 3))
                    act.wait_ge(*at("qk_ready", l, (d + 1) * len(STEPS)))
                    fn(Ex[:, :, some], F[d][:, :, some], ACT.Exp).then_inc(S("e_b", l), 1)
                    edge = P - 1 if d == 0 else 0
                    fn(ebl[:, :, :], F[d].rearrange("p h (c t) -> p h c t", t=P)[:, :, :, edge], ACT.Exp).then_inc(S("e_b", l), 1)
                    mods_until(l, ("lev", d, len(STEPS) - 1))
                    for h in range(HEADS):
                        act.wait_ge(*at("kd_exponent", l, d * HEADS + h + 1))
                        fn(QKd[:, h % 2, :], QKd[:, h % 2, :], ACT.Exp, scale=-1.0).then_inc(S("kd_decay", l), 1)
                    mods_until(l, ("keys", d))
                    for i in range(3):
                        o = read(act, ("kdT", l, d, i))
                        if i:
                            read(act, ("st", l, d, i - 1))
                        elif d:
                            read(act, ("st", l, 0, 2))
                        fn(kdT[:, :, :].rearrange("p h t -> p (h t)"), o, ACT.Copy).then_inc(S("kdT_ready", l), 1)
                        if i:
                            mods_until(l, ("chunk", d, i - 1))
                    mods_until(l, ("chunk", d, 2))
                mods_until(l, "end")
                act.wait_ge(*at("o_acc", l, 2 * len(tiles)))
                for h in range(HEADS):
                    if h >= 2:
                        read(act, ("ossq", l, h - 2))
                    fn(SQ[:, h % 2, some], O[:, h, some], ACT.Square).then_inc(S("o_sq", l), 1)
                for h in range(HEADS):
                    rsqrt(Ex[:, h, some], ("ossq", l, h), l, "o_rs", P, some, 2 * h)
                squares(dq, l, "dq_sq", some, 3)
                read(act, ("modT", *MODS_IN[l][-1]))
                rsqrt(RS[:, some], ("qssq", l), l, "mla_rs", QR, some)
                act.wait_ge(*at("dq_n", l, 3))
                squares(ckv, l, "ckv_sq", every, 2)
                rsqrt(RS[:, :], ("kssq", l), l, "mla_rs", KVR, every, 2)
                act.wait_ge(*at("a_ready", l, HEADS))
                for h in range(MH):
                    o = read(act, ("K", l, h))
                    fn(KT[0:NOPE, h, :], o[0:NOPE, :], ACT.Copy).then_inc(S("k_ready", l), 1)
                steps = attention_steps(l)
                for j in range(len(steps) + 1):
                    if j < len(steps):
                        keys = NCTX if steps[j][0] < 2 else T
                        act.wait_ge(*at("neg_max", l, j + 1))
                        o = read(act, ("sc", l, j))
                        fn(PR[:, j % 2, 0:keys], o[:, 0:keys], ACT.Exp, bias=mx[:, 1, j:j + 1], scale=SCALE,
                           accum_out=mx[:, 2, j:j + 1]).then_inc(S("p_exp", l), 1)
                    if j:
                        keys = NCTX if steps[j - 1][0] < 2 else T
                        o = read(act, ("pT", l, j - 1))
                        fn(PT[:, (j - 1) % 2, 0:keys], o[:, 0:keys], ACT.Copy).then_inc(S("pT_ready", l), 1)
                nc.scalar.preload_act_table_set("sigmoid_and_others")
                for m in range(KD):
                    for i, g in enumerate(("ga", "gb")):
                        o = read(act, (g, l, m))
                        if m >= 2:
                            act.wait_ge(*at("mixed", l, m - 1))
                        fn(mixT[:, m % 2 * 2 + i, some], o[:, some], ACT.Sigmoid).then_inc(S("mix_sig", l), 1)
                nc.scalar.preload_act_table_set("natural_log_exp_and_others")
                act.wait_ge(*at("z_mixed", l, KD))
                squares(Z, l, "sq2", some)
                rsqrt(RS[:, some], ("ssq2", l), l, "rs2", D, some)
                nc.scalar.preload_act_table_set("sigmoid_and_others")
                act.wait_ge(*at("gains", "g", 2 * l + 2))
                modulate(l, "h2", 1, (0, 1) if l == 0 else (1,))
                n = len(tiles)
                o = read(act, ("logit", l))
                fn(scoreT[0:NE, some], o[0:NE, some], ACT.Sigmoid).then_inc(S("score", l), 1)
                for j, t in enumerate(tiles):
                    for g in range(2):
                        o = read(act, ("hT", l, t, g))
                        fn(htok_hi[:, j, g * CH:(g + 1) * CH], o, ACT.Copy).then_inc(S("htok", l), 1)
                def round_weights(name, landed, chunks=range(CHUNKS)):
                    s = ("gate", "up", "down").index(name)
                    act.wait_ge(*at(f"{name}_in", l, landed * 16))
                    for i in chunks:
                        c = (i - 1) % CHUNKS
                        c = slice(c * 1024, (c + 1) * 1024)
                        fn(w_hi[name][:, c], W[:, s, c], ACT.Copy).then_inc(S("w_hi", l), 1)

                def take_gathered(it):
                    act.wait_ge(*at("gathered", l, it + 1))
                    for half in range(2):
                        fn(xs_tok[:, half * 512:(half + 1) * 512], banks[:, half, :], ACT.Copy).then_inc(S("xs_tok", l), 1)

                def round_turned(it):
                    act.wait_ge(*at("xsT_full", l, it + 1))
                    for half in range(2):
                        fn(xsT_hi[:, half * 4:half * 4 + 4, :].rearrange("p k s -> p (k s)"), banks[:, 2 + half, :], ACT.Copy) \
                            .then_inc(S("xh", l), 1)

                def give_out(it, more):
                    round_weights("down", it + 1)
                    act.wait_ge(*at("gate_used", l, it + 1))
                    fn(gate_t, banks[:, 4, :], ACT.Sigmoid).then_inc(S("gate_sig", l), 1)
                    act.wait_ge(*at("selT_full", l, it + 1))
                    fn(selT[:, 0:n * P], banks[:, 2, 0:n * P], ACT.Sign).then_inc(S("selT", l), 1)
                    fn(selw_copy[:, 0:n * P], banks[:, 2, 0:n * P], ACT.Copy, accum_out=wslot[:, 0:1]).then_inc(S("wslot", l), 1)
                    act.wait_ge(*at("hidT_full", l, it + 1))
                    fn(hidT_hi, banks[:, 3, :], ACT.Copy).then_inc(S("hidT", l), 1)
                    if more:
                        round_weights("gate", it + 2)
                        take_gathered(it + 1)
                    act.wait_ge(*at("wslot", l, it + 1))
                    for half, name in enumerate(("y0_full", "down_used")):
                        act.wait_ge(*at(name, l, it + 1))
                        fn(yd_hi[:, half * 512:(half + 1) * 512], banks[:, 4 + half, :], ACT.Copy, scale=wslot[:, 0:1]) \
                            .then_inc(S("yh", l), 1)
                        if more and half == 0:
                            round_weights("up", it + 2, range(2))
                    if more:
                        round_turned(it + 1)
                        round_weights("up", it + 2, range(2, CHUNKS))

                round_weights("gate", 1)
                round_weights("up", 1)
                act.wait_ge(*at("nb_ready", l, 1))
                nb = act.value_load(nbi[0:1, 0:1], min_val=0, max_val=3) + 1
                take_gathered(0)
                round_turned(0)
                with act.Fori(0, nb * NE - 1) as it:
                    give_out(it, True)
                give_out(nb * NE - 1, False)
            nc.scalar.preload_act_table_set("natural_log_exp_and_others")
            act.wait_ge(*at("z_ready", DEPTH - 1, 1))
            squares(Z, "g", "sqf", slice(NCTX, T))
            rsqrt(RS[:, NCTX:T], ("ssqf",), "g", "rsf", D, slice(NCTX, T))
            for t in range(NX // P):
                for g in range(2):
                    o = read(act, ("fin", t, g))
                    fn(ztok[:, t, g * CH:(g + 1) * CH], o, ACT.Copy).then_inc(S("fin_rows"), 1)

        @block.gpsimd
        def _(pool):
            nc.gpsimd.memset(uq_pad[:, 0:NOPE], 0.0)
            nc.gpsimd.memset(kpe_pad[:, 0:NOPE], 0.0)
            for l in range(DEPTH):
                def swapped(dst, src):
                    d4 = dst.rearrange("p h (a s i) -> p h a s i", a=2, s=2)
                    s4 = src.rearrange("p h (a s i) -> p h a s i", a=2, s=2)
                    for ax in range(2):
                        nc.gpsimd.tensor_scalar(d4[:, :, ax, 0, :], s4[:, :, ax, 1, :], -1.0, None, ALU.mult)
                        x = nc.gpsimd.tensor_copy(d4[:, :, ax, 1, :], s4[:, :, ax, 0, :])
                    return x

                u = ("dkv", l)
                pool.wait_ge(slot_landed[slot_of[u]], landed_at[u])
                swapped(kpe_sw[:, :, :], slot(u, KVR + ROPE)[:, 0:KD, KVR:KVR + ROPE]).then_inc(S("kpe_sw", l), 1)
                u = ("uq", l)
                pool.wait_ge(slot_landed[slot_of[u]], landed_at[u])
                if l:
                    read(pool, ("Qsw", l - 1, MH - 1))
                for k in range(3):
                    w = slot(u, MH * QK)[:, k, :].rearrange("p (h c) -> p h c", h=MH)
                    swapped(uq_sw[:, k, :, :], w[:, :, NOPE:QK]).then_inc(S("uq_sw", l), 1)
                pool.wait_ge(*at("uq_sw", l, 3))
                pool.wait_ge(*at("kpe_ready", l, 1))
                pool.wait_ge(*at("a_ready", l, HEADS))
                for h in range(MH):
                    nc.gpsimd.tensor_copy(KT[NOPE:QK, h, :], kpe[NOPE:QK, :]).then_inc(S("kpe_in", l), 1)

                def rest(name, rounded, before):
                    s = ("gate", "up", "down").index(name)
                    c = slice((CHUNKS - 1) * 1024, CHUNKS * 1024)
                    pool.wait_ge(*at("w_hi", l, rounded))
                    if before is not None:
                        pool.wait_ge(*at("w_lo_pool", l, before))
                    nc.gpsimd.tensor_tensor(W_r[:, s, c], W[:, s, c], w_hi[name][:, c].bitcast(F32), ALU.subtract) \
                        .then_inc(S("w_lo_pool", l), 1)

                rest("gate", 1, None)
                rest("up", 5, 1)
                pool.wait_ge(*at("nb_ready", l, 1))
                nb = pool.value_load(nbi[0:1, 0:1], min_val=0, max_val=3) + 1
                with pool.Fori(0, nb * NE - 1) as it:
                    for i, name in enumerate(("down", "gate", "up")):
                        rest(name, it * 12 + 9 + 4 * i, it * 3 + 2 + i)
                rest("down", nb * (NE * 12) - 3, nb * (NE * 3) - 1)

        @block.vector
        def _(dve):
            vv = nc.vector
            chain = [0]

            def link(ins):
                chain[0] += 1
                ins.then_inc(S("chain"), 1)
                dve.wait_ge(*at("chain", "g", chain[0]))

            vv.memset(eps[:], EPS).then_inc(S("eps"), 1)
            dve.wait_ge(*at("consts", "g", N_CONSTS))
            vv.tensor_copy(masks[:, :, :, :].rearrange("p d v t -> p (d v t)"), masks_in)
            o = read(dve, ("vec", 0))
            vv.tensor_copy(rb[:], o[:, 256:256 + NE])
            vv.tensor_copy(vecs[:], o[:, 0:NVEC]).then_inc(S("vec_read"), 1)
            o = read(dve, ("vec", 1))
            vv.tensor_copy(bmod[:], o[:, 0:NBMOD]).then_inc(S("vec_read"), 1)
            for k in range(KD):
                o = read(dve, ("z", k))
                vv.tensor_copy(Z[:, k, :], o).then_inc(S("z_loaded"), 1)
            dve.wait_ge(*at("c_exp", "g", 1))
            link(vv.tensor_scalar(silu_c[:], silu_c[:], 1.0, None, ALU.add))
            link(vv.reciprocal(silu_c[:], silu_c[:]))
            link(vv.tensor_tensor(small[:, 0, :], silu_c[:], vecs[:, 0:16], ALU.mult))
            link(vv.tensor_copy(silu_c[:, 0:8], small[:, 0, 8:16]))
            vv.tensor_copy(silu_c[:, 8:16], small[:, 0, 0:8]).then_inc(S("silu_c"), 1)
            for d, name in enumerate(("gamma_fwd", "gamma_bwd")):
                g = vec(name).rearrange("p (l h) -> p l h", l=DEPTH)
                e_, s_ = small[:, 3, 8 * d:8 * d + 8].rearrange("p (l h) -> p l h", l=2), small[:, 1 + d, 0:4]
                link(vv.tensor_tensor(s_, g[:, 0, :], g[:, 1, :], ALU.max))
                x = vv.tensor_tensor(e_, g, s_.unsqueeze(1).to_broadcast([P, 2, HEADS]), ALU.subtract)
            x.then_inc(S("gam_in"), 1)
            dve.wait_ge(*at("gam_exp", "g", 1))
            g4 = small[:, 3, :].rearrange("p (d l h) -> p d l h", d=2, l=2)
            s4 = small[:, 4, 0:8].rearrange("p (d h) -> p d h", d=2)
            link(vv.tensor_tensor(s4, g4[:, :, 0, :], g4[:, :, 1, :], ALU.add))
            link(vv.reciprocal(s4, s4))
            link(vv.tensor_tensor(g4, g4, s4.unsqueeze(2).to_broadcast([P, 2, 2, HEADS]), ALU.mult))
            link(vv.tensor_tensor(s4, g4[:, :, 0, :], g4[:, :, 1, :], ALU.add))
            vv.tensor_tensor(lb[:, :, 0, :], g4[:, :, 0, :], g4[:, :, 0, :], ALU.subtract)
            link(vv.tensor_tensor(lb[:, :, 1, :], s4, g4[:, :, 0, :], ALU.subtract))
            link(vv.tensor_scalar(oml[:], lb[:], -1.0, 1.0, ALU.mult, ALU.add))
            def add_mod(unit):
                l, j = unit
                o = read(dve, ("modT", l, j))
                vv.tensor_tensor(modT[:, l, 4 * j:4 * j + 4, :], o[:, 0:8].rearrange("p (n v) -> p n v", v=2),
                                 bmod[:, l * 48 + 4 * j:l * 48 + 4 * j + 4].unsqueeze(2).to_broadcast([P, 4, 2]), ALU.add) \
                  .then_inc(S("mod_added"), 1)

            def gains(l, i):
                dve.wait_ge(*at("mod_added", "g", MODS.index((l, 6 * i + 3)) + 1))
                first = VEC[("norm1_g", "norm2_g")[i]][0] + l * KD
                vv.scalar_tensor_tensor(
                    out=gainA[:, l, i, :, :], in0=modT[:, l, i * 24 + 8:i * 24 + 16, :], scalar=1.0,
                    in1=vecs[:, first:first + KD].unsqueeze(2).to_broadcast([P, KD, 2]), op0=ALU.add, op1=ALU.mult) \
                  .then_inc(S("gains"), 1)

            for unit in MODS_EARLY:
                add_mod(unit)
            turned = [0] * DEPTH

            def mods_until(l, place):
                for unit in MODS_IN[l][turned[l]:mod_turned(l, place)]:
                    add_mod(unit)
                turned[l] = mod_turned(l, place)

            for l in range(DEPTH):
                every, some = slice(0, T), Nx(l)
                tiles = range(first_token(l) // P, TILES)
                n = len(tiles)
                halves = (0, 1) if l == 0 else (1,)
                gains(l, 0)
                dve.wait_ge(*at("rs1", l, 2))
                for k in range(KD):
                    vv.tensor_tensor(H[:, k, :], Z[:, k, :], RS[:, :], ALU.mult).then_inc(S("h1_n", l), 1)
                for d in range(2):
                    for h in range(HEADS):
                        f = F[d][:, h, :]
                        dve.wait_ge(*at("f_sig", l, d * HEADS + h + 1))
                        link(vv.tensor_scalar(f, f, oml[:, d, l, h:h + 1], lb[:, d, l, h:h + 1], ALU.mult, ALU.add))
                        if d == 0:
                            vv.tensor_scalar(K[:, h, :], f, -1.0, 1.0, ALU.mult, ALU.add).then_inc(S("k_gate", l), 1)
                for t in range(TILES):
                    o = read(dve, ("v", l, t))
                    vv.tensor_copy(V[:, t, :], o).then_inc(S("v_ready", l), 1)
                for h in range(HEADS):
                    dve.wait_ge(*at("g_sig", l, h + 1))
                    g = G[:, h, some]
                    o = read(dve, ("g", l, h))
                    vv.tensor_tensor(g, o[:, some], g, ALU.mult).then_inc(S("g_ready", l), 1)
                rp = slice(NOPE, QK)
                o = read(dve, ("kpe", l, 0))
                vv.tensor_tensor(kpe[rp, :], o[rp, :], rope[rp, 0, :], ALU.mult).then_inc(S("kpe_mul", l), 1)
                o = read(dve, ("kpe", l, 1))
                vv.tensor_tensor(RS[rp, :], o[rp, :], rope[rp, 1, :], ALU.mult).then_inc(S("kpe_mul", l), 1)
                dve.wait_ge(*at("kpe_mul", l, 2))
                vv.tensor_tensor(kpe[rp, :], kpe[rp, :], RS[rp, :], ALU.add).then_inc(S("kpe_ready", l), 1)

                for d in range(2):
                    if d:
                        for h in range(HEADS):
                            vv.tensor_scalar(K[:, h, :], F[1][:, h, :], -1.0, 1.0, ALU.mult, ALU.add).then_inc(S("k_gate", l), 1)
                    vv.memset(att[:, :, :], 0.0).then_inc(S("att_zero", l), 1)
                    for h in range(HEADS):
                        dve.wait_ge(*at("logf", l, d * HEADS + h + 1))
                        for c in range(TILES):
                            b = F[d][:, h, c * P:(c + 1) * P]
                            b = b if d == 0 else b[:, ::-1]
                            x = vv.tensor_tensor_scan(b, ones[:, :], b, 0.0, ALU.mult, ALU.add)
                        x.then_inc(S("b_ready", l), 1)
                    dve.wait_ge(*at("b_ready", l, (d + 1) * HEADS))
                    dve.wait_ge(*at("q_ready", l, HEADS))
                    dve.wait_ge(*at("att_zero", l, d + 1))

                    def insert(turn, level, h):
                        o = read(dve, turn)
                        vv.copy_predicated(
                            att[:, h, some].rearrange("p (c t) -> p c t", t=P),
                            masks[:, d, level, :].unsqueeze(1).to_broadcast([P, n, P]),
                            o[:, some].rearrange("p (c t) -> p c t", t=P)).then_inc(S("att_in", l), 1)

                    for h in range(HEADS):
                        insert(("diag", l, d, h), 7, h)
                    base = d * len(STEPS)
                    for i in range(len(STEPS) + 3):
                        if i >= 3:
                            m, h = STEPS[i - 3]
                            insert(("lev", l, d, i - 3), LEVELS.index(m), h)
                            mods_until(l, ("lev", d, i - 3))
                        if i < len(STEPS):
                            m, h = STEPS[i]
                            v = F[d][:, h, some].rearrange("p (b s m) -> p b s m", s=2, m=m)
                            mid = v[:, :, 0, m - 1:m] if d == 0 else v[:, :, 1, 0:1]
                            nbk = n * P // (2 * m)
                            vv.tensor_tensor(Ex[:, i % 4, some].rearrange("p (b m) -> p b m", m=2 * m),
                                             F[d][:, h, some].rearrange("p (b m) -> p b m", m=2 * m),
                                             mid.to_broadcast([P, nbk, 2 * m]), ALU.subtract).then_inc(S("exponent", l), 1)
                        if 1 <= i <= len(STEPS):
                            m, h = STEPS[i - 1]
                            dve.wait_ge(*at("decay", l, base + i))
                            split = lambda x: x.rearrange("p (b s m) -> p b s m", s=2, m=m)
                            qs = 1 - d
                            for src, s, last in ((q, qs, False), (K, 1 - qs, True)):
                                x = vv.tensor_tensor(split(QKd[:, (i - 1) % 2, some])[:, :, s, :],
                                                     split(src[:, h, some])[:, :, s, :],
                                                     split(Ex[:, (i - 1) % 4, some])[:, :, s, :], ALU.mult)
                            x.then_inc(S("qk_ready", l), 1)
                    edge = P - 1 if d == 0 else 0

                    def decay_keys(h):
                        dve.wait_ge(*at("kd_decay", l, d * HEADS + h + 1))
                        vv.tensor_tensor(K[:, h, :], QKd[:, h % 2, :], K[:, h, :], ALU.mult).then_inc(S("kd_ready", l), 1)

                    for h in range(HEADS):
                        b = F[d][:, h, :].rearrange("p (c t) -> p c t", t=P)
                        if h >= 2:
                            dve.wait_ge(*at("kd_ready", l, d * HEADS + h - 1))
                        vv.tensor_tensor(QKd[:, h % 2, :].rearrange("p (c t) -> p c t", t=P), b,
                                         b[:, :, edge:edge + 1].to_broadcast([P, TILES, P]), ALU.subtract) \
                          .then_inc(S("kd_exponent", l), 1)
                        if h >= 1:
                            decay_keys(h - 1)
                    decay_keys(HEADS - 1)
                    dve.wait_ge(*at("e_b", l, 2 * d + 2))
                    vv.tensor_tensor(Ex[:, :, some], Ex[:, :, some], q[:, :, some], ALU.mult).then_inc(S("qe_ready", l), 1)
                    mods_until(l, ("keys", d))
                    for i, c in enumerate(ORDER[d]):
                        if c in tiles:
                            s = slice(c * P, (c + 1) * P)
                            o = read(dve, ("out", l, d, i)).rearrange("p (h t) -> p h t", h=HEADS)
                            if d == 0:
                                vv.tensor_copy(O[:, :, s], o).then_inc(S("o_acc", l), 1)
                            else:
                                vv.tensor_tensor(O[:, :, s], o, O[:, :, s], ALU.add).then_inc(S("o_acc", l), 1)
                        if i < 3:
                            o = read(dve, ("st", l, d, i))
                            if i:
                                mods_until(l, ("chunk", d, i - 1))
                                dve.wait_ge(*at("state", l, (d * 3 + i) * HEADS))
                            for h in range(HEADS):
                                ps = o[:, h * P:(h + 1) * P]
                                if i == 0:
                                    x = vv.tensor_copy(state[:, h, :], ps)
                                else:
                                    x = vv.scalar_tensor_tensor(out=state[:, h, :], in0=state[:, h, :], scalar=ebl[:, h, c:c + 1],
                                                                in1=ps, op0=ALU.mult, op1=ALU.add)
                                x.then_inc(S("state", l), 1)
                mods_until(l, "end")
                for h in range(HEADS):
                    dve.wait_ge(*at("o_rs", l, 2 * h + 2))
                    link(vv.tensor_tensor(O[:, h, some], O[:, h, some], Ex[:, h, some], ALU.mult))
                    vv.scalar_tensor_tensor(out=O[:, h, some], in0=O[:, h, some], scalar=vec("hg_norm_g")[:, l * HEADS + h:l * HEADS + h + 1],
                                            in1=G[:, h, some], op0=ALU.mult, op1=ALU.mult).then_inc(S("a_ready", l), 1)
                dve.wait_ge(*at("mla_rs", l, 2))
                for k in range(3):
                    vv.scalar_tensor_tensor(out=dq[:, k, some], in0=dq[:, k, some], scalar=vec("q_norm_g")[:, l * 3 + k:l * 3 + k + 1],
                                            in1=RS[:, some], op0=ALU.mult, op1=ALU.mult).then_inc(S("dq_n", l), 1)
                dve.wait_ge(*at("mla_rs", l, 4))
                for k in range(2):
                    vv.scalar_tensor_tensor(out=ckv[:, k, :], in0=ckv[:, k, :], scalar=vec("kv_norm_g")[:, l * 2 + k:l * 2 + k + 1],
                                            in1=RS[:, :], op0=ALU.mult, op1=ALU.mult).then_inc(S("ckv_n", l), 1)
                for h in range(MH):
                    o = read(dve, ("Q", l, h))
                    vv.tensor_tensor(QT[0:QK, h, some], o[0:QK, some], rope[0:QK, 0, some], ALU.mult).then_inc(S("q_rot", l), 1)
                    o = read(dve, ("Qsw", l, h))
                    vv.tensor_tensor(tmpQ[0:QK, h % 2, some], o[0:QK, some], rope[0:QK, 1, some], ALU.mult).then_inc(S("q_rot", l), 1)
                    dve.wait_ge(*at("q_rot", l, 2 * h + 2))
                    vv.tensor_tensor(QT[0:QK, h, some], QT[0:QK, h, some], tmpQ[0:QK, h % 2, some], ALU.add).then_inc(S("q_rope", l), 1)
                for t in range(TILES):
                    o = read(dve, ("V", l, t))
                    vv.tensor_copy(V2[:, t, :], o).then_inc(S("v2_ready", l), 1)
                steps = attention_steps(l)
                for j in range(len(steps) + 2):
                    if j < len(steps):
                        keys = NCTX if steps[j][0] < 2 else T
                        o = read(dve, ("sc", l, j))
                        link(vv.reduce_max(mx[:, 0, j:j + 1], o[:, 0:keys], AX_X))
                        vv.tensor_scalar(mx[:, 1, j:j + 1], mx[:, 0, j:j + 1], -SCALE, None, ALU.mult).then_inc(S("neg_max", l), 1)
                    if 1 <= j <= len(steps):
                        i = j - 1
                        keys = NCTX if steps[i][0] < 2 else T
                        dve.wait_ge(*at("p_exp", l, i + 1))
                        link(vv.reciprocal(mx[:, 3, i:i + 1], mx[:, 2, i:i + 1]))
                        vv.tensor_scalar(PR[:, i % 2, 0:keys], PR[:, i % 2, 0:keys], mx[:, 3, i:i + 1], None, ALU.mult) \
                          .then_inc(S("p_norm", l), 1)
                    if j >= 2:
                        qt, h = steps[j - 2]
                        rows = slice(h % 2 * MV, (h % 2 + 1) * MV)
                        o = read(dve, ("pv", l, j - 2))
                        vv.tensor_copy(MT[rows, h // 2, qt * P:(qt + 1) * P], o[rows, 0:P]).then_inc(S("m_ready", l), 1)
                for m in range(KD):
                    for i, (g, w, sem) in enumerate((("ga", "pa", "mix_a"), ("gb", "pb", "mix_b"))):
                        t_ = mixT[:, m % 2 * 2 + i, some]
                        dve.wait_ge(*at("mix_sig", l, 2 * m + i + 1))
                        o = read(dve, (w, l, m))
                        vv.tensor_tensor(t_, o[:, some], t_, ALU.mult).then_inc(S(sem, l), 1)
                    dve.wait_ge(*at("mix_a", l, m + 1))
                    dve.wait_ge(*at("mix_b", l, m + 1))
                    vv.tensor_tensor(mix[:, m, some], mixT[:, m % 2 * 2, some], mixT[:, m % 2 * 2 + 1, some], ALU.add) \
                      .then_inc(S("mixed", l), 1)
                for m in range(KD):
                    o = read(dve, ("y", l, m))
                    for v in halves:
                        s = slice(v * NCTX, (v + 1) * NCTX)
                        x = vv.scalar_tensor_tensor(out=Z[:, m, s], in0=o[:, s], scalar=modT[:, l, 16 + m, v:v + 1], in1=Z[:, m, s],
                                                    op0=ALU.mult, op1=ALU.add)
                    x.then_inc(S("z_mixed", l), 1)
                gains(l, 1)
                dve.wait_ge(*at("z_mixed", l, KD))
                dve.wait_ge(*at("rs2", l, 2))
                for k in range(KD):
                    vv.tensor_tensor(H[:, k, some], Z[:, k, some], RS[:, some], ALU.mult).then_inc(S("h2_n", l), 1)

                R = lambda i: rt[:, i, 0:n, :]
                o = read(dve, ("logitT", l))[:, 0:n * NE].rearrange("p (t e) -> p t e", e=NE)
                vv.tensor_tensor(R(2), o, rb[:, :].unsqueeze(1).to_broadcast([P, n, NE]), ALU.add)
                vv.tensor_copy(R(1), o).then_inc(S("scored", l), 1)
                dve.wait_ge(*at("scored", l, 1))
                s2 = R(2).rearrange("p t (g e) -> p (t g) e", g=NG)
                gs = rt[:, 3, :, :].rearrange("p t e -> p (t e)")[:, 0:n * NG].rearrange("p (t g) -> p t g", g=NG)

                def compare(dst, values, groups):
                    shape = [P, groups, EG, EG]
                    ge, gt = (compared[:, i, 0:groups * EG * EG].rearrange("p (x j i) -> p x j i", j=EG, i=EG) for i in range(2))
                    first, second = (values.unsqueeze(2).to_broadcast(shape), values.unsqueeze(3).to_broadcast(shape))
                    vv.tensor_tensor(ge, first, second, ALU.is_ge)
                    link(vv.tensor_tensor(gt, first, second, ALU.is_gt))
                    vv.tensor_tensor(ge, ge, pair[:, 0, :, :].unsqueeze(1).to_broadcast(shape), ALU.mult)
                    link(vv.tensor_tensor(gt, gt, pair[:, 1, :, :].unsqueeze(1).to_broadcast(shape), ALU.mult))
                    link(vv.tensor_tensor(ge, ge, gt, ALU.add))
                    link(vv.tensor_reduce(dst, ge, AX_X, ALU.add))

                sums = compared[:, 2, 0:n * NG * EG * EG].rearrange("p (x i j) -> p x i j", i=EG, j=EG)
                shape = [P, n * NG, EG, EG]
                link(vv.tensor_tensor(sums, s2.unsqueeze(2).to_broadcast(shape), s2.unsqueeze(3).to_broadcast(shape), ALU.add))
                link(vv.tensor_tensor(sums, sums, pair[:, 2, :, :].unsqueeze(1).to_broadcast(shape), ALU.add))
                link(vv.tensor_reduce(gs.rearrange("p t g -> p (t g)"), sums.rearrange("p x i j -> p x (i j)"), AX_X, ALU.max))
                ahead_e = R(4).rearrange("p t (g e) -> p (t g) e", g=NG)
                ahead_g = rt[:, 5, :, :].rearrange("p t e -> p (t e)")[:, 0:n * NG].rearrange("p (t g) -> p t g", g=NG)
                compare(ahead_e, s2, n * NG)
                compare(ahead_g, gs, n)
                link(vv.tensor_scalar(ahead_g, ahead_g, 0.5, None, ALU.is_lt))
                vv.scalar_tensor_tensor(out=R(0).rearrange("p t (g e) -> p (t g) e", g=NG), in0=ahead_e, scalar=1.5,
                                        in1=ahead_g.rearrange("p t g -> p (t g)").unsqueeze(2).to_broadcast([P, n * NG, EG]),
                                        op0=ALU.is_lt, op1=ALU.mult).then_inc(S("taken", l), 1)
                dve.wait_ge(*at("taken", l, 1))
                link(vv.tensor_tensor(R(9), R(1), R(0), ALU.mult))
                wsum = rt[:, 10, 0:n, 0]
                link(vv.tensor_reduce(wsum, R(9), AX_X, ALU.add))
                link(vv.reciprocal(wsum, wsum))
                for r in range(ROUNDS):
                    x = vv.tensor_tensor(gw[:, 0:n, r * NE:(r + 1) * NE], R(9), wsum.unsqueeze(2).to_broadcast([P, n, NE]), ALU.mult)
                link(x)
                for j, t in enumerate(tiles):
                    for g in range(2):
                        o = read(dve, ("hT", l, t, g))
                        c = slice(g * CH, (g + 1) * CH)
                        dve.wait_ge(*at("htok", l, j * 2 + g + 1))
                        vv.tensor_tensor(htok_lo[:, j, c], o, htok_hi[:, j, c].bitcast(F32), ALU.subtract) \
                          .then_inc(S("htok_lo", l), 1)

                o = read(dve, ("rank", l))
                place = rt[:, 11, 0:n, :]
                link(vv.scalar_tensor_tensor(out=place, in0=o[:, 0:n * NE].rearrange("p (t e) -> p t e", e=NE), scalar=FAR,
                                             in1=R(0), op0=ALU.add, op1=ALU.mult))
                for r in range(ROUNDS):
                    link(vv.tensor_scalar(pos[:, 0:n, r * NE:(r + 1) * NE], place, -FAR - CAP * r, None, ALU.add))
                link(vv.reduce_max(cnt[:, 0:1], o[:, n * NE:(n + 1) * NE], AX_X))
                for i in range(1, 4):
                    link(vv.tensor_scalar(cnt[:, i:i + 1], cnt[:, 0:1], float(CAP * i), None, ALU.is_gt))
                link(vv.tensor_tensor(cnt[:, 1:2], cnt[:, 1:2], cnt[:, 2:3], ALU.add))
                link(vv.tensor_tensor(cnt[:, 4:5], cnt[:, 1:2], cnt[:, 3:4], ALU.add))
                vv.tensor_copy(nbi[:, :], cnt[:, 4:5]).then_inc(S("nb_ready", l), 1)
                dve.wait_ge(*at("nb_ready", l, 1))
                nb = dve.value_load(nbi[0:1, 0:1], min_val=0, max_val=3) + 1

                def select(it):
                    for j in range(n):
                        x = vv.tensor_scalar(sel[:, j, :], slot_no[:, :], pos[:, j, bass.ds(it, 1)], None, ALU.is_equal)
                    x.then_inc(S("sel", l), 1)

                def rest(name, rounded, chunks=range(CHUNKS - 1)):
                    s = ("gate", "up", "down").index(name)
                    for i in chunks:
                        c = slice(i * 1024, (i + 1) * 1024)
                        dve.wait_ge(*at("w_hi", l, rounded + i + 1))
                        vv.tensor_tensor(W_r[:, s, c], W[:, s, c], w_hi[name][:, c].bitcast(F32), ALU.subtract) \
                          .then_inc(S("w_lo", l), 1)

                def rest_turned(it):
                    for half in range(2):
                        k = slice(half * 4, half * 4 + 4)
                        dve.wait_ge(*at("xh", l, it * 2 + half + 1))
                        vv.tensor_tensor(xsT_lo[:, k, :].rearrange("p k s -> p (k s)"), banks[:, 2 + half, :],
                                         xsT_hi[:, k, :].rearrange("p k s -> p (k s)").bitcast(F32), ALU.subtract) \
                          .then_inc(S("xl", l), 1)

                def give_out(it, more):
                    if more:
                        select(it + 1)
                    for j in range(n):
                        x = vv.tensor_scalar(selw[:, j, :], slot_no[:, :], pos[:, j, bass.ds(it, 1)], gw[:, j, bass.ds(it, 1)],
                                             ALU.is_equal, ALU.mult)
                    x.then_inc(S("selw", l), 1)
                    rest("down", it * 12 + 9)
                    dve.wait_ge(*at("gate_sig", l, it + 1))
                    vv.tensor_tensor(gate_t, banks[:, 4, :], gate_t, ALU.mult).then_inc(S("silu", l), 1)
                    dve.wait_ge(*at("silu", l, it + 1))
                    dve.wait_ge(*at("up_used", l, it + 1))
                    vv.tensor_tensor(hidden, banks[:, 5, :], gate_t, ALU.mult).then_inc(S("hidden", l), 1)
                    dve.wait_ge(*at("hidT", l, it + 1))
                    vv.tensor_tensor(hidT_lo, banks[:, 3, :], hidT_hi.bitcast(F32), ALU.subtract).then_inc(S("hidT_lo", l), 1)
                    if more:
                        rest("gate", it * 12 + 13)
                    for half in range(2):
                        c = slice(half * 512, (half + 1) * 512)
                        dve.wait_ge(*at("yh", l, it * 2 + half + 1))
                        vv.scalar_tensor_tensor(out=yd_lo[:, c], in0=banks[:, 4 + half, :], scalar=wslot[:, 0:1],
                                                in1=yd_hi[:, c].bitcast(F32), op0=ALU.mult, op1=ALU.subtract) \
                          .then_inc(S("yl", l), 1)
                        if more and half == 0:
                            rest("up", it * 12 + 17, range(1))
                    if more:
                        rest_turned(it + 1)
                    for k in range(KD):
                        if more and k == 4:
                            rest("up", it * 12 + 17, range(1, CHUNKS - 1))
                        dve.wait_ge(*at("combined", l, it * KD + k + 1))
                        for v in halves:
                            s = slice(v * NCTX, (v + 1) * NCTX)
                            c0 = v * NCTX - first_token(l)
                            x = vv.scalar_tensor_tensor(out=Z[:, k, s], in0=banks[:, COMBINE[k % 4], c0:c0 + NCTX],
                                                        scalar=modT[:, l, 40 + k, v:v + 1], in1=Z[:, k, s],
                                                        op0=ALU.mult, op1=ALU.add)
                        x.then_inc(S("z_added", l), 1)

                select(0)
                rest("gate", 1)
                rest("up", 5)
                rest_turned(0)
                with dve.Fori(0, nb * NE - 1) as it:
                    give_out(it, True)
                give_out(nb * NE - 1, False)
                vv.tensor_copy(small[:, 6, 0:1], small[:, 4, 0:1]).then_inc(S("z_ready", l), 1)

            dve.wait_ge(*at("rsf", "g", 2))
            for k in range(KD):
                vv.scalar_tensor_tensor(out=Z[:, k, NCTX:T], in0=Z[:, k, NCTX:T], scalar=vec("final_g")[:, k:k + 1],
                                        in1=RS[:, NCTX:T], op0=ALU.mult, op1=ALU.mult).then_inc(S("zf"), 1)


def shape_constants():
    p = np.arange(P)
    s, t = p[:, None], p[None, :]
    masks = np.zeros((P, 2, 8, P), np.int32)
    for i, m in enumerate(LEVELS):
        same = s // (2 * m) == t // (2 * m)
        masks[:, 0, i] = same & (s % (2 * m) < m) & (t % (2 * m) >= m)
        masks[:, 1, i] = same & (s % (2 * m) >= m) & (t % (2 * m) < m)
    masks[:, :, 7] = (s == t)[:, None, :]
    e = np.arange(EG)
    rope = np.zeros((P, 2, T), np.float32)
    rope[:, 0] = 1.0
    axis = ROPE // 2
    inv = np.float32(10000.0) ** (-np.arange(0, axis, 2, dtype=np.float32) / np.float32(axis))
    tok = np.arange(NX)
    for ax, at in enumerate((tok // 64, tok % 64)):
        ang = (at.astype(np.float32)[None, :] * inv[:, None]).astype(np.float32)
        for half in range(2):
            r = NOPE + ax * axis + half * 8
            rope[r:r + 8, 0, NCTX:] = np.cos(ang)
            rope[r:r + 8, 1, NCTX:] = np.sin(ang)
    return {
        "k_ident": np.eye(P, dtype=np.float32), "k_ones": np.ones((P, P), np.float32),
        "k_before": (s < t).astype(np.float32), "k_slot": np.broadcast_to(p.astype(np.float32), (P, P)).copy(),
        "k_pair": np.broadcast_to(np.stack([e[None, :] < e[:, None], e[None, :] > e[:, None], (e[None, :] == e[:, None]) * -1e30])
                                  .astype(np.float32), (P, 3, EG, EG)).copy(),
        "k_masks": masks.reshape(P, -1), "k_rope": rope,
    }


_INS = ['x', 'c', 'ctx', 'c_ctx', 'w_mod', 'b_mod', 'norm1_g', 'norm2_g', 'w_in', 'gamma_fwd', 'gamma_bwd', 'hg_norm_g',
        'q_norm_g', 'kv_norm_g', 'w_uq', 'w_ukv', 'w_pa', 'w_pb', 'w_o', 'w_router', 'router_bias',
        'w_gate_e', 'w_up_e', 'w_down_e', 'final_g']


def kernel(**inputs):
    import concourse.bacc as _bacc
    from concourse.bass_utils import run_bass_kernel_spmd as _run

    nc = _bacc.Bacc("TRN2", target_bir_lowering=False, num_devices=1)
    arrays, args = {}, {}
    given = {name: np.ascontiguousarray(inputs[name]) for name in _INS}
    for name, value in {**given, **shape_constants()}.items():
        arrays[f"in_{name}"] = value
        args[name] = nc.dram_tensor(f"in_{name}", value.shape, mybir.dt.from_np(value.dtype), kind="ExternalInput").ap()
    out = nc.dram_tensor("out_0", (1, NX, D), F32, kind="ExternalOutput").ap()
    bass_hybrid_transformer(nc, args, out)
    r = _run(nc, [arrays], core_ids=[0])
    return r.results[0]["out_0"]
```

```python
from contextlib import ExitStack

import numpy as np

import concourse.bass as bass
from concourse import mybir

ALU = mybir.AluOpType
ACT = mybir.ActivationFunctionType
F32 = mybir.dt.float32
F32R = mybir.dt.float32r
I32 = mybir.dt.int32
U8 = mybir.dt.uint8
AX_X = mybir.AxisListType.X

P = 128
D = 1024
KD = D // P
NCTX, NX = 256, 256
T = NCTX + NX
TILES = T // P
DEPTH = 2
EPS = 1e-6
HEADS = 4
MH, NOPE, ROPE, MV = 8, 64, 32, 64
QK = NOPE + ROPE
QR, KVR = 384, 256
SCALE = QK ** -0.5
NE, NG, EG = 16, 4, 4
DE = 512
COMBINE = (6, 7, 0, 1, 0, 1, 6, 7)
UNITS = ("gate", "up", "down")
CHUNKS = 4
BY_POOL = dict(gate=2, up=1, down=2)
POOL_UNTIL = {name: sum(BY_POOL[u] for u in UNITS[:i + 1]) for i, name in enumerate(UNITS)}
ROUNDING = {name: [(i - BY_POOL[name]) % CHUNKS for i in range(CHUNKS)] if name != "down" else list(range(CHUNKS))
            for name in UNITS}
DVE_UNTIL = {name: CHUNKS * (i + 1) - POOL_UNTIL[name] for i, name in enumerate(UNITS)}
CAP = P
MOD = 6 * D
CH = 512
OFF = dict(q=0, i=512, ff=1024, fb=1536, g=2048, dq=2560, dkv=2944, ga=3232, gb=4256)
LEVELS = (64, 32, 16, 8, 4, 2, 1)
STEPS = [(m, h) for m in LEVELS for h in range(HEADS)]
ORDER = ((0, 1, 2, 3), (1, 0, 3, 2))
MODS = [(l, j) for l in range(DEPTH) for j in range(12)]
MODS_EARLY = MODS[:4]
MODS_IN = (MODS[4:16], MODS[16:])
ROWS_BANKS, TURNED_BANK = (6, 7), 5
SPLIT_UNITS = ("ff", "fb", "i", "q", "g")
LATE_UNITS = ("ga0", "gb0", "ga1", "gb1", "o0", "o1")
FAR = 10000.0

SHARED = {
    "sq1": ("squared", 0), "o_sq": ("squared", 8), "dq_sq": ("squared", 12), "ckv_sq": ("squared", 15), "sq2": ("squared", 17),
    "sq1_used": ("square_used", 0), "dq_sq_used": ("square_used", 7), "ckv_sq_used": ("square_used", 9),
    "sq2_used": ("square_used", 10),
    "rs1": ("rsqrt", 0), "o_rs": ("rsqrt", 2), "mla_rs": ("rsqrt", 10), "rs2": ("rsqrt", 14),
    "h1": ("modulated", 0), "h2": ("modulated", 16), "h1_n": ("normed", 0), "h2_n": ("normed", 8),
    "h_back": ("h_lo", 8), "late_lo": ("h_lo", 16), "h_late_hi": ("h_hi", 8), "mixed_hi": ("h_hi", 16),
    "late_hi": ("unit_hi", 20), "h_late_lo": ("unit_lo", 20),
    "dq_raw": ("low_rank", 0), "ckv_raw": ("low_rank", 3), "dq_n": ("low_rank_normed", 0), "ckv_n": ("low_rank_normed", 3),
}
IN_LAYER_0 = dict(
    squared=25, square_used=17, rsqrt=16, modulated=32, normed=16, low_rank=5, low_rank_normed=5,
    f_sig=8, v_ready=4, q_ready=4, g_sig=4, g_ready=4,
    kpe_mul=2, kpe_ready=1, kpe_sw=1, uq_sw=3, kpe_in=8, k_gate=8, att_zero=2, logf=8, b_ready=8, att_in=64, exponent=56,
    decay=56, qk_ready=56, e_b=4, kd_exponent=8, kd_decay=8, kd_ready=8, qe_ready=2, kdT_ready=6, state=24, o_acc=8,
    a_ready=4, q_rot=16, q_rope=8, k_ready=8, v2_ready=4, neg_max=32, p_exp=32, p_norm=32, pT_ready=32, m_ready=32,
    mix_sig=16, mix_a=8, mix_b=8, mixed=8, z_mixed=8, score=1, scored=1, htok=8, htok_lo=8, taken=1, nb_ready=1, z_ready=1,
    h_hi=24, h_lo=40, unit_hi=44, unit_lo=28, mixed_lo=8)

VEC = {}
for _name, _rows in (("c", 8), ("c_ctx", 8), ("norm1_g", 16), ("norm2_g", 16), ("final_g", 8), ("hg_norm_g", 8),
                     ("q_norm_g", 6), ("kv_norm_g", 4), ("gamma_fwd", 8), ("gamma_bwd", 8)):
    VEC[_name] = (sum(r for _, r in VEC.values()), _rows)
NVEC = sum(r for _, r in VEC.values())
NBMOD = DEPTH * MOD // P


def first_token(l):
    return NCTX if l == DEPTH - 1 else 0


def splits_late(l):
    return first_token(l) == 0


def attention_steps(l):
    return [(qt, h) for qt in range(first_token(l) // P, TILES) for h in range(MH)]


def psum_plan():
    fixed, reserved = {}, []
    turns = [(("vec", 0), "g", "vec_read", 1), (("vec", 1), "g", "vec_read", 2)]
    turns += [(("z", k), "g", "z_loaded", k + 1) for k in range(KD)]

    def mods(some):
        for unit in some:
            m = MODS.index(unit)
            fixed[("mod", *unit)], fixed[("modT", *unit)] = ROWS_BANKS[m % 2], TURNED_BANK
            turns.extend([(("mod", *unit), "g", "mod_rows", m + 1), (("modT", *unit), "g", "mod_added", m + 1)])

    mods(MODS_EARLY)
    for l in range(DEPTH):
        tiles = range(first_token(l) // P, TILES)
        turns += [(("ssq1", l), l, "rs1", 1)]
        turns += [(("f", l, d, h), l, "f_sig", d * HEADS + h + 1) for d in range(2) for h in range(HEADS)]
        turns += [(("v", l, t), l, "v_ready", t + 1) for t in range(TILES)]
        turns += [(("q", l, h), l, "q_ready", h + 1) for h in range(HEADS)]
        turns += [(("g", l, h), l, "g_ready", h + 1) for h in range(HEADS)]
        turns += [(("dq", l, k), l, "dq_raw", k + 1) for k in range(QR // P)]
        turns += [(("ckv", l, k), l, "ckv_raw", k + 1) for k in range(KVR // P)]
        turns += [(("kpe", l, s), l, "kpe_mul", s + 1) for s in range(2)]
        mods(MODS_IN[l])
        start = len(turns)
        for d in range(2):
            turns += [(("diag", l, d, h), l, "att_in", d * 32 + h + 1) for h in range(HEADS)]
            turns += [(("lev", l, d, n), l, "att_in", d * 32 + HEADS + n + 1) for n in range(len(STEPS))]
            outs = 0
            for i, c in enumerate(ORDER[d]):
                if i < 3:
                    turns += [(("kdT", l, d, i), l, "kdT_ready", d * 3 + i + 1),
                              (("st", l, d, i), l, "state", (d * 3 + i + 1) * HEADS)]
                if c in tiles:
                    outs += 1
                    turns += [(("out", l, d, i), l, "o_acc", d * len(tiles) + outs)]
        reserved.append(range(start, len(turns)))
        turns += [(("ossq", l, h), l, "o_rs", 2 * h + 1) for h in range(HEADS)]
        turns += [(("qssq", l), l, "mla_rs", 1), (("kssq", l), l, "mla_rs", 3)]
        for h in range(MH):
            turns += [(("Q", l, h), l, "q_rot", 2 * h + 1), (("Qsw", l, h), l, "q_rot", 2 * h + 2)]
        turns += [(("K", l, h), l, "k_ready", h + 1) for h in range(MH)]
        turns += [(("V", l, t), l, "v2_ready", t + 1) for t in range(TILES)]
        nj = len(attention_steps(l))
        for j in range(nj + 3):
            if j < nj:
                turns += [(("sc", l, j), l, "p_exp", j + 1)]
            if 2 <= j < nj + 2:
                turns += [(("pT", l, j - 2), l, "pT_ready", j - 1)]
            if j >= 3:
                turns += [(("pv", l, j - 3), l, "m_ready", j - 2)]
        for m in range(KD):
            turns += [(("pa", l, m), l, "mix_a", m + 1), (("pb", l, m), l, "mix_b", m + 1),
                      (("ga", l, m), l, "mix_sig", 2 * m + 1), (("gb", l, m), l, "mix_sig", 2 * m + 2)]
        turns += [(("y", l, m), l, "z_mixed", m + 1) for m in range(KD)]
        turns += [(("ssq2", l), l, "rs2", 1)]
        turns += [(("logit", l), l, "score", 1)]
        turned = [(("hT", l, t, g), l, "htok_lo", (t - tiles[0]) * 2 + g + 1) for t in tiles for g in range(2)]
        turns += [turned[0], (("logitT", l), l, "scored", 1), *turned[1:]]
        turns += [(("rank", l), l, "nb_ready", 1)]
    turns += [(("ssqf",), "g", "rsf", 1)]
    turns += [(("fin", t, g), "g", "fin_rows", t * 2 + g + 1) for t in range(NX // P) for g in range(2)]
    bank, nth, before, last = {}, {}, {}, {}
    history = [[] for _ in range(8)]
    b = 0
    for n, (turn, *freed) in enumerate(turns):
        if turn in fixed:
            taken = fixed[turn]
        else:
            if any(n in part for part in reserved) and b >= TURNED_BANK:
                b = 0
            taken, b = b, (b + 1) % 8
        bank[turn], nth[turn] = taken, len(history[taken]) + 1
        before[turn] = history[taken][-1] if history[taken] else None
        history[taken].append(tuple(freed))
        if turn[0] == "rank":
            last[turn[1]] = [h[-1] for h in history]
    return bank, nth, before, last


PLACES = []
for _d in range(2):
    PLACES += [(("diag", _d, h), 1) for h in range(HEADS)] + [(("lev", _d, n), 1) for n in range(len(STEPS))]
    PLACES += [(("keys", _d), 8)] + [(("chunk", _d, i), 2) for i in range(3)]
TURN_PART = 4


def mod_parts(l, place):
    total, done = len(MODS_IN[l]) * KD, 0
    for name, n in PLACES:
        if first_token(l) and name[0] == "lev":
            n = 1 if name[2] % 5 < 3 else 0
        if name == place:
            return min(done, total), min(done + n, total)
        done += n
    return min(done, total), total


def mod_copied(l, place):
    return mod_parts(l, place)[1] // KD


def mod_turned(l, place):
    if place == "end":
        return len(MODS_IN[l])
    return max(0, (mod_parts(l, place)[1] - 1 - TURN_PART) // KD)


def weight_plan(a):
    units = []

    def rows(w):
        return w.rearrange("(k p) n -> p k n", p=P)

    def mods(some, s):
        return [(("mod", l, j), (s + i) % 4, rows(a["w_mod"][l, :, j * CH:(j + 1) * CH]), ("mod", l, j))
                for i, (l, j) in enumerate(some)]

    units += mods(MODS_EARLY, 0)
    for l in range(DEPTH):
        def w_in(name, width, shift=0):
            o = OFF[name] + shift
            return rows(a["w_in"][l, :, o:o + width])
        units += [
            (("ff", l), 0, w_in("ff", CH), ("f", l, 0, 3)), (("fb", l), 1, w_in("fb", CH), ("f", l, 1, 3)),
            (("i", l), 2, w_in("i", CH), ("v", l, 3)), (("q", l), 3, w_in("q", CH), ("q", l, 3)),
            (("g", l), 0, w_in("g", CH), ("g", l, 3)), (("dq", l), 1, w_in("dq", QR), ("dq", l, 2)),
            (("dkv", l), 2, w_in("dkv", KVR + ROPE), ("kpe", l, 1)), *mods(MODS_IN[l], 3),
            (("uq", l), 3, rows(a["w_uq"][l]), ("Qsw", l, 7)), (("ukv", l), 0, rows(a["w_ukv"][l]), ("V", l, 3)),
            (("pa", l), 1, rows(a["w_pa"][l]), ("pa", l, 7)), (("pb", l), 2, rows(a["w_pb"][l]), ("pb", l, 7)),
            (("ga0", l), 3, w_in("ga", CH), ("ga", l, 3)), (("gb0", l), 0, w_in("gb", CH), ("gb", l, 3)),
            (("ga1", l), 3, w_in("ga", CH, CH), ("ga", l, 7)), (("gb1", l), 0, w_in("gb", CH, CH), ("gb", l, 7)),
            (("o0", l), 1, rows(a["w_o"][l, :, 0:CH]), ("y", l, 3)), (("o1", l), 2, rows(a["w_o"][l, :, CH:D]), ("y", l, 7)),
        ]
    slot, landed, count = {}, {}, [0] * 4
    for unit, s, _, _ in units:
        count[s] += 1
        slot[unit], landed[unit] = s, 16 * count[s]
    return units, slot, landed


def bass_hybrid_transformer(nc, a, out):
    bank, nth, before, last_turns = psum_plan()
    units, slot_of, landed_at = weight_plan(a)

    with ExitStack() as ctx:
        def sb(name, shape, dt=F32):
            return ctx.enter_context(nc.sbuf_tensor(name, shape, dt))

        def twice(name, shape):
            with nc.sbuf_tensor(name, shape, F32) as plain:
                pass
            return plain, sb(f"{name}_r", shape, F32R)

        sems = {}

        def S(name, l="g"):
            name = SHARED.get(name, (name, 0))[0]
            if name in IN_LAYER_0 and l != "g":
                l = "layers"
            if (name, l) not in sems:
                sems[name, l] = ctx.enter_context(nc.semaphore(f"{name}_{l}"))
            return sems[name, l]

        def at(name, l, value):
            shared, first = SHARED.get(name, (name, 0))
            return S(name, l), value + first + (IN_LAYER_0[shared] if shared in IN_LAYER_0 and l in range(1, DEPTH) else 0)

        banks = ctx.enter_context(nc.psum_tensor("banks", [P, 8, 512], F32))
        bank_full = [ctx.enter_context(nc.semaphore(f"bank_full{b}")) for b in range(8)]
        slot_landed = [ctx.enter_context(nc.semaphore(f"slot_landed{s}")) for s in range(4)]

        ident = sb("ident_sb", [P, P])
        ones = sb("ones_sb", [P, P])
        before_m = sb("before_sb", [P, P])
        slot_no = sb("slot_no_sb", [P, P])
        masks = sb("masks_sb", [P, 2, 8, P], U8)
        rope = sb("rope_sb", [P, 2, T])
        vrows = sb("vrows", [P, 2, P])
        vecs = sb("vecs", [P, NVEC])
        bmod = sb("bmod", [P, NBMOD])
        eps = sb("eps", [P, 1])
        rbias = sb("rbias", [1, NE])
        rb = sb("rb", [P, NE])
        wr = sb("wr", [P, KD, NE])
        pair = sb("pair", [P, 3, EG, EG])
        modT = sb("modT", [P, DEPTH, 48, 2])
        gainA = sb("gainA", [P, DEPTH, 2, KD, 2])
        lb = sb("lb", [P, 2, DEPTH, HEADS])
        oml = sb("oml", [P, 2, DEPTH, HEADS])
        small = sb("small", [P, 8, 16])
        silu_c = sb("silu_c", [P, 16])

        Z = sb("Z", [P, KD, T])
        H, H_r = twice("H", [P, KD, T])
        W, W_r = twice("W", [P, 4, KD * CH])
        VG, VG_r = twice("VG", [P, 8 * T])
        V = VG[:, 0:4 * T].rearrange("p (t c) -> p t c", t=TILES)
        G = VG[:, 4 * T:].rearrange("p (h t) -> p h t", h=HEADS)
        OL, OL_r = twice("OL", [P, 10 * T])
        O = OL[:, 0:4 * T].rearrange("p (h t) -> p h t", h=HEADS)
        dq = OL[:, 4 * T:7 * T].rearrange("p (k t) -> p k t", k=3)
        ckv = OL[:, 7 * T:9 * T].rearrange("p (k t) -> p k t", k=2)
        kpe = OL[:, 9 * T:]
        RS = sb("RS", [P, T])
        SQ = sb("SQ", [P, 2, T])
        kdT = SQ[:, 0, :].rearrange("p (h t) -> p h t", h=HEADS)
        state = SQ[:, 1, :].rearrange("p (h t) -> p h t", h=HEADS)
        mx = sb("mx", [P, 4, 32])
        ebl = sb("ebl", [P, HEADS, TILES])
        uq_pad = sb("uq_pad", [P, NOPE + 3 * MH * ROPE])
        kpe_pad = sb("kpe_pad", [P, NOPE + KD * ROPE])
        uq_sw = uq_pad[:, NOPE:].rearrange("p (k h c) -> p k h c", k=3, h=MH)
        kpe_sw = kpe_pad[:, NOPE:].rearrange("p (k c) -> p k c", k=KD)
        arena, arena_r = twice("arena", [P, 6 * 2048 + 1024])

        def part(first, n, shape, **sizes):
            return arena[:, first * 2048:first * 2048 + n].rearrange(shape, **sizes)

        q = part(0, 2048, "p (h t) -> p h t", h=HEADS)
        F = [part(1 + d, 2048, "p (h t) -> p h t", h=HEADS) for d in range(2)]
        K = part(3, 2048, "p (h t) -> p h t", h=HEADS)
        Ex = part(4, 2048, "p (h t) -> p h t", h=HEADS)
        att = part(5, 2048, "p (h t) -> p h t", h=HEADS)
        QKd = part(6, 1024, "p (h t) -> p h t", h=2)
        QT = part(0, 4096, "p (h t) -> p h t", h=MH)
        KT = part(2, 4096, "p (h t) -> p h t", h=MH)
        V2 = part(4, 2048, "p (t c) -> p t c", t=TILES)
        PR = part(5, 1536, "p (r t) -> p r t", r=3)
        PT = arena[:, 5 * 2048 + 1536:5 * 2048 + 2560].rearrange("p (r t) -> p r t", r=2)
        tmpQ = SQ
        MT = V
        mix = part(0, 4096, "p (k t) -> p k t", k=KD)
        mixT = part(4, 2048, "p (r t) -> p r t", r=4)
        H_hi = [arena_r[:, 5 * 2048 + k * T:5 * 2048 + (k + 1) * T] for k in range(6)] + \
               [OL_r[:, k * T:(k + 1) * T] for k in range(2)]
        unit_hi = [arena_r[:, 3 * 2048:5 * 2048], OL_r[:, 2 * T:10 * T]]

        H_late_hi = [VG_r[:, (4 + k) * T:(5 + k) * T] for k in range(4)] + [OL_r[:, (4 + k) * T:(5 + k) * T] for k in range(4)]
        late_hi = [[arena_r[:, 2 * 2048 + i * 1024:2 * 2048 + (i + 1) * 1024] for i in range(CHUNKS)],
                   [arena_r[:, 5 * 2048 + i * 1024:5 * 2048 + (i + 1) * 1024] for i in range(CHUNKS - 1)] + [OL_r[:, 8 * T:10 * T]]]
        mix_lo = arena_r[:, 0:4096].rearrange("p (k t) -> p k t", k=KD)

        def piece(first, n):
            return arena[:, first:first + n]

        def piece_r(first, n):
            return arena_r[:, first:first + n]

        htok_hi = piece_r(4096, TILES * D).rearrange("p (t n) -> p t n", t=TILES)
        htok_lo = OL_r[:, 0:TILES * D].rearrange("p (t n) -> p t n", t=TILES)
        sel = piece_r(0, 512).rearrange("p (t s) -> p t s", t=TILES)
        selw = piece(512, 512).rearrange("p (t s) -> p t s", t=TILES)
        selT = piece_r(1024, 512)
        selw_copy = piece(1536, 512)
        gate_t = piece(2048, 512)
        hidden = piece(2560, 512)
        hidT_hi, hidT_lo = piece_r(3072, 512), piece_r(3584, 512)
        xs_tok = piece(8192, D)
        xsT_hi, xsT_lo = (piece_r(i, D).rearrange("p (k s) -> p k s", k=KD) for i in (9216, 10240))
        yd_hi, yd_lo = piece_r(11264, D), piece_r(12288, D)
        scoreT = piece(12288, 512)
        compared = piece(8192, 3 * 512).rearrange("p (a n) -> p a n", a=3)
        rt = piece(11264, 1024).rearrange("p (a t e) -> p a t e", a=16, t=TILES)
        ROUNDS = TILES
        pos, gw = (RS[:, i * 256:(i + 1) * 256].rearrange("p (t e) -> p t e", t=TILES) for i in range(2))
        wslot = sb("wslot", [P, 1])
        w_hi = {"gate": H_r[:, :, :].rearrange("p k t -> p (k t)"), "up": W_r[:, 3, :], "down": VG_r[:, :]}
        mod_row = RS
        masks_in = O[:, :, :].rearrange("p h t -> p (h t)").bitcast(I32)
        ztok = H[:, :, :].rearrange("p k t -> p (k t)").rearrange("p (t n) -> p t n", t=TILES)
        nbi = sb("nbi", [P, 1], I32)
        cnt = sb("cnt", [P, 8])

        def slot(unit, cols):
            return W[:, slot_of[unit], 0:KD * CH // cols * cols].rearrange("p (k n) -> p k n", n=cols)

        def read(eng, turn):
            eng.wait_ge(bank_full[bank[turn]], nth[turn])
            return banks[:, bank[turn], :]

        def vec(name):
            first, n = VEC[name]
            return vecs[:, first:first + n]

        def Nx(l):
            return slice(first_token(l), T)

        block = ctx.enter_context(nc.Block())

        @block.sync
        def _(sp):
            for t in range(2):
                sp.dma_start(ztok[:, t, :], a["ctx"][0, t * P:(t + 1) * P, :]).then_inc(S("x_in"), 16)
                sp.dma_start(ztok[:, 2 + t, :], a["x"][0, t * P:(t + 1) * P, :]).then_inc(S("x_in"), 16)
            for dst, src in ((ident, "k_ident"), (ones, "k_ones"), (before_m, "k_before"), (slot_no, "k_slot"),
                             (masks_in, "k_masks"), (rope, "k_rope"),
                             (pair, "k_pair")):
                sp.dma_start(dst[tuple(slice(None) for _ in dst.shape)], a[src]).then_inc(S("consts"), 16)
            for name, (first, n) in VEC.items():
                src = a[name]
                if len(src.shape) == 2:
                    src = src.rearrange("a n -> (a n)")
                sp.dma_start(vrows[first:first + n, 0, :], src.rearrange("(r p) -> r p", p=P)).then_inc(S("consts"), 16)
            sp.dma_start(vrows[0:NBMOD, 1, :], a["b_mod"].rearrange("l (r p) -> (l r) p", p=P)).then_inc(S("consts"), 16)
            sp.dma_start(rbias[:], a["router_bias"].rearrange("(o n) -> o n", o=1)).then_inc(S("consts"), 16)
            sp.dma_start(wr[:], a["w_router"].rearrange("(k p) n -> p k n", p=P)).then_inc(S("consts"), 16)

            previous = [None] * 4

            def load(n, l=0, nb=None):
                unit, s, src, last = units[n]
                if previous[s] in UNITS:
                    sp.wait_ge(*at(f"{previous[s]}_used", l - 1, nb * NE))
                elif previous[s]:
                    sp.wait_ge(bank_full[bank[previous[s]]], nth[previous[s]])
                previous[s] = last
                k, cols = src.shape[1], src.shape[2]
                sp.dma_start(W[:, s, 0:k * cols].rearrange("p (k n) -> p k n", n=cols), src).then_inc(slot_landed[s], 16)

            n = 0
            for _ in MODS_EARLY:
                load(n)
                n += 1
            nb = None
            for l in range(DEPTH):
                for _ in range(17 + len(MODS_IN[l])):
                    load(n, l, nb)
                    n += 1
                for s in range(4):
                    sp.wait_ge(bank_full[bank[previous[s]]], nth[previous[s]])

                def load_expert(e, done):
                    for s, (w, name) in enumerate((("w_gate_e", "gate"), ("w_up_e", "up"), ("w_down_e", "down"))):
                        if done is not None:
                            sp.wait_ge(*at(f"{name}_used", l, done))
                        cols = CH if s < 2 else D
                        src = a[w][l, bass.ds(e, 1)].rearrange("o (k p) n -> p (o k) n", p=P)
                        sp.dma_start(W[:, s, :].rearrange("p (k n) -> p k n", n=cols), src) \
                          .then_inc(S(f"{name}_in", l), 16)

                load_expert(0, None)
                sp.wait_ge(*at("nb_ready", l, 1))
                nb = sp.value_load(nbi[0:1, 0:1], min_val=0, max_val=3) + 1
                with sp.Fori(0, nb * NE - 1) as it:
                    load_expert((it + 1) % NE, it + 1)
                previous = [*UNITS, "up"]
            sp.wait_ge(*at("fin_rows", "g", 4))
            for t in range(NX // P):
                sp.dma_start(out[0, t * P:(t + 1) * P, :], ztok[:, t, :]).then_inc(S("out"), 16)
            sp.wait_ge(*at("out", "g", 16 * (NX // P)))

        N_CONSTS = 16 * (7 + len(VEC) + 3)

        @block.tensor
        def _(pe):
            mm = nc.tensor.matmul

            def claim(turn):
                if before[turn]:
                    l, name, value = before[turn]
                    pe.wait_ge(*at(name, l, value))
                return banks[:, bank[turn], :]

            def full(ins, turn):
                ins.then_inc(bank_full[bank[turn]], 1)

            def landed(unit):
                pe.wait_ge(slot_landed[slot_of[unit]], landed_at[unit])

            pe.wait_ge(*at("consts", "g", N_CONSTS))
            for i, n in ((0, NVEC), (1, NBMOD)):
                o = claim(("vec", i))
                x = nc.tensor.transpose(o[:, 0:n], vrows[0:n, i, :], ident[0:n, 0:n])
                if i == 0:
                    x = mm(o[:, 256:256 + NE], ones[0:1, :], rbias[0:1, :], start=True, stop=True)
                full(x, ("vec", i))
            pe.wait_ge(*at("x_in", "g", 64))
            for k in range(KD):
                o = claim(("z", k))
                for t in range(TILES):
                    x = nc.tensor.transpose(o[:, t * P:(t + 1) * P], ztok[:, t, k * P:(k + 1) * P], ident[:, :])
                full(x, ("z", k))
            pe.wait_ge(*at("silu_c", "g", 1))
            sc = silu_c[:, :].rearrange("p (v k) -> p k v", v=2)

            def mod_product(unit, k):
                u = ("mod", *unit)
                if k == 0:
                    claim(u)
                    landed(u)
                x = mm(banks[0:2, bank[u], :], sc[:, k, :], slot(u, CH)[:, k, :], start=(k == 0), stop=(k == KD - 1))
                if k == KD - 1:
                    full(x, u)

            def mod_turn(unit):
                o = claim(("modT", *unit))
                pe.wait_ge(*at("mod_rows", "g", MODS.index(unit) + 1))
                for i in range(4):
                    x = nc.tensor.transpose(o[:, 2 * i:2 * i + 2], mod_row[0:2, i * P:(i + 1) * P], ident[0:2, 0:2])
                full(x, ("modT", *unit))

            def mod_at(l, place):
                some = MODS_IN[l]
                for part in range(*mod_parts(l, place)):
                    mod_product(some[part // KD], part % KD)
                    if part % KD == TURN_PART and part > KD:
                        mod_turn(some[part // KD - 1])
                if place == "end":
                    mod_turn(some[-1])

            for i, unit in enumerate(MODS_EARLY):
                for k in range(KD):
                    mod_product(unit, k)
                if i:
                    mod_turn(MODS_EARLY[i - 1])
            mod_turn(MODS_EARLY[-1])

            def sum_squares(turn, l, sem, cols, tiles=KD):
                o = claim(turn)
                for k in range(tiles):
                    pe.wait_ge(*at(sem, l, k + 1))
                    x = mm(o[:, cols], ones[:, :], SQ[:, k % 2, cols], start=(k == 0), stop=(k == tiles - 1))
                    if k < tiles - 1:
                        x.then_inc(S(sem + "_used", l), 1)
                full(x, turn)

            def project(turn, unit, width, c0, m, cols, kt=KD, rhs=None, ready=None):
                o = claim(turn)
                landed(unit)
                w = slot(unit, width)
                rhs = H if rhs is None else rhs
                for k in range(kt):
                    if ready:
                        pe.wait_ge(*at(ready, l, k + 1))
                    x = mm(o[0:m, cols], w[:, k, c0:c0 + m], rhs[:, k, cols], start=(k == 0), stop=(k == kt - 1))
                full(x, turn)

            def split_products(turn, o, operands):
                for k, passes in enumerate(operands):
                    for i, (stationary, moving) in enumerate(passes):
                        x = mm(o, stationary, moving, start=(k == 0 and i == 0), stop=(k == KD - 1 and i == 2))
                full(x, turn)

            def split_weights(name, k, c):
                hi = unit_hi[SPLIT_UNITS.index(name) % 2].rearrange("p (k n) -> p k n", n=CH)
                lo = W_r[:, slot_of[name, l], :].rearrange("p (k n) -> p k n", n=CH)
                return hi[:, k, c], lo[:, k, c]

            def split_project(turn, name, c, cols):
                def passes(k):
                    hi, lo = split_weights(name, k, c)
                    return (lo, H_hi[k][:, cols]), (hi, H_hi[k][:, cols]), (hi, H_r[:, k, cols])
                o = claim(turn)
                pe.wait_ge(*at("unit_lo", l, CHUNKS * (SPLIT_UNITS.index(name) + 1)))
                split_products(turn, o[:, cols], [passes(k) for k in range(KD)])

            def late_weights(name, k, c):
                hi = late_hi[LATE_UNITS.index(name) % 2][k // 2][:, k % 2 * CH:(k % 2 + 1) * CH]
                lo = W_r[:, slot_of[name, l], k * CH:(k + 1) * CH]
                return hi[:, c], lo[:, c]

            def late_project(turn, name, c, cols, x_hi, x_lo):
                def passes(k):
                    hi, lo = late_weights(name, k, c)
                    return (lo, x_hi[k][:, cols]), (hi, x_hi[k][:, cols]), (hi, x_lo[:, k, cols])
                o = claim(turn)
                pe.wait_ge(*at("late_lo", l, CHUNKS * (LATE_UNITS.index(name) + 1)))
                split_products(turn, o[:, cols], [passes(k) for k in range(KD)])

            for l in range(DEPTH):
                every, some = slice(0, T), Nx(l)
                tiles = range(first_token(l) // P, TILES)
                if l:
                    pe.wait_ge(*at("z_ready", l - 1, 1))
                sum_squares(("ssq1", l), l, "sq1", every)
                for h in range(HEADS):
                    claim(("f", l, 0, h))
                pe.wait_ge(*at("unit_lo", l, CHUNKS))
                for k in range(KD):
                    pe.wait_ge(*at("h_hi", l, k + 1))
                    pe.wait_ge(*at("h_lo", l, k + 1))
                    for h in range(HEADS):
                        turn = ("f", l, 0, h)
                        hi, lo = split_weights("ff", k, slice(h * P, (h + 1) * P))
                        o = banks[:, bank[turn], :]
                        mm(o, lo, H_hi[k], start=(k == 0), stop=False)
                        mm(o, hi, H_hi[k], start=False, stop=False)
                        x = mm(o, hi, H_r[:, k, :], start=False, stop=(k == KD - 1))
                        if k == KD - 1:
                            full(x, turn)
                for h in range(HEADS):
                    split_project(("f", l, 1, h), "fb", slice(h * P, (h + 1) * P), every)
                for t in range(TILES):
                    def passes(k):
                        tokens = slice(t * P, (t + 1) * P)
                        hi, lo = split_weights("i", k, slice(0, CH))
                        return (H_hi[k][:, tokens], lo), (H_hi[k][:, tokens], hi), (H_r[:, k, tokens], hi)
                    o = claim(("v", l, t))
                    pe.wait_ge(*at("unit_lo", l, CHUNKS * (SPLIT_UNITS.index("i") + 1)))
                    split_products(("v", l, t), o, [passes(k) for k in range(KD)])
                for name in ("q", "g"):
                    for h in range(HEADS):
                        split_project((name, l, h), name, slice(h * P, (h + 1) * P), some)
                for k in range(3):
                    project(("dq", l, k), ("dq", l), QR, k * P, P, some, ready="h_back" if k == 0 else None)
                for k in range(2):
                    project(("ckv", l, k), ("dkv", l), KVR + ROPE, k * P, P, every)
                project(("kpe", l, 0), ("dkv", l), KVR + ROPE, KVR - NOPE, QK, every)
                o = claim(("kpe", l, 1))
                pe.wait_ge(*at("kpe_sw", l, 1))
                for k in range(KD):
                    x = mm(o[0:QK, :], kpe_pad[:, k * ROPE:k * ROPE + QK], H[:, k, :],
                           start=(k == 0), stop=(k == KD - 1))
                full(x, ("kpe", l, 1))

                for d in range(2):
                    pe.wait_ge(*at("q_ready", l, HEADS))
                    for h in range(HEADS):
                        mod_at(l, ("diag", d, h))
                        o = claim(("diag", l, d, h))
                        pe.wait_ge(*at("k_gate", l, d * HEADS + h + 1))
                        for c in tiles:
                            s = slice(c * P, (c + 1) * P)
                            x = mm(o[:, s], K[:, h, s], q[:, h, s], start=True, stop=True)
                        full(x, ("diag", l, d, h))
                    for n in range(len(STEPS)):
                        mod_at(l, ("lev", d, n))
                        o = claim(("lev", l, d, n))
                        pe.wait_ge(*at("qk_ready", l, d * len(STEPS) + n + 1))
                        for c in tiles:
                            s = slice(c * P, (c + 1) * P)
                            x = mm(o[:, s], QKd[:, n % 2, s], QKd[:, n % 2, s], start=True, stop=True)
                        full(x, ("lev", l, d, n))
                    mod_at(l, ("keys", d))
                    for i, c in enumerate(ORDER[d]):
                        s = slice(c * P, (c + 1) * P)
                        if i < 3:
                            o = claim(("kdT", l, d, i))
                            pe.wait_ge(*at("kd_ready", l, (d + 1) * HEADS))
                            for h in range(HEADS):
                                x = nc.tensor.transpose(o[:, h * P:(h + 1) * P], K[:, h, s], ident[:, :])
                            full(x, ("kdT", l, d, i))
                            o = claim(("st", l, d, i))
                            pe.wait_ge(*at("kdT_ready", l, d * 3 + i + 1))
                            pe.wait_ge(*at("v_ready", l, TILES))
                            for h in range(HEADS):
                                x = mm(o[:, h * P:(h + 1) * P], kdT[:, h, :], V[:, c, h * P:(h + 1) * P], start=True, stop=True)
                            full(x, ("st", l, d, i))
                            mod_at(l, ("chunk", d, i))
                        if c in tiles:
                            o = claim(("out", l, d, i))
                            pe.wait_ge(*at("att_in", l, d * 32 + 32))
                            pe.wait_ge(*at("qe_ready", l, d + 1))
                            if i:
                                pe.wait_ge(*at("state", l, (d * 3 + i) * HEADS))
                            for h in range(HEADS):
                                hp = slice(h * P, (h + 1) * P)
                                x = mm(o[:, hp], V[:, c, hp], att[:, h, s], start=True, stop=(i == 0))
                                if i:
                                    x = mm(o[:, hp], state[:, h, :], Ex[:, h, s], start=False, stop=True)
                            full(x, ("out", l, d, i))
                mod_at(l, "end")
                for h in range(HEADS):
                    o = claim(("ossq", l, h))
                    pe.wait_ge(*at("o_sq", l, h + 1))
                    full(mm(o[:, some], ones[:, :], SQ[:, h % 2, some], start=True, stop=True), ("ossq", l, h))

                sum_squares(("qssq", l), l, "dq_sq", some, 3)
                sum_squares(("kssq", l), l, "ckv_sq", every, 2)
                pe.wait_ge(*at("dq_n", l, 3))
                pe.wait_ge(*at("uq_sw", l, 3))
                for h in range(MH):
                    project(("Q", l, h), ("uq", l), MH * QK, h * QK, QK, some, 3, dq)
                    o = claim(("Qsw", l, h))
                    for k in range(3):
                        x = mm(o[0:QK, some], uq_pad[:, (k * MH + h) * ROPE:(k * MH + h) * ROPE + QK], dq[:, k, some],
                               start=(k == 0), stop=(k == 2))
                    full(x, ("Qsw", l, h))
                pe.wait_ge(*at("ckv_n", l, 2))
                for h in range(MH):
                    project(("K", l, h), ("ukv", l), MH * P, h * P, NOPE, every, 2, ckv)
                for t in range(TILES):
                    o = claim(("V", l, t))
                    w = slot(("ukv", l), MH * P)
                    for k in range(2):
                        x = mm(o[:, :].rearrange("p (h c) -> p h c", h=MH), ckv[:, k, t * P:(t + 1) * P],
                               w[:, k, :].rearrange("p (h c) -> p h c", h=MH)[:, :, NOPE:P],
                               start=(k == 0), stop=(k == 1))
                    full(x, ("V", l, t))
                steps = attention_steps(l)
                pe.wait_ge(*at("q_rope", l, MH))
                pe.wait_ge(*at("k_ready", l, MH))
                pe.wait_ge(*at("kpe_in", l, MH))
                for j in range(len(steps) + 3):
                    if j < len(steps):
                        qt, h = steps[j]
                        keys = NCTX if qt < 2 else T
                        o = claim(("sc", l, j))
                        full(mm(o[:, 0:keys], QT[0:QK, h, qt * P:(qt + 1) * P], KT[0:QK, h, 0:keys],
                                start=True, stop=True), ("sc", l, j))
                    if 2 <= j < len(steps) + 2:
                        i = j - 2
                        qt, h = steps[i]
                        o = claim(("pT", l, i))
                        pe.wait_ge(*at("p_norm", l, i + 1))
                        for k in range(2 if qt < 2 else 4):
                            x = nc.tensor.transpose(o[:, k * P:(k + 1) * P], PR[:, i % 3, k * P:(k + 1) * P], ident[:, :])
                        full(x, ("pT", l, i))
                    if j >= 3:
                        i = j - 3
                        qt, h = steps[i]
                        o = claim(("pv", l, i))
                        pe.wait_ge(*at("pT_ready", l, i + 1))
                        pe.wait_ge(*at("v2_ready", l, TILES))
                        n = 2 if qt < 2 else 4
                        for k in range(n):
                            x = mm(o[:, 0:P], V2[:, k, h // 2 * P:(h // 2 + 1) * P], PT[:, i % 2, k * P:(k + 1) * P],
                                   start=(k == 0), stop=(k == n - 1))
                        full(x, ("pv", l, i))

                pe.wait_ge(*at("a_ready", l, HEADS))
                pe.wait_ge(*at("m_ready", l, len(steps)))
                if splits_late(l):
                    pe.wait_ge(*at("h_late_lo", l, KD))
                for m in range(KD):
                    c0 = m % 4 * P
                    project(("pa", l, m), ("pa", l), D, m * P, P, some, 4, O)
                    project(("pb", l, m), ("pb", l), D, m * P, P, some, 4, MT)
                    for g in ("ga", "gb"):
                        if splits_late(l):
                            late_project((g, l, m), f"{g}{m // 4}", slice(c0, c0 + P), some, H_late_hi, H_r)
                        else:
                            project((g, l, m), (f"{g}{m // 4}", l), CH, c0, P, some)
                if splits_late(l):
                    for m in range(4):
                        claim(("y", l, m))
                    pe.wait_ge(*at("late_lo", l, CHUNKS * 5))
                    for k in range(KD):
                        pe.wait_ge(*at("mixed_hi", l, k + 1))
                        pe.wait_ge(*at("mixed_lo", l, k + 1))
                        for m in range(4):
                            turn = ("y", l, m)
                            hi, lo = late_weights("o0", k, slice(m * P, (m + 1) * P))
                            o = banks[:, bank[turn], some]
                            mm(o, lo, H_late_hi[k][:, some], start=(k == 0), stop=False)
                            mm(o, hi, H_late_hi[k][:, some], start=False, stop=False)
                            x = mm(o, hi, mix_lo[:, k, some], start=False, stop=(k == KD - 1))
                            if k == KD - 1:
                                full(x, turn)
                    for m in range(4, KD):
                        late_project(("y", l, m), "o1", slice((m - 4) * P, (m - 3) * P), some, H_late_hi, mix_lo)
                else:
                    for m in range(KD):
                        project(("y", l, m), (f"o{m // 4}", l), CH, m % 4 * P, P, some, KD, mix, ready="mixed")
                sum_squares(("ssq2", l), l, "sq2", some)
                halves = (0, 1) if l == 0 else (1,)
                o = claim(("logit", l))
                for k in range(KD):
                    pe.wait_ge(*at("h2", l, (k + 1) * len(halves)))
                    x = mm(o[0:NE, some], wr[:, k, :], H[:, k, some], start=(k == 0), stop=(k == KD - 1))
                full(x, ("logit", l))

                def turn_rows(t, g):
                    o = claim(("hT", l, t, g))
                    for k in range(4):
                        x = nc.tensor.transpose(o[:, k * P:(k + 1) * P], H[:, 4 * g + k, t * P:(t + 1) * P], ident[:, :])
                    full(x, ("hT", l, t, g))

                turn_rows(tiles[0], 0)
                o = claim(("logitT", l))
                pe.wait_ge(*at("score", l, 1))
                for i, t in enumerate(tiles):
                    x = nc.tensor.transpose(o[:, i * NE:(i + 1) * NE], scoreT[0:NE, t * P:(t + 1) * P], ident[0:NE, 0:NE])
                full(x, ("logitT", l))
                for t in tiles:
                    for g in range(2):
                        if (t, g) != (tiles[0], 0):
                            turn_rows(t, g)
                o = claim(("rank", l))
                pe.wait_ge(*at("taken", l, 1))
                n = len(tiles)
                for i in range(n):
                    for j in range(i + 1):
                        mm(o[:, i * NE:(i + 1) * NE], (before_m if j == i else ones)[:, :], rt[:, 0, j, :],
                           start=(j == 0), stop=(j == i))
                for j in range(n):
                    x = mm(o[:, n * NE:(n + 1) * NE], ones[:, :], rt[:, 0, j, :], start=(j == 0), stop=(j == n - 1))
                full(x, ("rank", l))

                for ll, name, value in last_turns[l]:
                    pe.wait_ge(*at(name, ll, value))
                pe.wait_ge(*at("htok", l, 2 * n))
                pe.wait_ge(*at("htok_lo", l, 2 * n))
                nb = pe.value_load(nbi[0:1, 0:1], min_val=0, max_val=3) + 1

                def gather(it):
                    pe.wait_ge(*at("sel", l, it + 1))
                    for half in range(2):
                        c = slice(half * 512, (half + 1) * 512)
                        for j in range(n):
                            mm(banks[:, half, :], sel[:, j, :], htok_hi[:, j, c], start=(j == 0), stop=False)
                            x = mm(banks[:, half, :], sel[:, j, :], htok_lo[:, j, c], start=False, stop=(j == n - 1))
                    x.then_inc(S("gathered", l), 1)

                def turn_gathered(it):
                    pe.wait_ge(*at("xs_tok", l, 2 * it + 2))
                    for k in range(KD):
                        x = nc.tensor.transpose(banks[:, 2 + k // 4, k % 4 * P:(k % 4 + 1) * P],
                                                xs_tok[:, k * P:(k + 1) * P], ident[:, :])
                    x.then_inc(S("xsT_full", l), 1)

                def product(o, a_hi, a_lo, w_unit, s, kt, col):
                    cols = KD * CH // kt
                    hi = w_hi[w_unit].rearrange("p (k n) -> p k n", n=cols)
                    lo = W_r[:, s, :].rearrange("p (k n) -> p k n", n=cols)
                    for k in range(kt):
                        mm(o, a_hi(k), lo[:, k, col], start=(k == 0), stop=False)
                        mm(o, a_hi(k), hi[:, k, col], start=False, stop=False)
                        x = mm(o, a_lo(k), hi[:, k, col], start=False, stop=(k == kt - 1))
                    return x

                def split(it, name):
                    pe.wait_ge(*at("w_lo", l, it * DVE_UNTIL["down"] + DVE_UNTIL[name]))
                    pe.wait_ge(*at("w_lo_pool", l, it * POOL_UNTIL["down"] + POOL_UNTIL[name]))

                def take_in(it, name):
                    pe.wait_ge(*at("xh", l, 2 * it + 2))
                    pe.wait_ge(*at("xl", l, 2 * it + 2))
                    split(it, name)
                    i = UNITS.index(name)
                    product(banks[:, 4 + i, :], lambda k: xsT_hi[:, k, :], lambda k: xsT_lo[:, k, :], name, i, KD,
                            slice(0, CH)).then_inc(S(f"{name}_used", l), 1)

                def down(it, half):
                    product(banks[:, 4 + half, :], lambda f: hidT_hi[:, f * P:(f + 1) * P], lambda f: hidT_lo[:, f * P:(f + 1) * P],
                            "down", 2, 4, slice(half * CH, (half + 1) * CH)) \
                        .then_inc(S(("y0_full", "down_used")[half], l), 1)

                def combine(it, tiles):
                    for k in tiles:
                        if k >= 4:
                            earlier = max(i for i in range(4) if COMBINE[i] == COMBINE[k])
                            pe.wait_ge(*at("z_added", l, it * KD + earlier + 1))
                        o = banks[:, COMBINE[k], 0:n * P]
                        mm(o, yd_hi[:, k * P:(k + 1) * P], selT[:, 0:n * P], start=True, stop=False)
                        x = mm(o, yd_lo[:, k * P:(k + 1) * P], selT[:, 0:n * P], start=False, stop=True)
                        x.then_inc(S("combined", l), 1)

                def give_out(it, more):
                    pe.wait_ge(*at("selw", l, it + 1))
                    for j in range(n):
                        x = nc.tensor.transpose(banks[:, 2, j * P:(j + 1) * P], selw[:, j, :], ident[:, :])
                    x.then_inc(S("selT_full", l), 1)
                    pe.wait_ge(*at("hidden", l, it + 1))
                    for f in range(4):
                        x = nc.tensor.transpose(banks[:, 3, f * P:(f + 1) * P], hidden[:, f * P:(f + 1) * P], ident[:, :])
                    x.then_inc(S("hidT_full", l), 1)
                    if more:
                        gather(it + 1)
                    pe.wait_ge(*at("hidT", l, it + 1))
                    pe.wait_ge(*at("hidT_lo", l, it + 1))
                    split(it, "down")
                    down(it, 0)
                    if more:
                        turn_gathered(it + 1)
                    down(it, 1)
                    if more:
                        pe.wait_ge(*at("yl", l, it * 2 + 1))
                        take_in(it + 1, "gate")
                    pe.wait_ge(*at("selT", l, it + 1))
                    pe.wait_ge(*at("yl", l, it * 2 + 2))
                    combine(it, range(4))
                    if more:
                        take_in(it + 1, "up")
                    combine(it, range(4, KD))

                gather(0)
                turn_gathered(0)
                take_in(0, "gate")
                take_in(0, "up")
                with pe.Fori(0, nb * NE - 1) as it:
                    give_out(it, True)
                give_out(nb * NE - 1, False)

            pe.wait_ge(*at("z_ready", DEPTH - 1, 1))
            sum_squares(("ssqf",), "g", "sqf", slice(NCTX, T))
            pe.wait_ge(*at("zf", "g", KD))
            for t in range(NX // P):
                for g in range(2):
                    o = claim(("fin", t, g))
                    for k in range(4):
                        s = slice(NCTX + t * P, NCTX + (t + 1) * P)
                        x = nc.tensor.transpose(o[:, k * P:(k + 1) * P], Z[:, 4 * g + k, s], ident[:, :])
                    full(x, ("fin", t, g))

        @block.scalar
        def _(act):
            fn = nc.scalar.activation

            def squares(src, l, sem, cols, tiles=KD):
                for k in range(tiles):
                    if k >= 2:
                        act.wait_ge(*at(sem + "_used", l, k - 1))
                    fn(SQ[:, k % 2, cols], src[:, k, cols], ACT.Square).then_inc(S(sem, l), 1)

            def rsqrt(dst, turn, l, sem, n, cols, first=0):
                o = read(act, turn)
                fn(dst, o[:, cols], ACT.Ln, bias=eps[:, 0:1], scale=1.0 / n).then_inc(S(sem, l), 1)
                act.wait_ge(*at(sem, l, first + 1))
                fn(dst, dst, ACT.Exp, scale=-0.5).then_inc(S(sem, l), 1)

            nc.scalar.preload_act_table_set("natural_log_exp_and_others")
            act.wait_ge(*at("vec_read", "g", 2))
            fn(silu_c[:, :], vecs[:, 0:16], ACT.Exp, scale=-1.0).then_inc(S("c_exp"), 1)
            act.wait_ge(*at("gam_in", "g", 1))
            fn(small[:, 3, :], small[:, 3, :], ACT.Exp).then_inc(S("gam_exp"), 1)

            def take_mod(unit):
                m = MODS.index(unit)
                o = read(act, ("mod", *unit))
                if m:
                    read(act, ("modT", *MODS[m - 1]))
                fn(mod_row[0:2, :], o[0:2, :], ACT.Copy).then_inc(S("mod_rows"), 1)

            for unit in MODS_EARLY:
                take_mod(unit)
            copied = [0] * DEPTH

            def mods_until(l, place):
                for unit in MODS_IN[l][copied[l]:mod_copied(l, place)]:
                    take_mod(unit)
                copied[l] = mod_copied(l, place)


            def modulate(l, sem, n_norm, vecs_, tiles=range(KD)):
                for k in tiles:
                    act.wait_ge(*at(sem + "_n", l, k + 1))
                    for v in vecs_:
                        s = slice(v * NCTX, (v + 1) * NCTX)
                        fn(H[:, k, s], H[:, k, s], ACT.Identity, bias=modT[:, l, n_norm * 24 + k, v:v + 1],
                           scale=gainA[:, l, n_norm, k, v:v + 1]).then_inc(S(sem, l), 1)

            for l in range(DEPTH):
                every, some = slice(0, T), Nx(l)
                tiles = range(first_token(l) // P, TILES)
                nc.scalar.preload_act_table_set("natural_log_exp_and_others")

                def round_unit(name):
                    act.wait_ge(slot_landed[slot_of[name, l]], landed_at[name, l])
                    for i in range(CHUNKS):
                        c = slice(i * 1024, (i + 1) * 1024)
                        fn(unit_hi[SPLIT_UNITS.index(name) % 2][:, c], W[:, slot_of[name, l], c], ACT.Copy) \
                            .then_inc(S("unit_hi", l), 1)

                round_unit("ff")
                if l == 0:
                    act.wait_ge(*at("z_loaded", "g", KD))
                    act.wait_ge(*at("eps", "g", 1))
                else:
                    act.wait_ge(*at("z_ready", l - 1, 1))
                squares(Z, l, "sq1", every)
                read(act, ("modT", *(MODS_EARLY if l == 0 else MODS_IN[l - 1])[-1]))
                rsqrt(RS[:, :], ("ssq1", l), l, "rs1", D, every)
                act.wait_ge(*at("gains", "g", 2 * l + 1))
                for k in range(KD + 1):
                    if k < KD:
                        modulate(l, "h1", 0, (0, 1), [k])
                    if k:
                        act.wait_ge(*at("h1", l, 2 * k))
                        fn(H_hi[k - 1], H[:, k - 1, :], ACT.Copy).then_inc(S("h_hi", l), 1)
                nc.scalar.preload_act_table_set("sigmoid_and_others")
                round_unit("fb")
                for d in range(2):
                    for h in range(HEADS):
                        o = read(act, ("f", l, d, h))
                        fn(F[d][:, h, :], o, ACT.Sigmoid).then_inc(S("f_sig", l), 1)
                    round_unit(("i", "q")[d])
                read(act, ("v", l, TILES - 1))
                round_unit("g")
                for h in range(HEADS):
                    o = read(act, ("q", l, h))
                    fn(q[:, h, some], o[:, some], ACT.Copy).then_inc(S("q_ready", l), 1)
                for h in range(HEADS):
                    o = read(act, ("g", l, h))
                    fn(G[:, h, some], o[:, some], ACT.Sigmoid).then_inc(S("g_sig", l), 1)
                nc.scalar.preload_act_table_set("natural_log_exp_and_others")
                for k in range(3):
                    o = read(act, ("dq", l, k))
                    fn(dq[:, k, some], o[:, some], ACT.Copy).then_inc(S("dq_raw", l), 1)
                for k in range(2):
                    o = read(act, ("ckv", l, k))
                    fn(ckv[:, k, :], o, ACT.Copy).then_inc(S("ckv_raw", l), 1)
                for d in range(2):
                    for h in range(HEADS):
                        act.wait_ge(*at("k_gate", l, d * HEADS + h + 1))
                        fn(F[d][:, h, :], F[d][:, h, :], ACT.Ln).then_inc(S("logf", l), 1)
                    for n, (m, h) in enumerate(STEPS):
                        act.wait_ge(*at("exponent", l, d * len(STEPS) + n + 1))
                        v = Ex[:, n % 4, some].rearrange("p (b s m) -> p b s m", s=2, m=m)
                        qs = 1 - d
                        fn(v[:, :, 1 - qs, :], v[:, :, 1 - qs, :], ACT.Exp, scale=-1.0)
                        fn(v[:, :, qs, :], v[:, :, qs, :], ACT.Exp).then_inc(S("decay", l), 1)
                        if n >= 3:
                            mods_until(l, ("lev", d, n - 3))
                    act.wait_ge(*at("qk_ready", l, (d + 1) * len(STEPS)))
                    fn(Ex[:, :, some], F[d][:, :, some], ACT.Exp).then_inc(S("e_b", l), 1)
                    edge = P - 1 if d == 0 else 0
                    fn(ebl[:, :, :], F[d].rearrange("p h (c t) -> p h c t", t=P)[:, :, :, edge], ACT.Exp).then_inc(S("e_b", l), 1)
                    mods_until(l, ("lev", d, len(STEPS) - 1))
                    for h in range(HEADS):
                        act.wait_ge(*at("kd_exponent", l, d * HEADS + h + 1))
                        fn(QKd[:, h % 2, :], QKd[:, h % 2, :], ACT.Exp, scale=-1.0).then_inc(S("kd_decay", l), 1)
                    mods_until(l, ("keys", d))
                    for i in range(3):
                        o = read(act, ("kdT", l, d, i))
                        if i:
                            read(act, ("st", l, d, i - 1))
                        elif d:
                            read(act, ("st", l, 0, 2))
                        fn(kdT[:, :, :].rearrange("p h t -> p (h t)"), o, ACT.Copy).then_inc(S("kdT_ready", l), 1)
                        if i:
                            mods_until(l, ("chunk", d, i - 1))
                    mods_until(l, ("chunk", d, 2))
                mods_until(l, "end")
                act.wait_ge(*at("o_acc", l, 2 * len(tiles)))
                for h in range(HEADS):
                    if h >= 2:
                        read(act, ("ossq", l, h - 2))
                    fn(SQ[:, h % 2, some], O[:, h, some], ACT.Square).then_inc(S("o_sq", l), 1)
                for h in range(HEADS):
                    rsqrt(Ex[:, h, some], ("ossq", l, h), l, "o_rs", P, some, 2 * h)
                squares(dq, l, "dq_sq", some, 3)
                read(act, ("modT", *MODS_IN[l][-1]))
                rsqrt(RS[:, some], ("qssq", l), l, "mla_rs", QR, some)
                act.wait_ge(*at("dq_n", l, 3))
                squares(ckv, l, "ckv_sq", every, 2)
                rsqrt(RS[:, :], ("kssq", l), l, "mla_rs", KVR, every, 2)
                act.wait_ge(*at("a_ready", l, HEADS))
                for h in range(MH):
                    o = read(act, ("K", l, h))
                    fn(KT[0:NOPE, h, :], o[0:NOPE, :], ACT.Copy).then_inc(S("k_ready", l), 1)
                steps = attention_steps(l)
                for j in range(len(steps) + 2):
                    if j < len(steps):
                        keys = NCTX if steps[j][0] < 2 else T
                        act.wait_ge(*at("neg_max", l, j + 1))
                        o = read(act, ("sc", l, j))
                        fn(PR[:, j % 3, 0:keys], o[:, 0:keys], ACT.Exp, bias=mx[:, 1, j:j + 1], scale=SCALE,
                           accum_out=mx[:, 2, j:j + 1]).then_inc(S("p_exp", l), 1)
                    if j >= 2:
                        keys = NCTX if steps[j - 2][0] < 2 else T
                        o = read(act, ("pT", l, j - 2))
                        fn(PT[:, j % 2, 0:keys], o[:, 0:keys], ACT.Copy).then_inc(S("pT_ready", l), 1)
                    if splits_late(l) and 4 <= j < 4 + KD:
                        fn(H_late_hi[j - 4][:, some], H[:, j - 4, some], ACT.Copy).then_inc(S("h_late_hi", l), 1)

                def round_late(name):
                    act.wait_ge(slot_landed[slot_of[name, l]], landed_at[name, l])
                    for i in range(CHUNKS):
                        fn(late_hi[LATE_UNITS.index(name) % 2][i], W[:, slot_of[name, l], i * 1024:(i + 1) * 1024], ACT.Copy) \
                            .then_inc(S("late_hi", l), 1)

                if splits_late(l):
                    read(act, ("pv", l, len(steps) - 1))
                    round_late("ga0")
                    round_late("gb0")
                nc.scalar.preload_act_table_set("sigmoid_and_others")
                for m in range(KD):
                    for i, g in enumerate(("ga", "gb")):
                        o = read(act, (g, l, m))
                        if m >= 2:
                            act.wait_ge(*at("mixed", l, m - 1))
                        fn(mixT[:, m % 2 * 2 + i, some], o[:, some], ACT.Sigmoid).then_inc(S("mix_sig", l), 1)
                        if splits_late(l) and (m, g) == (KD - 1, "ga"):
                            round_late("o0")
                    if splits_late(l) and m == 3:
                        round_late("ga1")
                        round_late("gb1")
                if splits_late(l):
                    for k in range(KD):
                        act.wait_ge(*at("mixed", l, k + 1))
                        fn(H_late_hi[k][:, some], mix[:, k, some], ACT.Copy).then_inc(S("mixed_hi", l), 1)
                    round_late("o1")
                nc.scalar.preload_act_table_set("natural_log_exp_and_others")
                act.wait_ge(*at("z_mixed", l, KD))
                squares(Z, l, "sq2", some)
                rsqrt(RS[:, some], ("ssq2", l), l, "rs2", D, some)
                nc.scalar.preload_act_table_set("sigmoid_and_others")
                act.wait_ge(*at("gains", "g", 2 * l + 2))
                modulate(l, "h2", 1, (0, 1) if l == 0 else (1,))
                n = len(tiles)
                o = read(act, ("logit", l))
                fn(scoreT[0:NE, some], o[0:NE, some], ACT.Sigmoid).then_inc(S("score", l), 1)
                for j, t in enumerate(tiles):
                    for g in range(2):
                        o = read(act, ("hT", l, t, g))
                        fn(htok_hi[:, j, g * CH:(g + 1) * CH], o, ACT.Copy).then_inc(S("htok", l), 1)
                def round_weights(name, it):
                    act.wait_ge(*at(f"{name}_in", l, it * 16 + 16))
                    for c in ROUNDING[name]:
                        c = slice(c * 1024, (c + 1) * 1024)
                        fn(w_hi[name][:, c], W[:, UNITS.index(name), c], ACT.Copy).then_inc(S("w_hi", l), 1)

                def take_gathered(it):
                    act.wait_ge(*at("gathered", l, it + 1))
                    for half in range(2):
                        fn(xs_tok[:, half * 512:(half + 1) * 512], banks[:, half, :], ACT.Copy).then_inc(S("xs_tok", l), 1)

                def round_turned(it):
                    act.wait_ge(*at("xsT_full", l, it + 1))
                    for half in range(2):
                        fn(xsT_hi[:, half * 4:half * 4 + 4, :].rearrange("p k s -> p (k s)"), banks[:, 2 + half, :], ACT.Copy) \
                            .then_inc(S("xh", l), 1)

                def gate_sigmoid(it):
                    act.wait_ge(*at("gate_used", l, it + 1))
                    fn(gate_t, banks[:, 4, :], ACT.Sigmoid).then_inc(S("gate_sig", l), 1)

                def give_out(it, more):
                    act.wait_ge(*at("selT_full", l, it + 1))
                    fn(selT[:, 0:n * P], banks[:, 2, 0:n * P], ACT.Sign).then_inc(S("selT", l), 1)
                    fn(selw_copy[:, 0:n * P], banks[:, 2, 0:n * P], ACT.Copy, accum_out=wslot[:, 0:1]).then_inc(S("wslot", l), 1)
                    act.wait_ge(*at("hidT_full", l, it + 1))
                    fn(hidT_hi, banks[:, 3, :], ACT.Copy).then_inc(S("hidT", l), 1)
                    if more:
                        round_weights("gate", it + 1)
                        take_gathered(it + 1)
                    act.wait_ge(*at("wslot", l, it + 1))
                    for half, name in enumerate(("y0_full", "down_used")):
                        act.wait_ge(*at(name, l, it + 1))
                        fn(yd_hi[:, half * 512:(half + 1) * 512], banks[:, 4 + half, :], ACT.Copy, scale=wslot[:, 0:1]) \
                            .then_inc(S("yh", l), 1)
                        if more and half == 0:
                            round_turned(it + 1)
                    if more:
                        round_weights("up", it + 1)
                        gate_sigmoid(it + 1)
                        round_weights("down", it + 1)

                round_weights("gate", 0)
                round_weights("up", 0)
                act.wait_ge(*at("nb_ready", l, 1))
                nb = act.value_load(nbi[0:1, 0:1], min_val=0, max_val=3) + 1
                take_gathered(0)
                round_turned(0)
                gate_sigmoid(0)
                round_weights("down", 0)
                with act.Fori(0, nb * NE - 1) as it:
                    give_out(it, True)
                give_out(nb * NE - 1, False)
            nc.scalar.preload_act_table_set("natural_log_exp_and_others")
            act.wait_ge(*at("z_ready", DEPTH - 1, 1))
            squares(Z, "g", "sqf", slice(NCTX, T))
            rsqrt(RS[:, NCTX:T], ("ssqf",), "g", "rsf", D, slice(NCTX, T))
            for t in range(NX // P):
                for g in range(2):
                    o = read(act, ("fin", t, g))
                    fn(ztok[:, t, g * CH:(g + 1) * CH], o, ACT.Copy).then_inc(S("fin_rows"), 1)

        @block.gpsimd
        def _(pool):
            nc.gpsimd.memset(uq_pad[:, 0:NOPE], 0.0)
            nc.gpsimd.memset(kpe_pad[:, 0:NOPE], 0.0)
            for l in range(DEPTH):
                some = Nx(l)
                def swapped(dst, src):
                    d4 = dst.rearrange("p h (a s i) -> p h a s i", a=2, s=2)
                    s4 = src.rearrange("p h (a s i) -> p h a s i", a=2, s=2)
                    for ax in range(2):
                        nc.gpsimd.tensor_scalar(d4[:, :, ax, 0, :], s4[:, :, ax, 1, :], -1.0, None, ALU.mult)
                        x = nc.gpsimd.tensor_copy(d4[:, :, ax, 1, :], s4[:, :, ax, 0, :])
                    return x

                for n, name in enumerate(SPLIT_UNITS):
                    for i in range(CHUNKS):
                        c = slice(i * 1024, (i + 1) * 1024)
                        w = (slice(None), slot_of[name, l], c)
                        pool.wait_ge(*at("unit_hi", l, n * CHUNKS + i + 1))
                        if n or i:
                            pool.wait_ge(*at("unit_lo", l, n * CHUNKS + i))
                        nc.gpsimd.tensor_tensor(W_r[w], W[w], unit_hi[n % 2][:, c].bitcast(F32), ALU.subtract) \
                            .then_inc(S("unit_lo", l), 1)
                u = ("dkv", l)
                pool.wait_ge(slot_landed[slot_of[u]], landed_at[u])
                swapped(kpe_sw[:, :, :], slot(u, KVR + ROPE)[:, 0:KD, KVR:KVR + ROPE]).then_inc(S("kpe_sw", l), 1)
                u = ("uq", l)
                pool.wait_ge(slot_landed[slot_of[u]], landed_at[u])
                if l:
                    read(pool, ("Qsw", l - 1, MH - 1))
                for k in range(3):
                    w = slot(u, MH * QK)[:, k, :].rearrange("p (h c) -> p h c", h=MH)
                    swapped(uq_sw[:, k, :, :], w[:, :, NOPE:QK]).then_inc(S("uq_sw", l), 1)
                pool.wait_ge(*at("uq_sw", l, 3))
                pool.wait_ge(*at("kpe_ready", l, 1))
                pool.wait_ge(*at("a_ready", l, HEADS))
                for h in range(MH):
                    nc.gpsimd.tensor_copy(KT[NOPE:QK, h, :], kpe[NOPE:QK, :]).then_inc(S("kpe_in", l), 1)
                for k in range(KD if splits_late(l) else 0):
                    pool.wait_ge(*at("h_late_hi", l, k + 1))
                    nc.gpsimd.tensor_tensor(H_r[:, k, some], H[:, k, some], H_late_hi[k][:, some].bitcast(F32), ALU.subtract) \
                        .then_inc(S("h_late_lo", l), 1)

                def rest(it, name, first=False):
                    s = UNITS.index(name)
                    for i in range(BY_POOL[name]):
                        c = CHUNKS - BY_POOL[name] + i
                        pool.wait_ge(*at("w_hi", l, it * (3 * CHUNKS) + s * CHUNKS + ROUNDING[name].index(c) + 1))
                        c = slice(c * 1024, (c + 1) * 1024)
                        before = POOL_UNTIL[name] - BY_POOL[name] + i
                        if not (first and before == 0):
                            pool.wait_ge(*at("w_lo_pool", l, it * POOL_UNTIL["down"] + before))
                        nc.gpsimd.tensor_tensor(W_r[:, s, c], W[:, s, c], w_hi[name][:, c].bitcast(F32), ALU.subtract) \
                            .then_inc(S("w_lo_pool", l), 1)

                for name in UNITS:
                    rest(0, name, True)
                pool.wait_ge(*at("nb_ready", l, 1))
                nb = pool.value_load(nbi[0:1, 0:1], min_val=0, max_val=3) + 1
                with pool.Fori(0, nb * NE - 1) as it:
                    for name in UNITS:
                        rest(it + 1, name)

        @block.vector
        def _(dve):
            vv = nc.vector
            chain = [0]

            def link(ins):
                chain[0] += 1
                ins.then_inc(S("chain"), 1)
                dve.wait_ge(*at("chain", "g", chain[0]))

            vv.memset(eps[:], EPS).then_inc(S("eps"), 1)
            dve.wait_ge(*at("consts", "g", N_CONSTS))
            vv.tensor_copy(masks[:, :, :, :].rearrange("p d v t -> p (d v t)"), masks_in)
            o = read(dve, ("vec", 0))
            vv.tensor_copy(rb[:], o[:, 256:256 + NE])
            vv.tensor_copy(vecs[:], o[:, 0:NVEC]).then_inc(S("vec_read"), 1)
            o = read(dve, ("vec", 1))
            vv.tensor_copy(bmod[:], o[:, 0:NBMOD]).then_inc(S("vec_read"), 1)
            for k in range(KD):
                o = read(dve, ("z", k))
                vv.tensor_copy(Z[:, k, :], o).then_inc(S("z_loaded"), 1)
            dve.wait_ge(*at("c_exp", "g", 1))
            link(vv.tensor_scalar(silu_c[:], silu_c[:], 1.0, None, ALU.add))
            link(vv.reciprocal(silu_c[:], silu_c[:]))
            link(vv.tensor_tensor(small[:, 0, :], silu_c[:], vecs[:, 0:16], ALU.mult))
            link(vv.tensor_copy(silu_c[:, 0:8], small[:, 0, 8:16]))
            vv.tensor_copy(silu_c[:, 8:16], small[:, 0, 0:8]).then_inc(S("silu_c"), 1)
            for d, name in enumerate(("gamma_fwd", "gamma_bwd")):
                g = vec(name).rearrange("p (l h) -> p l h", l=DEPTH)
                e_, s_ = small[:, 3, 8 * d:8 * d + 8].rearrange("p (l h) -> p l h", l=2), small[:, 1 + d, 0:4]
                link(vv.tensor_tensor(s_, g[:, 0, :], g[:, 1, :], ALU.max))
                x = vv.tensor_tensor(e_, g, s_.unsqueeze(1).to_broadcast([P, 2, HEADS]), ALU.subtract)
            x.then_inc(S("gam_in"), 1)
            dve.wait_ge(*at("gam_exp", "g", 1))
            g4 = small[:, 3, :].rearrange("p (d l h) -> p d l h", d=2, l=2)
            s4 = small[:, 4, 0:8].rearrange("p (d h) -> p d h", d=2)
            link(vv.tensor_tensor(s4, g4[:, :, 0, :], g4[:, :, 1, :], ALU.add))
            link(vv.reciprocal(s4, s4))
            link(vv.tensor_tensor(g4, g4, s4.unsqueeze(2).to_broadcast([P, 2, 2, HEADS]), ALU.mult))
            link(vv.tensor_tensor(s4, g4[:, :, 0, :], g4[:, :, 1, :], ALU.add))
            vv.tensor_tensor(lb[:, :, 0, :], g4[:, :, 0, :], g4[:, :, 0, :], ALU.subtract)
            link(vv.tensor_tensor(lb[:, :, 1, :], s4, g4[:, :, 0, :], ALU.subtract))
            link(vv.tensor_scalar(oml[:], lb[:], -1.0, 1.0, ALU.mult, ALU.add))
            def add_mod(unit):
                l, j = unit
                o = read(dve, ("modT", l, j))
                vv.tensor_tensor(modT[:, l, 4 * j:4 * j + 4, :], o[:, 0:8].rearrange("p (n v) -> p n v", v=2),
                                 bmod[:, l * 48 + 4 * j:l * 48 + 4 * j + 4].unsqueeze(2).to_broadcast([P, 4, 2]), ALU.add) \
                  .then_inc(S("mod_added"), 1)

            def gains(l, i):
                dve.wait_ge(*at("mod_added", "g", MODS.index((l, 6 * i + 3)) + 1))
                first = VEC[("norm1_g", "norm2_g")[i]][0] + l * KD
                vv.scalar_tensor_tensor(
                    out=gainA[:, l, i, :, :], in0=modT[:, l, i * 24 + 8:i * 24 + 16, :], scalar=1.0,
                    in1=vecs[:, first:first + KD].unsqueeze(2).to_broadcast([P, KD, 2]), op0=ALU.add, op1=ALU.mult) \
                  .then_inc(S("gains"), 1)

            for unit in MODS_EARLY:
                add_mod(unit)
            turned = [0] * DEPTH

            def mods_until(l, place):
                for unit in MODS_IN[l][turned[l]:mod_turned(l, place)]:
                    add_mod(unit)
                turned[l] = mod_turned(l, place)

            for l in range(DEPTH):
                every, some = slice(0, T), Nx(l)
                tiles = range(first_token(l) // P, TILES)
                n = len(tiles)
                halves = (0, 1) if l == 0 else (1,)
                gains(l, 0)
                dve.wait_ge(*at("rs1", l, 2))
                for k in range(KD + 3):
                    if k < KD:
                        vv.tensor_tensor(H[:, k, :], Z[:, k, :], RS[:, :], ALU.mult).then_inc(S("h1_n", l), 1)
                    if k >= 3:
                        i = k - 3
                        dve.wait_ge(*at("h_hi", l, i + 1))
                        vv.tensor_tensor(H_r[:, i, :], H[:, i, :], H_hi[i].bitcast(F32), ALU.subtract).then_inc(S("h_lo", l), 1)
                for d in range(2):
                    for h in range(HEADS):
                        f = F[d][:, h, :]
                        dve.wait_ge(*at("f_sig", l, d * HEADS + h + 1))
                        link(vv.tensor_scalar(f, f, oml[:, d, l, h:h + 1], lb[:, d, l, h:h + 1], ALU.mult, ALU.add))
                for t in range(TILES):
                    o = read(dve, ("v", l, t))
                    vv.tensor_copy(V[:, t, :], o).then_inc(S("v_ready", l), 1)
                for h in range(HEADS):
                    dve.wait_ge(*at("g_sig", l, h + 1))
                    g = G[:, h, some]
                    o = read(dve, ("g", l, h))
                    vv.tensor_tensor(g, o[:, some], g, ALU.mult).then_inc(S("g_ready", l), 1)
                for k in range(KD):
                    vv.tensor_tensor(H[:, k, :], H_r[:, k, :].bitcast(F32), H_hi[k].bitcast(F32), ALU.add).then_inc(S("h_back", l), 1)
                rp = slice(NOPE, QK)
                o = read(dve, ("kpe", l, 0))
                vv.tensor_tensor(kpe[rp, :], o[rp, :], rope[rp, 0, :], ALU.mult).then_inc(S("kpe_mul", l), 1)
                o = read(dve, ("kpe", l, 1))
                vv.tensor_tensor(RS[rp, :], o[rp, :], rope[rp, 1, :], ALU.mult).then_inc(S("kpe_mul", l), 1)
                dve.wait_ge(*at("kpe_mul", l, 2))
                vv.tensor_tensor(kpe[rp, :], kpe[rp, :], RS[rp, :], ALU.add).then_inc(S("kpe_ready", l), 1)

                for d in range(2):
                    for h in range(HEADS):
                        vv.tensor_scalar(K[:, h, :], F[d][:, h, :], -1.0, 1.0, ALU.mult, ALU.add).then_inc(S("k_gate", l), 1)
                    vv.memset(att[:, :, :], 0.0).then_inc(S("att_zero", l), 1)
                    for h in range(HEADS):
                        dve.wait_ge(*at("logf", l, d * HEADS + h + 1))
                        for c in range(TILES):
                            b = F[d][:, h, c * P:(c + 1) * P]
                            b = b if d == 0 else b[:, ::-1]
                            x = vv.tensor_tensor_scan(b, ones[:, :], b, 0.0, ALU.mult, ALU.add)
                        x.then_inc(S("b_ready", l), 1)
                    dve.wait_ge(*at("b_ready", l, (d + 1) * HEADS))
                    dve.wait_ge(*at("q_ready", l, HEADS))
                    dve.wait_ge(*at("att_zero", l, d + 1))

                    def insert(turn, level, h):
                        o = read(dve, turn)
                        vv.copy_predicated(
                            att[:, h, some].rearrange("p (c t) -> p c t", t=P),
                            masks[:, d, level, :].unsqueeze(1).to_broadcast([P, n, P]),
                            o[:, some].rearrange("p (c t) -> p c t", t=P)).then_inc(S("att_in", l), 1)

                    for h in range(HEADS):
                        insert(("diag", l, d, h), 7, h)
                    base = d * len(STEPS)
                    for i in range(len(STEPS) + 3):
                        if i >= 3:
                            m, h = STEPS[i - 3]
                            insert(("lev", l, d, i - 3), LEVELS.index(m), h)
                            mods_until(l, ("lev", d, i - 3))
                        if i < len(STEPS):
                            m, h = STEPS[i]
                            v = F[d][:, h, some].rearrange("p (b s m) -> p b s m", s=2, m=m)
                            mid = v[:, :, 0, m - 1:m] if d == 0 else v[:, :, 1, 0:1]
                            nbk = n * P // (2 * m)
                            vv.tensor_tensor(Ex[:, i % 4, some].rearrange("p (b m) -> p b m", m=2 * m),
                                             F[d][:, h, some].rearrange("p (b m) -> p b m", m=2 * m),
                                             mid.to_broadcast([P, nbk, 2 * m]), ALU.subtract).then_inc(S("exponent", l), 1)
                        if 1 <= i <= len(STEPS):
                            m, h = STEPS[i - 1]
                            dve.wait_ge(*at("decay", l, base + i))
                            split = lambda x: x.rearrange("p (b s m) -> p b s m", s=2, m=m)
                            qs = 1 - d
                            for src, s, last in ((q, qs, False), (K, 1 - qs, True)):
                                x = vv.tensor_tensor(split(QKd[:, (i - 1) % 2, some])[:, :, s, :],
                                                     split(src[:, h, some])[:, :, s, :],
                                                     split(Ex[:, (i - 1) % 4, some])[:, :, s, :], ALU.mult)
                            x.then_inc(S("qk_ready", l), 1)
                    edge = P - 1 if d == 0 else 0

                    def decay_keys(h):
                        dve.wait_ge(*at("kd_decay", l, d * HEADS + h + 1))
                        vv.tensor_tensor(K[:, h, :], QKd[:, h % 2, :], K[:, h, :], ALU.mult).then_inc(S("kd_ready", l), 1)

                    for h in range(HEADS):
                        b = F[d][:, h, :].rearrange("p (c t) -> p c t", t=P)
                        if h >= 2:
                            dve.wait_ge(*at("kd_ready", l, d * HEADS + h - 1))
                        vv.tensor_tensor(QKd[:, h % 2, :].rearrange("p (c t) -> p c t", t=P), b,
                                         b[:, :, edge:edge + 1].to_broadcast([P, TILES, P]), ALU.subtract) \
                          .then_inc(S("kd_exponent", l), 1)
                        if h >= 1:
                            decay_keys(h - 1)
                    decay_keys(HEADS - 1)
                    dve.wait_ge(*at("e_b", l, 2 * d + 2))
                    vv.tensor_tensor(Ex[:, :, some], Ex[:, :, some], q[:, :, some], ALU.mult).then_inc(S("qe_ready", l), 1)
                    mods_until(l, ("keys", d))
                    for i, c in enumerate(ORDER[d]):
                        if c in tiles:
                            s = slice(c * P, (c + 1) * P)
                            o = read(dve, ("out", l, d, i)).rearrange("p (h t) -> p h t", h=HEADS)
                            if d == 0:
                                vv.tensor_copy(O[:, :, s], o).then_inc(S("o_acc", l), 1)
                            else:
                                vv.tensor_tensor(O[:, :, s], o, O[:, :, s], ALU.add).then_inc(S("o_acc", l), 1)
                        if i < 3:
                            o = read(dve, ("st", l, d, i))
                            if i:
                                mods_until(l, ("chunk", d, i - 1))
                                dve.wait_ge(*at("state", l, (d * 3 + i) * HEADS))
                            for h in range(HEADS):
                                ps = o[:, h * P:(h + 1) * P]
                                if i == 0:
                                    x = vv.tensor_copy(state[:, h, :], ps)
                                else:
                                    x = vv.scalar_tensor_tensor(out=state[:, h, :], in0=state[:, h, :], scalar=ebl[:, h, c:c + 1],
                                                                in1=ps, op0=ALU.mult, op1=ALU.add)
                                x.then_inc(S("state", l), 1)
                mods_until(l, "end")
                for h in range(HEADS):
                    dve.wait_ge(*at("o_rs", l, 2 * h + 2))
                    link(vv.tensor_tensor(O[:, h, some], O[:, h, some], Ex[:, h, some], ALU.mult))
                    vv.scalar_tensor_tensor(out=O[:, h, some], in0=O[:, h, some], scalar=vec("hg_norm_g")[:, l * HEADS + h:l * HEADS + h + 1],
                                            in1=G[:, h, some], op0=ALU.mult, op1=ALU.mult).then_inc(S("a_ready", l), 1)
                dve.wait_ge(*at("mla_rs", l, 2))
                for k in range(3):
                    vv.scalar_tensor_tensor(out=dq[:, k, some], in0=dq[:, k, some], scalar=vec("q_norm_g")[:, l * 3 + k:l * 3 + k + 1],
                                            in1=RS[:, some], op0=ALU.mult, op1=ALU.mult).then_inc(S("dq_n", l), 1)
                dve.wait_ge(*at("mla_rs", l, 4))
                for k in range(2):
                    vv.scalar_tensor_tensor(out=ckv[:, k, :], in0=ckv[:, k, :], scalar=vec("kv_norm_g")[:, l * 2 + k:l * 2 + k + 1],
                                            in1=RS[:, :], op0=ALU.mult, op1=ALU.mult).then_inc(S("ckv_n", l), 1)
                for h in range(MH):
                    o = read(dve, ("Q", l, h))
                    vv.tensor_tensor(QT[0:QK, h, some], o[0:QK, some], rope[0:QK, 0, some], ALU.mult).then_inc(S("q_rot", l), 1)
                    o = read(dve, ("Qsw", l, h))
                    vv.tensor_tensor(tmpQ[0:QK, h % 2, some], o[0:QK, some], rope[0:QK, 1, some], ALU.mult).then_inc(S("q_rot", l), 1)
                    dve.wait_ge(*at("q_rot", l, 2 * h + 2))
                    vv.tensor_tensor(QT[0:QK, h, some], QT[0:QK, h, some], tmpQ[0:QK, h % 2, some], ALU.add).then_inc(S("q_rope", l), 1)
                for t in range(TILES):
                    o = read(dve, ("V", l, t))
                    vv.tensor_copy(V2[:, t, :], o).then_inc(S("v2_ready", l), 1)
                steps = attention_steps(l)
                for j in range(len(steps) + 3):
                    if j < len(steps):
                        keys = NCTX if steps[j][0] < 2 else T
                        o = read(dve, ("sc", l, j))
                        link(vv.reduce_max(mx[:, 0, j:j + 1], o[:, 0:keys], AX_X))
                        vv.tensor_scalar(mx[:, 1, j:j + 1], mx[:, 0, j:j + 1], -SCALE, None, ALU.mult).then_inc(S("neg_max", l), 1)
                    if 1 <= j <= len(steps):
                        i = j - 1
                        keys = NCTX if steps[i][0] < 2 else T
                        dve.wait_ge(*at("p_exp", l, i + 1))
                        link(vv.reciprocal(mx[:, 3, i:i + 1], mx[:, 2, i:i + 1]))
                        vv.tensor_scalar(PR[:, i % 3, 0:keys], PR[:, i % 3, 0:keys], mx[:, 3, i:i + 1], None, ALU.mult) \
                          .then_inc(S("p_norm", l), 1)
                    if j >= 3:
                        qt, h = steps[j - 3]
                        rows = slice(h % 2 * MV, (h % 2 + 1) * MV)
                        o = read(dve, ("pv", l, j - 3))
                        vv.tensor_copy(MT[rows, h // 2, qt * P:(qt + 1) * P], o[rows, 0:P]).then_inc(S("m_ready", l), 1)
                def rest_late(name):
                    n_ = LATE_UNITS.index(name)
                    for i in range(CHUNKS):
                        w = (slice(None), slot_of[name, l], slice(i * 1024, (i + 1) * 1024))
                        dve.wait_ge(*at("late_hi", l, n_ * CHUNKS + i + 1))
                        vv.tensor_tensor(W_r[w], W[w], late_hi[n_ % 2][i].bitcast(F32), ALU.subtract).then_inc(S("late_lo", l), 1)

                if splits_late(l):
                    rest_late("ga0")
                    rest_late("gb0")
                for m in range(KD):
                    if splits_late(l) and m == KD - 1:
                        rest_late("o0")
                    for i, (g, w, sem) in enumerate((("ga", "pa", "mix_a"), ("gb", "pb", "mix_b"))):
                        t_ = mixT[:, m % 2 * 2 + i, some]
                        dve.wait_ge(*at("mix_sig", l, 2 * m + i + 1))
                        o = read(dve, (w, l, m))
                        vv.tensor_tensor(t_, o[:, some], t_, ALU.mult).then_inc(S(sem, l), 1)
                    dve.wait_ge(*at("mix_a", l, m + 1))
                    dve.wait_ge(*at("mix_b", l, m + 1))
                    vv.tensor_tensor(mix[:, m, some], mixT[:, m % 2 * 2, some], mixT[:, m % 2 * 2 + 1, some], ALU.add) \
                      .then_inc(S("mixed", l), 1)
                    if splits_late(l) and m == 3:
                        rest_late("ga1")
                        rest_late("gb1")
                if splits_late(l):
                    for k in range(KD):
                        dve.wait_ge(*at("mixed_hi", l, k + 1))
                        vv.tensor_tensor(mix_lo[:, k, some], mix[:, k, some], H_late_hi[k][:, some].bitcast(F32), ALU.subtract) \
                          .then_inc(S("mixed_lo", l), 1)
                    rest_late("o1")
                for m in range(KD):
                    o = read(dve, ("y", l, m))
                    for v in halves:
                        s = slice(v * NCTX, (v + 1) * NCTX)
                        x = vv.scalar_tensor_tensor(out=Z[:, m, s], in0=o[:, s], scalar=modT[:, l, 16 + m, v:v + 1], in1=Z[:, m, s],
                                                    op0=ALU.mult, op1=ALU.add)
                    x.then_inc(S("z_mixed", l), 1)
                gains(l, 1)
                dve.wait_ge(*at("z_mixed", l, KD))
                dve.wait_ge(*at("rs2", l, 2))
                for k in range(KD):
                    vv.tensor_tensor(H[:, k, some], Z[:, k, some], RS[:, some], ALU.mult).then_inc(S("h2_n", l), 1)

                R = lambda i: rt[:, i, 0:n, :]
                o = read(dve, ("logitT", l))[:, 0:n * NE].rearrange("p (t e) -> p t e", e=NE)
                vv.tensor_tensor(R(2), o, rb[:, :].unsqueeze(1).to_broadcast([P, n, NE]), ALU.add)
                vv.tensor_copy(R(1), o).then_inc(S("scored", l), 1)
                dve.wait_ge(*at("scored", l, 1))
                s2 = R(2).rearrange("p t (g e) -> p (t g) e", g=NG)
                gs = rt[:, 3, :, :].rearrange("p t e -> p (t e)")[:, 0:n * NG].rearrange("p (t g) -> p t g", g=NG)

                def compare(dst, values, groups):
                    shape = [P, groups, EG, EG]
                    ge, gt = (compared[:, i, 0:groups * EG * EG].rearrange("p (x j i) -> p x j i", j=EG, i=EG) for i in range(2))
                    first, second = (values.unsqueeze(2).to_broadcast(shape), values.unsqueeze(3).to_broadcast(shape))
                    vv.tensor_tensor(ge, first, second, ALU.is_ge)
                    link(vv.tensor_tensor(gt, first, second, ALU.is_gt))
                    vv.tensor_tensor(ge, ge, pair[:, 0, :, :].unsqueeze(1).to_broadcast(shape), ALU.mult)
                    link(vv.tensor_tensor(gt, gt, pair[:, 1, :, :].unsqueeze(1).to_broadcast(shape), ALU.mult))
                    link(vv.tensor_tensor(ge, ge, gt, ALU.add))
                    link(vv.tensor_reduce(dst, ge, AX_X, ALU.add))

                sums = compared[:, 2, 0:n * NG * EG * EG].rearrange("p (x i j) -> p x i j", i=EG, j=EG)
                shape = [P, n * NG, EG, EG]
                link(vv.tensor_tensor(sums, s2.unsqueeze(2).to_broadcast(shape), s2.unsqueeze(3).to_broadcast(shape), ALU.add))
                link(vv.tensor_tensor(sums, sums, pair[:, 2, :, :].unsqueeze(1).to_broadcast(shape), ALU.add))
                link(vv.tensor_reduce(gs.rearrange("p t g -> p (t g)"), sums.rearrange("p x i j -> p x (i j)"), AX_X, ALU.max))
                ahead_e = R(4).rearrange("p t (g e) -> p (t g) e", g=NG)
                ahead_g = rt[:, 5, :, :].rearrange("p t e -> p (t e)")[:, 0:n * NG].rearrange("p (t g) -> p t g", g=NG)
                compare(ahead_e, s2, n * NG)
                compare(ahead_g, gs, n)
                link(vv.tensor_scalar(ahead_g, ahead_g, 0.5, None, ALU.is_lt))
                vv.scalar_tensor_tensor(out=R(0).rearrange("p t (g e) -> p (t g) e", g=NG), in0=ahead_e, scalar=1.5,
                                        in1=ahead_g.rearrange("p t g -> p (t g)").unsqueeze(2).to_broadcast([P, n * NG, EG]),
                                        op0=ALU.is_lt, op1=ALU.mult).then_inc(S("taken", l), 1)
                dve.wait_ge(*at("taken", l, 1))
                link(vv.tensor_tensor(R(9), R(1), R(0), ALU.mult))
                wsum = rt[:, 10, 0:n, 0]
                link(vv.tensor_reduce(wsum, R(9), AX_X, ALU.add))
                link(vv.reciprocal(wsum, wsum))
                for r in range(ROUNDS):
                    x = vv.tensor_tensor(gw[:, 0:n, r * NE:(r + 1) * NE], R(9), wsum.unsqueeze(2).to_broadcast([P, n, NE]), ALU.mult)
                link(x)
                for j, t in enumerate(tiles):
                    for g in range(2):
                        o = read(dve, ("hT", l, t, g))
                        c = slice(g * CH, (g + 1) * CH)
                        dve.wait_ge(*at("htok", l, j * 2 + g + 1))
                        vv.tensor_tensor(htok_lo[:, j, c], o, htok_hi[:, j, c].bitcast(F32), ALU.subtract) \
                          .then_inc(S("htok_lo", l), 1)

                o = read(dve, ("rank", l))
                place = rt[:, 11, 0:n, :]
                link(vv.scalar_tensor_tensor(out=place, in0=o[:, 0:n * NE].rearrange("p (t e) -> p t e", e=NE), scalar=FAR,
                                             in1=R(0), op0=ALU.add, op1=ALU.mult))
                for r in range(ROUNDS):
                    link(vv.tensor_scalar(pos[:, 0:n, r * NE:(r + 1) * NE], place, -FAR - CAP * r, None, ALU.add))
                link(vv.reduce_max(cnt[:, 0:1], o[:, n * NE:(n + 1) * NE], AX_X))
                for i in range(1, 4):
                    link(vv.tensor_scalar(cnt[:, i:i + 1], cnt[:, 0:1], float(CAP * i), None, ALU.is_gt))
                link(vv.tensor_tensor(cnt[:, 1:2], cnt[:, 1:2], cnt[:, 2:3], ALU.add))
                link(vv.tensor_tensor(cnt[:, 4:5], cnt[:, 1:2], cnt[:, 3:4], ALU.add))
                vv.tensor_copy(nbi[:, :], cnt[:, 4:5]).then_inc(S("nb_ready", l), 1)
                dve.wait_ge(*at("nb_ready", l, 1))
                nb = dve.value_load(nbi[0:1, 0:1], min_val=0, max_val=3) + 1

                def select(it):
                    for j in range(n):
                        x = vv.tensor_scalar(sel[:, j, :], slot_no[:, :], pos[:, j, bass.ds(it, 1)], None, ALU.is_equal)
                    x.then_inc(S("sel", l), 1)

                def rest(it, name):
                    s = UNITS.index(name)
                    for i in range(CHUNKS - BY_POOL[name]):
                        c = slice(i * 1024, (i + 1) * 1024)
                        dve.wait_ge(*at("w_hi", l, it * (3 * CHUNKS) + s * CHUNKS + ROUNDING[name].index(i) + 1))
                        vv.tensor_tensor(W_r[:, s, c], W[:, s, c], w_hi[name][:, c].bitcast(F32), ALU.subtract) \
                          .then_inc(S("w_lo", l), 1)

                def rest_turned(it):
                    for half in range(2):
                        k = slice(half * 4, half * 4 + 4)
                        dve.wait_ge(*at("xh", l, it * 2 + half + 1))
                        vv.tensor_tensor(xsT_lo[:, k, :].rearrange("p k s -> p (k s)"), banks[:, 2 + half, :],
                                         xsT_hi[:, k, :].rearrange("p k s -> p (k s)").bitcast(F32), ALU.subtract) \
                          .then_inc(S("xl", l), 1)

                def weigh(it):
                    for j in range(n):
                        x = vv.tensor_scalar(selw[:, j, :], slot_no[:, :], pos[:, j, bass.ds(it, 1)], gw[:, j, bass.ds(it, 1)],
                                             ALU.is_equal, ALU.mult)
                    x.then_inc(S("selw", l), 1)

                def silu(it):
                    dve.wait_ge(*at("gate_sig", l, it + 1))
                    vv.tensor_tensor(gate_t, banks[:, 4, :], gate_t, ALU.mult).then_inc(S("silu", l), 1)

                def hide(it):
                    dve.wait_ge(*at("silu", l, it + 1))
                    dve.wait_ge(*at("up_used", l, it + 1))
                    vv.tensor_tensor(hidden, banks[:, 5, :], gate_t, ALU.mult).then_inc(S("hidden", l), 1)

                def add(it, tiles):
                    for k in tiles:
                        dve.wait_ge(*at("combined", l, it * KD + k + 1))
                        for v in halves:
                            s = slice(v * NCTX, (v + 1) * NCTX)
                            c0 = v * NCTX - first_token(l)
                            x = vv.scalar_tensor_tensor(out=Z[:, k, s], in0=banks[:, COMBINE[k], c0:c0 + NCTX],
                                                        scalar=modT[:, l, 40 + k, v:v + 1], in1=Z[:, k, s],
                                                        op0=ALU.mult, op1=ALU.add)
                        x.then_inc(S("z_added", l), 1)

                def give_out(it, more):
                    dve.wait_ge(*at("hidT", l, it + 1))
                    vv.tensor_tensor(hidT_lo, banks[:, 3, :], hidT_hi.bitcast(F32), ALU.subtract).then_inc(S("hidT_lo", l), 1)
                    if more:
                        rest(it + 1, "gate")
                        weigh(it + 1)
                    for half in range(2):
                        c = slice(half * 512, (half + 1) * 512)
                        dve.wait_ge(*at("yh", l, it * 2 + half + 1))
                        vv.scalar_tensor_tensor(out=yd_lo[:, c], in0=banks[:, 4 + half, :], scalar=wslot[:, 0:1],
                                                in1=yd_hi[:, c].bitcast(F32), op0=ALU.mult, op1=ALU.subtract) \
                          .then_inc(S("yl", l), 1)
                        if more and half == 0:
                            rest_turned(it + 1)
                    if more:
                        rest(it + 1, "up")
                    add(it, range(4))
                    if more:
                        silu(it + 1)
                        rest(it + 1, "down")
                        hide(it + 1)
                        add(it, range(4, 6))
                        select((it + 2) % (ROUNDS * NE))
                        add(it, range(6, KD))
                    else:
                        add(it, range(4, KD))

                select(0)
                rest(0, "gate")
                rest(0, "up")
                rest_turned(0)
                weigh(0)
                select(1)
                silu(0)
                rest(0, "down")
                hide(0)
                with dve.Fori(0, nb * NE - 1) as it:
                    give_out(it, True)
                give_out(nb * NE - 1, False)
                vv.tensor_copy(small[:, 6, 0:1], small[:, 4, 0:1]).then_inc(S("z_ready", l), 1)

            dve.wait_ge(*at("rsf", "g", 2))
            for k in range(KD):
                vv.scalar_tensor_tensor(out=Z[:, k, NCTX:T], in0=Z[:, k, NCTX:T], scalar=vec("final_g")[:, k:k + 1],
                                        in1=RS[:, NCTX:T], op0=ALU.mult, op1=ALU.mult).then_inc(S("zf"), 1)


def shape_constants():
    p = np.arange(P)
    s, t = p[:, None], p[None, :]
    masks = np.zeros((P, 2, 8, P), np.int32)
    for i, m in enumerate(LEVELS):
        same = s // (2 * m) == t // (2 * m)
        masks[:, 0, i] = same & (s % (2 * m) < m) & (t % (2 * m) >= m)
        masks[:, 1, i] = same & (s % (2 * m) >= m) & (t % (2 * m) < m)
    masks[:, :, 7] = (s == t)[:, None, :]
    e = np.arange(EG)
    rope = np.zeros((P, 2, T), np.float32)
    rope[:, 0] = 1.0
    axis = ROPE // 2
    inv = np.float32(10000.0) ** (-np.arange(0, axis, 2, dtype=np.float32) / np.float32(axis))
    tok = np.arange(NX)
    for ax, at in enumerate((tok // 64, tok % 64)):
        ang = (at.astype(np.float32)[None, :] * inv[:, None]).astype(np.float32)
        for half in range(2):
            r = NOPE + ax * axis + half * 8
            rope[r:r + 8, 0, NCTX:] = np.cos(ang)
            rope[r:r + 8, 1, NCTX:] = np.sin(ang)
    return {
        "k_ident": np.eye(P, dtype=np.float32), "k_ones": np.ones((P, P), np.float32),
        "k_before": (s < t).astype(np.float32), "k_slot": np.broadcast_to(p.astype(np.float32), (P, P)).copy(),
        "k_pair": np.broadcast_to(np.stack([e[None, :] < e[:, None], e[None, :] > e[:, None], (e[None, :] == e[:, None]) * -1e30])
                                  .astype(np.float32), (P, 3, EG, EG)).copy(),
        "k_masks": masks.reshape(P, -1), "k_rope": rope,
    }


_INS = ['x', 'c', 'ctx', 'c_ctx', 'w_mod', 'b_mod', 'norm1_g', 'norm2_g', 'w_in', 'gamma_fwd', 'gamma_bwd', 'hg_norm_g',
        'q_norm_g', 'kv_norm_g', 'w_uq', 'w_ukv', 'w_pa', 'w_pb', 'w_o', 'w_router', 'router_bias',
        'w_gate_e', 'w_up_e', 'w_down_e', 'final_g']


def kernel(**inputs):
    import concourse.bacc as _bacc
    from concourse.bass_utils import run_bass_kernel_spmd as _run

    nc = _bacc.Bacc("TRN2", target_bir_lowering=False, num_devices=1)
    arrays, args = {}, {}
    given = {name: np.ascontiguousarray(inputs[name]) for name in _INS}
    for name, value in {**given, **shape_constants()}.items():
        arrays[f"in_{name}"] = value
        args[name] = nc.dram_tensor(f"in_{name}", value.shape, mybir.dt.from_np(value.dtype), kind="ExternalInput").ap()
    out = nc.dram_tensor("out_0", (1, NX, D), F32, kind="ExternalOutput").ap()
    bass_hybrid_transformer(nc, args, out)
    r = _run(nc, [arrays], core_ids=[0])
    return r.results[0]["out_0"]
```
